# Optimizing a Trainium2 kernel written in Bass

```python
import math
import jax
import jax.numpy as jnp
from jax import lax
import numpy as np

D_MODEL = 1024
BATCH = 1
SEQ = 256
DEPTH = 4
DEC_BATCH = 8
DEC_SEQ = 4
PAST_LEN = 2048
PAGE_SIZE = 128

N_MIXERS = 3
LAYER_MIXER = tuple(i % N_MIXERS for i in range(DEPTH))
N_GDN = LAYER_MIXER.count(0)
N_MLA = LAYER_MIXER.count(1)
N_MLSTM = LAYER_MIXER.count(2)

GDN_HEADS = D_MODEL // 128
GDN_DK = 128
GDN_DV = 128
GDN_CONV = 4
GDN_CHUNK = 64
GDN_QKV = GDN_HEADS * (2 * GDN_DK + GDN_DV)
GDN_Z = GDN_HEADS * GDN_DV

MLA_HEADS = D_MODEL // 128
MLA_NOPE = 128
MLA_ROPE = 64
MLA_V = 128
MLA_Q_RANK = 3 * D_MODEL // 8
MLA_KV_RANK = D_MODEL // 4
MLA_SCALE = (MLA_NOPE + MLA_ROPE) ** -0.5
ROPE_THETA = 10000.0
Q_BLOCK = 128

ML_HEADS = 4
ML_DK = D_MODEL // (2 * ML_HEADS)
ML_DV = D_MODEL // ML_HEADS
ML_CHUNK = 64
ML_QK = ML_HEADS * ML_DK
ML_V = ML_HEADS * ML_DV

D_FF = ((8 * D_MODEL // 3 + 127) // 128) * 128
EPS = 1e-6

kernel_name = 'hybrid_gdn_mla_mlstm_macaron_step'

def _rmsnorm(x, g):
    xf = x.astype(jnp.float32)
    y = xf * lax.rsqrt(jnp.mean(xf * xf, axis=-1, keepdims=True) + EPS)
    return (y * g.astype(jnp.float32)).astype(x.dtype)

def _l2norm(x):
    return x * lax.rsqrt(jnp.sum(x * x, axis=-1, keepdims=True) + EPS)

def _swiglu(x, w_up, w_down):
    g, u = jnp.split(x @ w_up, 2, axis=-1)
    return (jax.nn.silu(g) * u) @ w_down

def _rope(x, pos):
    half = x.shape[-1] // 2
    inv = ROPE_THETA ** (-jnp.arange(half, dtype=jnp.float32) / half)
    ang = pos.astype(jnp.float32)[:, None] * inv
    ang = ang.reshape((ang.shape[0],) + (1,) * (x.ndim - 3) + (half,))
    cos, sin = jnp.cos(ang), jnp.sin(ang)
    xf = x.astype(jnp.float32)
    x1, x2 = xf[..., :half], xf[..., half:]
    return jnp.concatenate([x1 * cos - x2 * sin, x2 * cos + x1 * sin], axis=-1).astype(x.dtype)

def _to_chunks(t, L):
    B, T, H = t.shape[:3]
    t = t.reshape((B, T // L, L, H) + t.shape[3:])
    return jnp.moveaxis(t, (1, 3), (0, 2))

def _from_chunks(t):
    N, B, H, L = t.shape[:4]
    t = jnp.moveaxis(t, (0, 2), (1, 3))
    return t.reshape((B, N * L, H) + t.shape[4:])

def _causal_conv(xp, buf, w):
    T = xp.shape[1]
    full = jnp.concatenate([buf.astype(xp.dtype), xp], axis=1)
    y = sum(full[:, j:j + T] * w[j] for j in range(w.shape[0]))
    return y, full[:, T:]

def _gated_delta(q, k, v, g, beta, S0):
    B, T, H, _ = q.shape
    DV = v.shape[-1]
    L = math.gcd(T, GDN_CHUNK)
    qc, kc, vc = _to_chunks(q, L), _to_chunks(k, L), _to_chunks(v, L)
    gc = jnp.cumsum(_to_chunks(g, L), axis=-1)
    bc = _to_chunks(beta, L)
    incl = jnp.tril(jnp.ones((L, L), bool))
    strict = jnp.tril(jnp.ones((L, L), bool), -1)
    diff = gc[..., :, None] - gc[..., None, :]
    decay_incl = jnp.exp(jnp.where(incl, diff, -jnp.inf))
    decay_strict = jnp.where(strict, decay_incl, 0.0)
    kb = kc * bc[..., None]
    a_mat = jnp.eye(L, dtype=jnp.float32) + jnp.einsum('nbhid,nbhjd->nbhij', kb, kc) * decay_strict
    rhs = jnp.concatenate([vc * bc[..., None], kb * jnp.exp(gc)[..., None]], axis=-1)
    sol = lax.linalg.triangular_solve(a_mat, rhs, left_side=True, lower=True, unit_diagonal=True)
    u, w = sol[..., :DV], sol[..., DV:]
    attn = jnp.einsum('nbhid,nbhjd->nbhij', qc, kc) * decay_incl
    qg = qc * jnp.exp(gc)[..., None]
    kdec = kc * jnp.exp(gc[..., -1:] - gc)[..., None]
    glast = jnp.exp(gc[..., -1])

    def step(S, xs):
        u_n, w_n, qg_n, attn_n, kdec_n, gl_n = xs
        v_new = u_n - jnp.einsum('bhld,bhde->bhle', w_n, S)
        o = jnp.einsum('bhld,bhde->bhle', qg_n, S) + jnp.einsum('bhij,bhje->bhie', attn_n, v_new)
        S = S * gl_n[..., None, None] + jnp.einsum('bhld,bhle->bhde', kdec_n, v_new)
        return S, o

    S, o = lax.scan(step, S0, (u, w, qg, attn, kdec, glast))
    return _from_chunks(o), S

def _gdn_mixer(x, S0, conv_buf, w_in, conv_w, a_log, dt_bias, norm_w, w_out):
    B, T, _ = x.shape
    f32 = jnp.float32
    proj = x @ w_in
    qkv_pre, z, b, a = jnp.split(proj, [GDN_QKV, GDN_QKV + GDN_Z, GDN_QKV + GDN_Z + GDN_HEADS], axis=-1)
    qkv, new_buf = _causal_conv(qkv_pre, conv_buf, conv_w)
    qkv = jax.nn.silu(qkv.astype(f32))
    q, k, v = jnp.split(qkv, [GDN_HEADS * GDN_DK, 2 * GDN_HEADS * GDN_DK], axis=-1)
    q = _l2norm(q.reshape(B, T, GDN_HEADS, GDN_DK)) * GDN_DK ** -0.5
    k = _l2norm(k.reshape(B, T, GDN_HEADS, GDN_DK))
    v = v.reshape(B, T, GDN_HEADS, GDN_DV)
    beta = jax.nn.sigmoid(b.astype(f32))
    g = -jnp.exp(a_log.astype(f32)) * jax.nn.softplus(a.astype(f32) + dt_bias.astype(f32))
    o, S = _gated_delta(q, k, v, g, beta, S0.astype(f32))
    o = _rmsnorm(o, norm_w) * jax.nn.silu(z.astype(f32).reshape(B, T, GDN_HEADS, GDN_DV))
    y = o.reshape(B, T, GDN_Z).astype(x.dtype) @ w_out
    return y, S.astype(x.dtype), new_buf

def _mlstm_chunked(q, k, v, ig, lf, C0, n0, m0):
    T = q.shape[1]
    L = math.gcd(T, ML_CHUNK)
    incl = jnp.tril(jnp.ones((L, L), bool))

    def step(carry, xs):
        C, n, m = carry
        q_n, k_n, v_n, ig_n, lf_n = xs
        b = jnp.cumsum(lf_n, axis=-1)
        dmat = jnp.where(incl, b[..., :, None] - b[..., None, :] + ig_n[..., None, :], -jnp.inf)
        inter = b + m[..., None]
        m_t = jnp.maximum(inter, jnp.max(dmat, axis=-1))
        w_intra = jnp.exp(dmat - m_t[..., None])
        w_inter = jnp.exp(inter - m_t)
        s = jnp.einsum('bhid,bhjd->bhij', q_n, k_n) * w_intra
        num = w_inter[..., None] * jnp.einsum('bhld,bhde->bhle', q_n, C) + jnp.einsum('bhij,bhje->bhie', s, v_n)
        den = w_inter * jnp.einsum('bhld,bhd->bhl', q_n, n) + jnp.sum(s, axis=-1)
        h = num / jnp.maximum(jnp.abs(den), jnp.exp(-m_t))[..., None]
        m_new = m_t[..., -1]
        w_state = jnp.exp(dmat[..., -1, :] - m_new[..., None])
        carry_decay = jnp.exp(inter[..., -1] - m_new)
        C = carry_decay[..., None, None] * C + jnp.einsum('bhl,bhld,bhle->bhde', w_state, k_n, v_n)
        n = carry_decay[..., None] * n + jnp.einsum('bhl,bhld->bhd', w_state, k_n)
        return (C, n, m_new), h

    xs = (_to_chunks(q, L), _to_chunks(k, L), _to_chunks(v, L), _to_chunks(ig, L), _to_chunks(lf, L))
    (C, n, m), h = lax.scan(step, (C0, n0, m0), xs)
    return _from_chunks(h), C, n, m

def _mlstm_mixer(x, C0, n0, m0, w_in, i_bias, f_bias, w_out):
    B, T, _ = x.shape
    f32 = jnp.float32
    proj = x @ w_in
    q, k, v, o, ig, fg = jnp.split(
        proj, [ML_QK, 2 * ML_QK, 2 * ML_QK + ML_V, 2 * ML_QK + 2 * ML_V, 2 * ML_QK + 2 * ML_V + ML_HEADS], axis=-1)
    q = q.astype(f32).reshape(B, T, ML_HEADS, ML_DK) * ML_DK ** -0.5
    k = k.astype(f32).reshape(B, T, ML_HEADS, ML_DK)
    v = v.astype(f32).reshape(B, T, ML_HEADS, ML_DV)
    ig = ig.astype(f32) + i_bias.astype(f32)
    lf = jax.nn.log_sigmoid(fg.astype(f32) + f_bias.astype(f32))
    h, C, n, m = _mlstm_chunked(q, k, v, ig, lf, C0.astype(f32), n0.astype(f32), m0.astype(f32))
    h = h * jax.nn.sigmoid(o.astype(f32).reshape(B, T, ML_HEADS, ML_DV))
    y = h.reshape(B, T, ML_V).astype(x.dtype) @ w_out
    return y, C.astype(x.dtype), n.astype(x.dtype), m.astype(x.dtype)

def _mla_project(x, pos, w_in, q_norm, kv_norm, w_uq):
    B, T, _ = x.shape
    proj = x @ w_in
    cq, ckv, kr = jnp.split(proj, [MLA_Q_RANK, MLA_Q_RANK + MLA_KV_RANK], axis=-1)
    cq = _rmsnorm(cq, q_norm)
    ckv = _rmsnorm(ckv, kv_norm)
    q = (cq @ w_uq).reshape(B, T, MLA_HEADS, MLA_NOPE + MLA_ROPE)
    q_nope = q[..., :MLA_NOPE]
    q_rope = _rope(q[..., MLA_NOPE:], pos)
    k_rope = _rope(kr, pos)
    return q_nope, q_rope, ckv, k_rope

def _mla_prompt(x, w_in, q_norm, kv_norm, w_uq, w_ukv, w_out):
    B, T, _ = x.shape
    pos = jnp.arange(T)
    q_nope, q_rope, ckv, k_rope = _mla_project(x, pos, w_in, q_norm, kv_norm, w_uq)
    kv = (ckv @ w_ukv).reshape(B, T, MLA_HEADS, MLA_NOPE + MLA_V)
    k_nope, v = kv[..., :MLA_NOPE], kv[..., MLA_NOPE:]
    qb = math.gcd(T, Q_BLOCK)
    nb = T // qb
    qn_b = q_nope.reshape(B, nb, qb, MLA_HEADS, MLA_NOPE).swapaxes(0, 1)
    qr_b = q_rope.reshape(B, nb, qb, MLA_HEADS, MLA_ROPE).swapaxes(0, 1)
    starts = jnp.arange(nb) * qb
    key_pos = jnp.arange(T)

    def block(args):
        qn, qr, s0 = args
        sc = (jnp.einsum('bqhd,bkhd->bhqk', qn, k_nope)
              + jnp.einsum('bqhd,bkd->bhqk', qr, k_rope)).astype(jnp.float32) * MLA_SCALE
        qpos = s0 + jnp.arange(qb)
        mask = key_pos[None, :] <= qpos[:, None]
        p = jax.nn.softmax(jnp.where(mask, sc, -jnp.inf), axis=-1)
        return jnp.einsum('bhqk,bkhd->bqhd', p.astype(v.dtype), v)

    o = lax.map(block, (qn_b, qr_b, starts))
    o = o.swapaxes(0, 1).reshape(B, T, MLA_HEADS * MLA_V)
    return o @ w_out, ckv, k_rope

def _mla_sample(x, lat_pages, rope_pages, page_table, w_in, q_norm, kv_norm, w_uq, w_ukv, w_out):
    B, T, _ = x.shape
    past = page_table.shape[1] * PAGE_SIZE
    pos = past + jnp.arange(T)
    q_nope, q_rope, ckv, k_rope = _mla_project(x, pos, w_in, q_norm, kv_norm, w_uq)
    lat_past = lat_pages[page_table].reshape(B, past, MLA_KV_RANK)
    rope_past = rope_pages[page_table].reshape(B, past, MLA_ROPE)
    lat_all = jnp.concatenate([lat_past.astype(ckv.dtype), ckv], axis=1)
    rope_all = jnp.concatenate([rope_past.astype(k_rope.dtype), k_rope], axis=1)
    w = w_ukv.reshape(MLA_KV_RANK, MLA_HEADS, MLA_NOPE + MLA_V)
    w_uk, w_uv = w[..., :MLA_NOPE], w[..., MLA_NOPE:]
    q_lat = jnp.einsum('bqhn,rhn->bqhr', q_nope, w_uk)
    sc = (jnp.einsum('bqhr,bkr->bhqk', q_lat, lat_all)
          + jnp.einsum('bqhd,bkd->bhqk', q_rope, rope_all)).astype(jnp.float32) * MLA_SCALE
    mask = jnp.arange(past + T)[None, :] <= pos[:, None]
    p = jax.nn.softmax(jnp.where(mask, sc, -jnp.inf), axis=-1)
    o_lat = jnp.einsum('bhqk,bkr->bqhr', p.astype(lat_all.dtype), lat_all)
    o = jnp.einsum('bqhr,rhv->bqhv', o_lat, w_uv).reshape(B, T, MLA_HEADS * MLA_V)
    return o @ w_out, ckv, k_rope

def _trunk(x, sample, gdn_S, gdn_conv, mla_lat, mla_rope, ml_C, ml_n, ml_m, page_table,
           norm_gains, w_ffn_up, w_ffn_down,
           gdn_w_in, gdn_conv_w, gdn_a_log, gdn_dt_bias, gdn_norm_w, gdn_w_out,
           mla_w_in, mla_q_norm, mla_kv_norm, mla_w_uq, mla_w_ukv, mla_w_out,
           mlstm_w_in, mlstm_i_bias, mlstm_f_bias, mlstm_w_out):
    new = ([], [], [], [], [], [], [])
    for layer in range(DEPTH):
        kind = LAYER_MIXER[layer]
        j = LAYER_MIXER[:layer].count(kind)
        ng = norm_gains[layer]
        x = x + 0.5 * _rmsnorm(_swiglu(_rmsnorm(x, ng[0]), w_ffn_up[layer, 0], w_ffn_down[layer, 0]), ng[1])
        h = _rmsnorm(x, ng[2])
        if kind == 0:
            h, s_new, c_new = _gdn_mixer(h, gdn_S[j], gdn_conv[j], gdn_w_in[j], gdn_conv_w[j], gdn_a_log[j],
                                         gdn_dt_bias[j], gdn_norm_w[j], gdn_w_out[j])
            new[0].append(s_new)
            new[1].append(c_new)
        elif kind == 1:
            if sample:
                h, lat, kr = _mla_sample(h, mla_lat[j], mla_rope[j], page_table, mla_w_in[j], mla_q_norm[j],
                                         mla_kv_norm[j], mla_w_uq[j], mla_w_ukv[j], mla_w_out[j])
            else:
                h, lat, kr = _mla_prompt(h, mla_w_in[j], mla_q_norm[j], mla_kv_norm[j], mla_w_uq[j],
                                         mla_w_ukv[j], mla_w_out[j])
                lat = lat.reshape(-1, PAGE_SIZE, MLA_KV_RANK)
                kr = kr.reshape(-1, PAGE_SIZE, MLA_ROPE)
            new[2].append(lat)
            new[3].append(kr)
        else:
            h, C, n, m = _mlstm_mixer(h, ml_C[j], ml_n[j], ml_m[j], mlstm_w_in[j], mlstm_i_bias[j],
                                      mlstm_f_bias[j], mlstm_w_out[j])
            new[4].append(C)
            new[5].append(n)
            new[6].append(m)
        x = x + _rmsnorm(h, ng[3])
        x = x + 0.5 * _rmsnorm(_swiglu(_rmsnorm(x, ng[4]), w_ffn_up[layer, 1], w_ffn_down[layer, 1]), ng[5])
    return x, [jnp.stack(s) for s in new]

def setup_inputs(seed: int = 0) -> dict:
    key = jax.random.key(seed)
    ks = jax.random.split(key, 32)
    f32 = jnp.float32
    n_pages = PAST_LEN // PAGE_SIZE
    n_phys = (5 * DEC_BATCH * n_pages + 3) // 4

    def nrm(k, shape, s=1.0):
        return s * jax.random.normal(k, shape, f32)

    def gain(k, shape):
        return 1.0 + 0.05 * jax.random.normal(k, shape, f32)

    perm = jax.random.permutation(ks[5], n_phys)
    page_table = perm[:DEC_BATCH * n_pages].reshape(DEC_BATCH, n_pages).astype(jnp.int32)
    dt = jnp.exp(jax.random.uniform(ks[13], (N_GDN, GDN_HEADS), f32, math.log(1e-3), math.log(1e-1)))
    dt_bias = dt + jnp.log(-jnp.expm1(-dt))
    a_log = jnp.log(jax.random.uniform(ks[16], (N_GDN, GDN_HEADS), f32, 1.0, 16.0))
    f_bias = jnp.linspace(3.0, 6.0, ML_HEADS, dtype=f32)[None, :] + nrm(ks[27], (N_MLSTM, ML_HEADS), 0.1)
    return {
        'x_prompt': nrm(ks[0], (BATCH, SEQ, D_MODEL)),
        'x_sample': nrm(ks[1], (DEC_BATCH, DEC_SEQ, D_MODEL)),
        'state_gdn_S': nrm(ks[2], (N_GDN, DEC_BATCH, GDN_HEADS, GDN_DK, GDN_DV), 0.5),
        'state_gdn_conv': nrm(ks[3], (N_GDN, DEC_BATCH, GDN_CONV - 1, GDN_QKV)),
        'cache_mla_latent': nrm(ks[4], (N_MLA, n_phys, PAGE_SIZE, MLA_KV_RANK)),
        'cache_mla_rope': nrm(ks[6], (N_MLA, n_phys, PAGE_SIZE, MLA_ROPE)),
        'state_mlstm_C': nrm(ks[7], (N_MLSTM, DEC_BATCH, ML_HEADS, ML_DK, ML_DV), 0.5),
        'state_mlstm_n': nrm(ks[8], (N_MLSTM, DEC_BATCH, ML_HEADS, ML_DK), 0.5),
        'state_mlstm_m': nrm(ks[9], (N_MLSTM, DEC_BATCH, ML_HEADS)),
        'page_table': page_table,
        'norm_gains': gain(ks[10], (DEPTH, 6, D_MODEL)),
        'w_ffn_up': nrm(ks[11], (DEPTH, 2, D_MODEL, 2 * D_FF), D_MODEL ** -0.5),
        'w_ffn_down': nrm(ks[12], (DEPTH, 2, D_FF, D_MODEL), D_FF ** -0.5),
        'gdn_w_in': nrm(ks[14], (N_GDN, D_MODEL, GDN_QKV + GDN_Z + 2 * GDN_HEADS), D_MODEL ** -0.5),
        'gdn_conv_w': nrm(ks[15], (N_GDN, GDN_CONV, GDN_QKV), GDN_CONV ** -0.5),
        'gdn_a_log': a_log,
        'gdn_dt_bias': dt_bias,
        'gdn_norm_w': gain(ks[17], (N_GDN, GDN_DV)),
        'gdn_w_out': nrm(ks[18], (N_GDN, GDN_Z, D_MODEL), GDN_Z ** -0.5),
        'mla_w_in': nrm(ks[19], (N_MLA, D_MODEL, MLA_Q_RANK + MLA_KV_RANK + MLA_ROPE), D_MODEL ** -0.5),
        'mla_q_norm': gain(ks[20], (N_MLA, MLA_Q_RANK)),
        'mla_kv_norm': gain(ks[21], (N_MLA, MLA_KV_RANK)),
        'mla_w_uq': nrm(ks[22], (N_MLA, MLA_Q_RANK, MLA_HEADS * (MLA_NOPE + MLA_ROPE)), MLA_Q_RANK ** -0.5),
        'mla_w_ukv': nrm(ks[23], (N_MLA, MLA_KV_RANK, MLA_HEADS * (MLA_NOPE + MLA_V)), MLA_KV_RANK ** -0.5),
        'mla_w_out': nrm(ks[24], (N_MLA, MLA_HEADS * MLA_V, D_MODEL), (MLA_HEADS * MLA_V) ** -0.5),
        'mlstm_w_in': nrm(ks[25], (N_MLSTM, D_MODEL, 2 * ML_QK + 2 * ML_V + 2 * ML_HEADS), D_MODEL ** -0.5),
        'mlstm_i_bias': nrm(ks[26], (N_MLSTM, ML_HEADS), 0.1),
        'mlstm_f_bias': f_bias,
        'mlstm_w_out': nrm(ks[28], (N_MLSTM, ML_V, D_MODEL), ML_V ** -0.5),
    }

def reference(x_prompt, x_sample, state_gdn_S, state_gdn_conv, cache_mla_latent, cache_mla_rope,
              state_mlstm_C, state_mlstm_n, state_mlstm_m, page_table,
              norm_gains, w_ffn_up, w_ffn_down,
              gdn_w_in, gdn_conv_w, gdn_a_log, gdn_dt_bias, gdn_norm_w, gdn_w_out,
              mla_w_in, mla_q_norm, mla_kv_norm, mla_w_uq, mla_w_ukv, mla_w_out,
              mlstm_w_in, mlstm_i_bias, mlstm_f_bias, mlstm_w_out):
    B = x_prompt.shape[0]
    dt = x_prompt.dtype
    z_S = jnp.zeros((N_GDN, B, GDN_HEADS, GDN_DK, GDN_DV), dt)
    z_conv = jnp.zeros((N_GDN, B, GDN_CONV - 1, GDN_QKV), dt)
    z_C = jnp.zeros((N_MLSTM, B, ML_HEADS, ML_DK, ML_DV), dt)
    z_n = jnp.zeros((N_MLSTM, B, ML_HEADS, ML_DK), dt)
    z_m = jnp.zeros((N_MLSTM, B, ML_HEADS), dt)
    y_prompt, st_p = _trunk(
        x_prompt, False, z_S, z_conv, None, None, z_C, z_n, z_m, None,
        norm_gains, w_ffn_up, w_ffn_down,
        gdn_w_in, gdn_conv_w, gdn_a_log, gdn_dt_bias, gdn_norm_w, gdn_w_out,
        mla_w_in, mla_q_norm, mla_kv_norm, mla_w_uq, mla_w_ukv, mla_w_out,
        mlstm_w_in, mlstm_i_bias, mlstm_f_bias, mlstm_w_out)
    y_sample, st_s = _trunk(
        x_sample, True, state_gdn_S, state_gdn_conv, cache_mla_latent, cache_mla_rope,
        state_mlstm_C, state_mlstm_n, state_mlstm_m, page_table,
        norm_gains, w_ffn_up, w_ffn_down,
        gdn_w_in, gdn_conv_w, gdn_a_log, gdn_dt_bias, gdn_norm_w, gdn_w_out,
        mla_w_in, mla_q_norm, mla_kv_norm, mla_w_uq, mla_w_ukv, mla_w_out,
        mlstm_w_in, mlstm_i_bias, mlstm_f_bias, mlstm_w_out)
    gdn_S_p, gdn_conv_p, mla_lat_p, mla_rope_p, ml_C_p, ml_n_p, ml_m_p = st_p
    gdn_S_s, gdn_conv_s, mla_lat_s, mla_rope_s, ml_C_s, ml_n_s, ml_m_s = st_s
    return (y_prompt, y_sample, gdn_S_p, gdn_S_s, gdn_conv_p, gdn_conv_s, mla_lat_p, mla_lat_s,
            mla_rope_p, mla_rope_s, ml_C_p, ml_C_s, ml_n_p, ml_n_s, ml_m_p, ml_m_s)


_drawn_inputs = setup_inputs


def setup_inputs(seed=0):
    import zlib

    import numpy as np

    out = dict(_drawn_inputs(seed))
    spreads = {}
    factors = {}
    for name, (base, spread) in spreads.items():
        noise = np.random.default_rng([zlib.crc32(name.encode()), seed]).standard_normal(out[name].shape)
        drawn = base * np.exp(spread * noise) if base else spread * noise
        out[name] = jnp.asarray(drawn.astype(out[name].dtype))
    for name, factor in factors.items():
        out[name] = (out[name] * factor).astype(out[name].dtype)
    return out
```

```python
from contextlib import ExitStack

import numpy as np

import concourse.bass as bass
from concourse import mybir

F32 = mybir.dt.float32
F32R = mybir.dt.float32r
I32 = mybir.dt.int32
ALU = mybir.AluOpType
ACT = mybir.ActivationFunctionType
AX = mybir.AxisListType

P = 128
D = 1024
KC = D // P
SEQ = 256
NB, NT = 8, 4
NS = NB * NT
T = SEQ + NS
DFF = ((8 * D // 3 + 127) // 128) * 128
FC = DFF // P
PAIRS = FC // 2
DEPTH = 4
MIXER = [i % 3 for i in range(DEPTH)]
EPS = 1e-6
CH = 128
HG = 8
MH = 8
LH = 4
GQKV = 3 * HG * P
PAST, PAGE = 2048, 128
NP = PAST // PAGE
N_PHYS = (5 * NB * NP + 3) // 4
QR, KVR, ROPE = 384, 256, 64
SCALE = (128 + 64) ** -0.5
LV = 7
NEG = -1e30

UNIT = 2048
NRAW = 4
NSPL = 2




def tables():
    def pack(items):
        cols, at, n = [], {}, 0
        for name, a in items:
            full = np.zeros((P, a.shape[1]), np.float32)
            full[:a.shape[0]] = a
            at[name] = (n, a.shape[1], a.shape[0])
            n += a.shape[1]
            cols.append(full)
        return np.concatenate(cols, axis=1), at

    j, i = np.arange(P)[:, None], np.arange(P)[None, :]
    js, si = np.arange(P)[:, None], np.arange(NS)[None, :]
    same = (js // NT == si // NT) & (js < NS)
    incl = np.concatenate([j <= i, j <= i, same & (js <= si)], axis=1)
    strict = np.concatenate([j < i, j < i, same & (js < si)], axis=1)
    tok = np.arange(T)
    start_s = (tok >= SEQ) & ((tok - SEQ) % NT == 0)
    start_g = start_s | ((tok < SEQ) & (tok % CH == 0))
    start_m = start_s | (tok == 0)
    rows = lambda a: np.tile(a.astype(np.float32), (8, 1))
    select = np.repeat(np.eye(8, dtype=np.float32), P, axis=1)
    mask = np.where(incl, 0.0, NEG).astype(np.float32)
    gdn = [("mask", mask), ("strict", strict.astype(np.float32))]
    for l in range(LV):
        b = 2 ** l
        gdn.append((f"level{l}", ((j // (2 * b) == i // (2 * b)) & (j // b < i // b)).astype(np.float32)))
    seqcol = (np.arange(NS)[:, None] // NT == np.arange(NB)[None, :]).astype(np.float32)
    gdn += [("keep", rows(~start_g)), ("select", select), ("seqcol", seqcol)]
    wide = np.concatenate([mask[:, 0:P], np.zeros((P, P), np.float32), mask[:, P:]], axis=1)
    mls = [("mask", wide), ("keep", rows(~start_m)), ("drop", rows(np.where(start_m, NEG, 0.0))),
           ("select", select), ("seqcol", seqcol)]
    half = ROPE // 2
    inv = (10000.0 ** (-np.arange(half, dtype=np.float32) / half)).astype(np.float32)
    pos = np.where(tok < SEQ, tok, PAST + (tok - SEQ) % NT).astype(np.float32)
    ang = (inv[:, None] * pos[None, :]).astype(np.float32)
    rot = np.zeros((ROPE, ROPE), np.float32)
    for m in range(half):
        rot[m + half, m] = -1.0
        rot[m, m + half] = 1.0
    causal = np.where(i <= j, 0.0, NEG).astype(np.float32)
    own = np.full((NS, NB, NS), NEG, np.float32)
    for b in range(NB):
        for r in range(NS):
            own[r, b, b * NT:b * NT + r % NT + 1] = 0.0
    mla = [("cos", np.concatenate([np.cos(ang)] * 2)), ("sin", np.concatenate([np.sin(ang)] * 2)),
           ("rot", rot), ("own", own.reshape(NS, NB * NS)), ("causal", np.concatenate([causal, 0 * causal, causal], axis=1))]
    base = [("ident", np.eye(P, dtype=np.float32)), ("ones", np.ones((P, P), np.float32))]
    return {"c_base": pack(base), "c_gdn": pack(gdn), "c_mla": pack(mla), "c_mlstm": pack(mls)}



SIGNALS = {
    "gdn": dict(
        g_tab_in=48, g_conv_in=16, g_conv_out=32, g_s_in0=64, g_s_in1=64, g_s_out0=128, g_s_out1=128,
        g_hist_turned=1, g_ss=8, g_tail_turned=6, g_col_turned=1, g_bc_done=8, g_kk=8, g_p_done=56,
        g_xp_done=48, g_ks=8, g_kd_turned=8, g_r_turned=8, g_vn_done=8, g_s1_done=8, g_o1_done=8, g_ks1=8,
        g_r1_turned=8, g_vn1_done=8, g_o_done=8, g_ds_done=8, g_oss=8, g_evac=16, g_silu=12, g_sq=8, g_qln=8,
        g_root=8, g_alog=1, g_act_seq=3, g_lnp=1, g_eb=1, g_rows=1, g_trow_ready=6, g_bc=8, g_dt=8, g_pc=48,
        g_kq=8, g_kd=8, g_vn=8, g_s1=8, g_r1=8, g_vn1=8, g_osq=8, g_oln=8, g_or=8, g_o_hi=8, g_gate_read=2,
        g_dve_seq=138, g_hist=1, g_cbuf_half=2, g_cbuf_set=1, g_conv=12, g_tail=12, g_qk_unit=8, g_abs=1,
        g_gg=1, g_beta=1, g_ncol=1, g_tm=8, g_ao=56, g_xupd=56, g_qg=8, g_kdt=8, g_rt=8, g_r=8, g_rt1=8, g_o=8,
        g_sp_new=8, g_kdb=8, g_s_new=8, g_on=8, g_o_split=8,
    ),
    "mla": dict(
        a_tab_in=32, a_pages_in=16, a_tok_out=96, a_lat_in0=2048, a_lat_in1=2048, a_wk_turned=4, a_css=1,
        a_krot=1, a_qrot=4, a_k_done=4, a_v_done=4, a_ql_done=1, a_tok_turned=1, a_sc_done=8, a_p_turned=8,
        a_pv_done=8, a_lat_turned=32, a_ssc_done=40, a_sp_turned=8, a_spv_done=8, a_so_done=1, a_craw=3,
        a_csq=2, a_act_seq=1, a_croot=1, a_cq_hi=1, a_q_evac=4, a_v=4, a_ql=1, a_p=8, a_pt=8, a_o_hi=5,
        a_latt_a=32, a_sp=8, a_wkt=4, a_cqn=1, a_ckv=1, a_cq_split=1, a_dve_seq=37, a_kr=1, a_q=4, a_k=4,
        a_tok=1, a_pm=8, a_max=8, a_pn=8, a_o_pair=4, a_o_low=4, a_o_split=2, a_latt=32, a_ssc=40, a_smax=8,
        a_spn=8, a_spt=8, a_sol=8, a_so=1,
    ),
    "mlstm": dict(
        l_tab_in=80, l_c_in0=32, l_c_in1=32, l_c_out0=64, l_c_out1=64, l_rows_out=64, l_n_turned=2,
        l_col_turned=1, l_bc_done=4, l_kk=4, l_num=4, l_kd_turned=4, l_cp_done=4, l_dc_done=4, l_evac=12,
        l_act_seq=1, l_lnp=1, l_rows=1, l_bc=4, l_w_ready=4, l_den=4, l_kd=4, l_cp=4, l_o_hi=4, l_n_out=1,
        l_dve_seq=33, l_abs=1, l_m_new=1, l_pre_rows=1, l_gate_sum=4, l_acol=1, l_tm=4, l_qn=4, l_st=4,
        l_kdt=4, l_nall=4, l_h=4, l_kdb=4, l_c_new=4, l_o_split=4,
    ),
}


MIXERS = ("gdn", "mla", "mlstm")
DOWN_K = (6, 6, 5, 5)
NGAIN = DEPTH * 6 * KC
NCONV = 2 * 4 * (GQKV // P)
V_GAIN, V_CONV, V_GN = 0, NGAIN, NGAIN + NCONV
V_QN, V_KVN, V_ALL = V_GN + 2, V_GN + 2 + QR // P, V_GN + 2 + QR // P + KVR // P


def sublayers():
    subs, seen = [], {}
    for l in range(DEPTH):
        kind = MIXERS[MIXER[l]]
        n = seen.get(kind, 0)
        seen[kind] = n + 1
        subs += [("ffn", l, 0), (kind, l, n), ("ffn", l, 1)]
    return subs


def cols_units(w, k, start, stop, group=256):
    v = w.rearrange("(k p) n -> p k n", p=P)
    return [(v[:, 0:k, c:min(c + group, stop)], k, min(group, stop - c)) for c in range(start, stop, group)]


def units_of(sub, a):
    kind, l, n = sub
    if kind == "ffn":
        up = a["w_ffn_up"][l, n].rearrange("(k p) n -> p k n", p=P)
        down = a["w_ffn_down"][l, n].rearrange("(k p) n -> p k n", p=P)
        out = []
        for j in range(PAIRS):
            for half in range(2):
                c = half * DFF + j * 256
                out.append((up[:, :, c:c + 256], KC, 256))
        for i in range(KC // 2):
            k = 0
            for nk in DOWN_K:
                out.append((down[:, k:k + nk, i * 256:(i + 1) * 256], nk, 256))
                k += nk
        return out
    if kind == "gdn":
        w = a["gdn_w_in"][n]
        return (cols_units(w, KC, GQKV + HG * P, GQKV + HG * P + 2 * HG) + cols_units(w, KC, 0, GQKV + HG * P)
                + cols_units(a["gdn_w_out"][n], KC, 0, D))
    if kind == "mla":
        w = a["mla_w_in"][n]
        return (cols_units(w, KC, 0, QR + KVR + ROPE) + cols_units(a["mla_w_uq"][n], QR // P, 0, MH * 192, 384)
                + cols_units(a["mla_w_out"][n], KC, 0, D))
    w = a["mlstm_w_in"][n]
    return (cols_units(w, KC, 3072, 3080) + cols_units(w, KC, 0, 3072) + cols_units(a["mlstm_w_out"][n], KC, 0, D))


def trunk(nc, a, subs):
    ctx = ExitStack()
    sems = {}
    TAB = tables()

    def sb(name, shape, dt=F32):
        return ctx.enter_context(nc.sbuf_tensor(name, shape, dt))

    place, counted = {}, {}
    for n, sub in enumerate(subs):
        place[n], used = {}, {}
        for name, count in SIGNALS.get(sub[0], {}).items():
            kind = "mix_dma" if count % 16 == 0 and name.endswith(("_in", "_in0", "_in1", "_out", "_out0", "_out1")) else "mix"
            used[kind] = used.get(kind, -1) + 1
            pool = f"{kind}{used[kind]}"
            place[n][name] = (pool, counted.get(pool, 0))
            counted[pool] = counted.get(pool, 0) + count
    here = [0]

    def sem(name):
        name = place[here[0]][name][0] if name in place.get(here[0], {}) else name
        if name not in sems:
            sems[name] = ctx.enter_context(nc.semaphore(name))
        return sems[name]

    def before(name):
        return place[here[0]][name][1] if name in place.get(here[0], {}) else 0

    def once(eng, name, v):
        eng.wait_ge(sem(name), v + before(name))

    with ctx:
        raw = [sb(f"raw{s}", [P, UNIT]) for s in range(NRAW)]
        w_hi = [sb(f"w_hi{s}", [P, UNIT], F32R) for s in range(NSPL)]
        w_lo = [sb(f"w_lo{s}", [P, UNIT], F32R) for s in range(NSPL)]
        x = sb("x", [P, KC, T])
        xn_hi = sb("xn_hi", [P, KC, T], F32R)
        xn_lo = sb("xn_lo", [P, KC, T], F32R)
        base = sb("base", [P, 2 * P])
        ident, ones = base[:, 0:P], base[:, P:2 * P]
        vec = sb("vec", [P, V_ALL])
        eps_t = sb("eps_t", [P, 2])
        rr = sb("rr", [P, 2, T])
        y = sb("y", [P, KC, T])
        sq = sb("sq", [P, KC, T])
        fbuf = sb("fbuf", [P, 2, 2, T])
        psum = ctx.enter_context(nc.psum_tensor("psum", [P, 8, 512], F32))
        free_at = -(-nc.sbuf_base // 64) * 64
        mix_words = (nc.sbuf_usable_end - free_at) // 4

        def at(name, shape, word, dt=F32):
            assert word + int(np.prod(shape[1:])) <= mix_words, (name, mix_words)
            return nc.alloc_sbuf_tensor_at(name, shape, dt, offset=free_at + 4 * word)
        h_hi = at("h_hi", [P, FC, T], 0, F32R)
        h_lo = at("h_lo", [P, FC, T], FC * T, F32R)
        sg = at("sg", [P, 2, 2, T], 2 * FC * T)

        raw_in = [sem(f"raw_in{s}") for s in range(NRAW)]
        hi_ready, lo_ready, unit_used = sem("hi_ready"), sem("lo_ready"), sem("unit_used")
        block = ctx.enter_context(nc.Block())

        units, ubase, uend = [], [], []
        for sub in subs:
            ubase.append(len(units))
            units += units_of(sub, a)
            uend.append(len(units))
        NU = len(units)
        NSUB = len(subs)
        nffn = [sum(q[0] == "ffn" for q in subs[:n]) for n in range(NSUB)]

        def gain(l, n, k):
            r = V_GAIN + (l * 6 + n) * KC + k
            return vec[:, r:r + 1]

        def post_gain(sub):
            return 3 if sub[0] != "ffn" else (1, 5)[sub[2]]

        def pre_gain(sub):
            return 2 if sub[0] != "ffn" else (0, 4)[sub[2]]

        def wview(buf, u):
            _, k, n = units[u]
            return buf[:, 0:k * n].rearrange("p (k n) -> p k n", k=k)

        def xin(t):
            return (y, sq, fbuf)[t][:].rearrange(("p k t -> p (k t)", "p a b t -> p (a b t)")[t == 2])[:, 0:D]

        vt = at("vt", [P, 4, P], (mix_words - 4 * P) // 8 * 8)

        def sp_unit(sp, u):
            if u >= NRAW:
                sp.wait_ge(lo_ready, u - NRAW + 1)
            sp.dma_start(wview(raw[u % NRAW], u), units[u][0]).then_inc(raw_in[u % NRAW], 16)

        def act_split(act, u, i=0):
            if u >= NU:
                return
            act.wait_ge(raw_in[u % NRAW], 16 * i + 16 * (u // NRAW + 1))
            if u >= NSPL:
                act.wait_ge(unit_used, 4 * i + u - NSPL + 1)
            act.activation(wview(w_hi[u % NSPL], u), wview(raw[u % NRAW], u), ACT.Copy).then_inc(hi_ready, 1)

        def dve_split(dve, u, i=0):
            if u >= NU:
                return
            dve.wait_ge(hi_ready, 4 * i + u + 1)
            dve.tensor_tensor(wview(w_lo[u % NSPL], u), wview(raw[u % NRAW], u),
                              wview(w_hi[u % NSPL], u).bitcast(F32), ALU.subtract).then_inc(lo_ready, 1)

        def pe_unit(pe, u, outs, hi, lo, start, stop, i=0, ready=None):
            _, nk, n = units[u]
            pe.wait_ge(lo_ready, 4 * i + u + 1)
            wh, wl = wview(w_hi[u % NSPL], u), wview(w_lo[u % NSPL], u)
            for m, out in enumerate(outs):
                c = slice(m * P, min((m + 1) * P, n))
                for k in range(nk):
                    if ready is not None and m == 0:
                        ready(k)
                    st, sp_ = start and k == 0, stop and k == nk - 1
                    pe.matmul(out, wh[:, k, c], hi(k), start=st, stop=False)
                    pe.matmul(out, wh[:, k, c], lo(k), start=False, stop=False)
                    last = pe.matmul(out, wl[:, k, c], hi(k), start=False, stop=sp_)
            last.then_inc(unit_used, 1)

        y_copied, sq_ready, ss_done, r_ready = sem("y_copied"), sem("sq_ready"), sem("ss_done"), sem("r_ready")
        x_ready, f_ready, xhi_ready, xlo_ready = sem("x_ready"), sem("f_ready"), sem("xhi_ready"), sem("xlo_ready")
        ln_done = sem("ln_done")
        half_ready = sem("half_ready")
        H = KC // 2

        def pe_sum_squares(pe, q):
            for i in range(H):
                pe.wait_ge(sq_ready, H * q + i + 1)
                for k in (2 * i, 2 * i + 1):
                    last = pe.matmul(psum[:, q % 2, 0:T], ones, sq[:, k, :], start=k == 0, stop=k == KC - 1)
            last.then_inc(ss_done, 1)

        def act_root(act, q):
            act.wait_ge(ss_done, q + 1)
            act.activation(rr[:, q % 2, :], psum[:, q % 2, 0:T], ACT.Ln, scale=1.0 / D,
                           bias=eps_t[:, 0:1]).then_inc(ln_done, 1)
            act.wait_ge(ln_done, q + 1)
            act.activation(rr[:, q % 2, :], rr[:, q % 2, :], ACT.Exp, scale=-0.5).then_inc(r_ready, 1)

        def act_pre(act, n):
            q = 2 * n
            for i in range(H):
                act.wait_ge(x_ready, H * n + i + 1)
                if q > 0:
                    act.wait_ge(ss_done, q)
                act.activation(sq[:, 2 * i:2 * i + 2, :], x[:, 2 * i:2 * i + 2, :], ACT.Square).then_inc(sq_ready, 1)
            act_root(act, q)
            for i in range(H):
                act.wait_ge(f_ready, H * n + i + 1)
                act.activation(xn_hi[:, 2 * i:2 * i + 2, :], fbuf[:, i % 2], ACT.Copy).then_inc(xhi_ready, 1)

        def dve_pre(dve, n):
            l, g = subs[n][1], pre_gain(subs[n])
            dve.wait_ge(r_ready, 2 * n + 1)
            if n == 0:
                dve.wait_ge(vec_ready, 3)
            for i in range(H + 1):
                if i < H:
                    if i >= 2:
                        dve.wait_ge(xlo_ready, H * n + i - 1)
                    for k in (2 * i, 2 * i + 1):
                        last = dve.scalar_tensor_tensor(out=fbuf[:, i % 2, k % 2], in0=x[:, k, :], scalar=gain(l, g, k),
                                                        in1=rr[:, 0, :], op0=ALU.mult, op1=ALU.mult)
                    last.then_inc(f_ready, 1)
                if i > 0:
                    dve.wait_ge(xhi_ready, H * n + i)
                    dve.tensor_tensor(xn_lo[:, 2 * i - 2:2 * i, :], fbuf[:, (i - 1) % 2],
                                      xn_hi[:, 2 * i - 2:2 * i, :].bitcast(F32), ALU.subtract).then_inc(xlo_ready, 1)

        def xn(part):
            return lambda k: part[:, k, :]

        def x_chunks(pe, n):
            return lambda k: pe.wait_ge(xlo_ready, H * n + k // 2 + 1) if k % 2 == 0 else None

        def dve_take_y(dve, n, i, u):
            dve.wait_ge(unit_used, u + 1)
            dve.tensor_copy(y[:, 2 * i:2 * i + 2, :], psum[:, 2 * i:2 * i + 2, 0:T]).then_inc(y_copied, 1)

        def act_square_y(act, n, i):
            act.wait_ge(y_copied, H * n + i + 1)
            act.activation(sq[:, 2 * i:2 * i + 2, :], y[:, 2 * i:2 * i + 2, :], ACT.Square).then_inc(sq_ready, 1)

        def dve_update(dve, n):
            l, g = subs[n][1], post_gain(subs[n])
            dve.wait_ge(r_ready, 2 * n + 2)
            t = sem("x_term")
            for i in range(H):
                for k in (2 * i, 2 * i + 1):
                    last = dve.scalar_tensor_tensor(out=y[:, k, :], in0=y[:, k, :], scalar=gain(l, g, k),
                                                    in1=rr[:, 1, :], op0=ALU.mult, op1=ALU.mult)
                last.then_inc(t, 1)
                if i > 0:
                    dve.wait_ge(t, H * n + i)
                    dve.tensor_tensor(x[:, 2 * i - 2:2 * i, :], x[:, 2 * i - 2:2 * i, :], y[:, 2 * i - 2:2 * i, :],
                                      ALU.add).then_inc(x_ready, 1)
            dve.wait_ge(t, H * (n + 1))
            dve.tensor_tensor(x[:, KC - 2:KC, :], x[:, KC - 2:KC, :], y[:, KC - 2:KC, :], ALU.add).then_inc(x_ready, 1)

        def pe_out(pe, n, u0, hi, lo, ready):
            for i in range(H):
                pe_unit(pe, u0 + i, [psum[:, 2 * i, 0:T], psum[:, 2 * i + 1, 0:T]], hi, lo, True, True,
                        ready=ready if i == 0 else None)

        silu_done, h_done, hhi_done, hlo_done = sem("silu_done"), sem("h_done"), sem("hhi_done"), sem("hlo_done")
        ROUNDS = PAIRS // 2
        DU = len(DOWN_K)

        def sp_ffn(sp, n):
            _, l, f = subs[n]
            up = a["w_ffn_up"][l, f].rearrange("(k p) n -> p k n", p=P)
            u0 = ubase[n]
            for q in range(4):
                sp_unit(sp, u0 + q)
            with sp.Fori(1, ROUNDS) as i:
                for q in range(4):
                    u = u0 + q
                    sp.wait_ge(lo_ready, 4 * i + u - NRAW + 1)
                    sp.dma_start(wview(raw[u % NRAW], u),
                                 up[:, :, bass.ds(512 * i + (q // 2) * 256 + (q % 2) * DFF, 256)]
                                 ).then_inc(raw_in[u % NRAW], 16)
            for u in range(u0 + 4 * ROUNDS, uend[n]):
                sp_unit(sp, u)

        def pe_ffn(pe, n):
            u0, f0 = ubase[n], nffn[n] * PAIRS

            def pair(j, i, jj):
                s = 4 * ((j + 1) % 2)
                if jj is None or jj >= 2:
                    pe.wait_ge(h_done, 2 * i + f0 + j - 1)
                first = x_chunks(pe, n) if jj == 0 else None
                for g in range(2):
                    pe_unit(pe, u0 + 2 * j + g, [psum[:, s + 2 * g, 0:T], psum[:, s + 2 * g + 1, 0:T]],
                            xn(xn_hi), xn(xn_lo), True, True, i=i, ready=first if g == 0 else None)
            pair(0, 0, 0)
            pair(1, 0, 1)
            with pe.Fori(1, ROUNDS) as i:
                pair(0, i, None)
                pair(1, i, None)
            pair(PAIRS - 1, 0, PAIRS - 1)
            for i in range(H):
                if i in (0, 2):
                    pe.wait_ge(h_done, f0 + PAIRS - 1 + i // 2)
                k0 = 0
                for q, nk in enumerate(DOWN_K):
                    if i == 0:
                        pe.wait_ge(hlo_done, f0 + -(-(k0 + nk) // 2))
                    pe_unit(pe, u0 + 2 * PAIRS + DU * i + q, [psum[:, 2 * i, 0:T], psum[:, 2 * i + 1, 0:T]],
                            lambda k: h_hi[:, k0 + k, :], lambda k: h_lo[:, k0 + k, :], q == 0, q == DU - 1)
                    k0 += nk

        def act_ffn(act, n):
            u0, f0 = ubase[n], nffn[n] * PAIRS

            def high(j, i):
                act.wait_ge(h_done, 2 * i + f0 + j + 1)
                dst = h_hi[:, 2 * j:2 * j + 2, :] if isinstance(i, int) else h_hi[:, bass.ds(4 * i + 2 * j, 2), :]
                act.activation(dst, fbuf[:, j % 2], ACT.Copy).then_inc(hhi_done, 1)

            def pair(j, i, jj):
                s = 4 * ((j + 1) % 2)
                act_split(act, u0 + 2 * j + 1, i)
                if jj is None or jj > 0:
                    high_before(j, i)
                act_split(act, u0 + 2 * j + 2, i)
                act.wait_ge(unit_used, 4 * i + u0 + 2 * j + 2)
                if jj is None or jj >= 2:
                    act.wait_ge(h_done, 2 * i + f0 + j - 1)
                act.activation(sg[:, j % 2], psum[:, s:s + 2, 0:T], ACT.Silu).then_inc(silu_done, 1)

            def high_before(j, i):
                if j > 0:
                    high(j - 1, i)
                else:
                    act.wait_ge(h_done, 2 * i + f0)
                    act.activation(h_hi[:, bass.ds(4 * i - 2, 2), :], fbuf[:, 1], ACT.Copy).then_inc(hhi_done, 1)
            pair(0, 0, 0)
            pair(1, 0, 1)
            with act.Fori(1, ROUNDS) as i:
                pair(0, i, None)
                pair(1, i, None)
            pair(PAIRS - 1, 0, PAIRS - 1)
            high(PAIRS - 1, 0)
            for i in range(H):
                for q in range(DU):
                    act_split(act, u0 + 2 * PAIRS + DU * i + q + 1)
                    if i > 0 and q == 0:
                        act_square_y(act, n, i - 1)
            act_square_y(act, n, H - 1)

        def dve_ffn(dve, n):
            u0, f0 = ubase[n], nffn[n] * PAIRS

            def low(j, i, before=0):
                dve.wait_ge(hhi_done, 2 * i + f0 + j + 1 - before)
                k = 2 * (j - before)
                sl = slice(k, k + 2) if isinstance(i, int) else bass.ds(4 * i + k, 2)
                dve.tensor_tensor(h_lo[:, sl, :], fbuf[:, (j - before) % 2], h_hi[:, sl, :].bitcast(F32),
                                  ALU.subtract).then_inc(hlo_done, 1)

            def pair(j, i, jj):
                s = 4 * ((j + 1) % 2)
                dve_split(dve, u0 + 2 * j + 1, i)
                if jj is None or jj > 0:
                    low(j, i, before=1)
                dve_split(dve, u0 + 2 * j + 2, i)
                dve.wait_ge(silu_done, 2 * i + f0 + j + 1)
                if jj is None or jj >= 2:
                    dve.wait_ge(hlo_done, 2 * i + f0 + j - 1)
                else:
                    dve.wait_ge(xlo_ready, H * (n + 1))
                dve.tensor_tensor(fbuf[:, j % 2], sg[:, j % 2], psum[:, s + 2:s + 4, 0:T], ALU.mult).then_inc(h_done, 1)
            pair(0, 0, 0)
            pair(1, 0, 1)
            with dve.Fori(1, ROUNDS) as i:
                pair(0, i, None)
                pair(1, i, None)
            pair(PAIRS - 1, 0, PAIRS - 1)
            low(PAIRS - 1, 0)
            for i in range(H):
                for q in range(DU):
                    dve_split(dve, u0 + 2 * PAIRS + DU * i + q + 1)
                    if i > 0 and q == 0:
                        dve_take_y(dve, n, i - 1, u0 + 2 * PAIRS + DU * i - 1)
            dve_take_y(dve, n, H - 1, uend[n] - 1)

        SP, PE, ACTE, DVE, POOL = {"ffn": sp_ffn}, {"ffn": pe_ffn}, {"ffn": act_ffn}, {"ffn": dve_ffn}, {}

        token_tiles = [(slice(0, P), a["x_prompt"][0, 0:P, :], a["y_prompt"][0, 0:P, :]),
                       (slice(P, 2 * P), a["x_prompt"][0, P:2 * P, :], a["y_prompt"][0, P:2 * P, :]),
                       (slice(SEQ, T), a["x_sample"].rearrange("b t d -> (b t) d"),
                        a["y_sample"].rearrange("b t d -> (b t) d"))]

        table = {k: v for k, (_, v) in TAB.items()}
        w = [0]

        def carve(name, shape):
            t = at(name, shape, w[0])
            w[0] += -(-int(np.prod(shape[1:])) // 8) * 8
            return t
        KDB = sq[0:NS, 4:8, :].rearrange("p k t -> p (k t)")[:, 0:NB * P].rearrange("p (b e) -> p b e", b=NB)
        if any(q[0] == "gdn" for q in subs):
            GN = TAB["c_gdn"][0].shape[1]
            qkv = carve("g_qkv", [P, 3 * HG, T])
            gz = carve("g_z", [P, HG, T])
            gtab = carve("g_tab", [P, GN])
            gsm = carve("g_small", [HG, 4])
            ncol = carve("g_ncol", [P, 3, HG])
            w1 = w[0]
            crow = carve("g_crow", [NB * 3, GQKV])
            trow = carve("g_trow", [NB * 3 + 3, GQKV])
            CW = 3 + SEQ + NB * 7
            cbuf = carve("g_cbuf", [P, 2, 2, CW])
            cacc = carve("g_cacc", [P, 2, 2, CW])
            chist = carve("g_chist", [P, 3 * HG, NB * 3])
            tail = carve("g_tail", [P, 3 * HG, NB * 3 + 3])
            w[0] = w1
            X, XT, AT, AN, AO, PC = (carve("g_" + q, [P, 2, T]) for q in ("x", "xt", "at", "an", "ao", "pc"))
            bc = carve("g_bc", [P, 2, 4, T])
            Sin = carve("g_sin", [P, 2, NB, P])
            Sp = carve("g_sp", [P, 2, P])
            R, VN, KD = (carve("g_" + q, [P, 3, P]) for q in ("r", "vn", "kd"))
            R2, VN2, KD2 = (carve("g_" + q, [P, 3, P]) for q in ("r2", "vn2", "kd2"))
            kq = carve("g_kq", [P, 2, NB, 2, NT])
            RS, VS, KS_ = (R, R2), (VN, VN2), (KD, KD2)

        def gt(name):
            o, n, r = table["c_gdn"][name]
            return gtab[0:r, o:o + n]

        CHUNKS = (slice(0, CH), slice(CH, SEQ), slice(SEQ, T))
        rows8 = lambda r: y[0:HG, r, :]
        BETA, EG, ED, GG, T1, T2, T3 = range(7)
        smp = lambda v: v[..., SEQ:T]
        GP = HG // 2

        def sp_gdn(sp, n):
            gi, u0 = subs[n][2], ubase[n]
            if n > 0:
                once(sp, "unit_used", u0)
            sp.dma_start(gtab[:], a["c_gdn"]).then_inc(sem("g_tab_in"), 16)
            sp.dma_start(gsm[:, 0:1], a["gdn_dt_bias"][gi].rearrange("(h o) -> h o", o=1)).then_inc(sem("g_tab_in"), 16)
            sp.dma_start(gsm[:, 1:2], a["gdn_a_log"][gi].rearrange("(h o) -> h o", o=1)).then_inc(sem("g_tab_in"), 16)
            sp.dma_start(crow[:], a["state_gdn_conv"][gi].rearrange("b j c -> (b j) c")).then_inc(sem("g_conv_in"), 16)
            for u in range(u0, uend[n]):
                sp_unit(sp, u)
                if u == u0 + 17 + 2:
                    heads_io(sp, gi)
        def heads_io(sp, gi):
            once(sp, "g_trow_ready", 6)
            sp.dma_start(a["gdn_conv_p"][gi, 0], trow[0:3, :]).then_inc(sem("g_conv_out"), 16)
            sp.dma_start(a["gdn_conv_s"][gi].rearrange("b j c -> (b j) c"), trow[3:27, :]).then_inc(sem("g_conv_out"), 16)
            once(sp, "g_conv_out", 32)
            for h in range(HG + 2):
                if h >= 2:
                    q = h - 2
                    once(sp, "g_s_new", q + 1)
                    sp.dma_start(a["gdn_S_s"][gi, :, h - 2].rearrange("b d e -> d b e"), Sin[:, h % 2]
                                 ).then_inc(sem(f"g_s_out{h % 2}"), 16)
                    once(sp, "g_sp_new", q + 1)
                    sp.dma_start(a["gdn_S_p"][gi, 0, h - 2], Sp[:, h % 2]).then_inc(sem(f"g_s_out{h % 2}"), 16)
                    once(sp, f"g_s_out{h % 2}", 32 * (h // 2))
                if h < HG:
                    sp.dma_start(Sin[:, h % 2], a["state_gdn_S"][gi, :, h].rearrange("b d e -> d b e")
                                 ).then_inc(sem(f"g_s_in{h % 2}"), 16)

        def pe_gdn(pe, n):
            gi, u0 = subs[n][2], ubase[n]
            gates = [psum[0:HG, 4, 0:T], psum[0:HG, 5, 0:T]]
            pe.wait_ge(lo_ready, u0 + 1)
            wh, wl = wview(w_hi[u0 % NSPL], u0), wview(w_lo[u0 % NSPL], u0)
            ready = x_chunks(pe, n)
            for m in range(2):
                for k in range(KC):
                    if m == 0:
                        ready(k)
                    c = slice(m * HG, (m + 1) * HG)
                    pe.matmul(gates[m], wh[:, k, c], xn_hi[:, k, :], start=k == 0, stop=False)
                    pe.matmul(gates[m], wh[:, k, c], xn_lo[:, k, :], start=False, stop=False)
                    last = pe.matmul(gates[m], wl[:, k, c], xn_hi[:, k, :], start=False, stop=k == KC - 1)
            last.then_inc(unit_used, 1)
            once(pe, "g_conv_in", 16)
            for k in range(3 * HG):
                last = pe.transpose(psum[:, 6 + k // 12, (k % 12) * 24:(k % 12) * 24 + 24],
                                    crow[:, k * P:(k + 1) * P], ident[0:24, 0:24])
            last.then_inc(sem("g_hist_turned"), 1)
            for i in range(16):
                if i >= 2:
                    once(pe, "g_evac", i - 1)
                pe_unit(pe, u0 + 1 + i, [psum[:, 2 * (i % 2), 0:T], psum[:, 2 * (i % 2) + 1, 0:T]],
                        xn(xn_hi), xn(xn_lo), True, True)
            for q in range(8):
                once(pe, "g_sq", q + 1)
                if q == 0:
                    once(pe, "g_hist", 1)
                    once(pe, "g_gate_read", 2)
                if q >= 2:
                    once(pe, "g_root", q - 1)
                for k in range(2):
                    last = pe.matmul(psum[:, 4 + 2 * (q % 2) + k, 0:T], ones, sq[:, 2 * (q % 4) + k, :],
                                     start=True, stop=True)
                last.then_inc(sem("g_ss"), 1)
            once(pe, "g_tail", 12)
            for k in range(3 * HG):
                if k == 0:
                    once(pe, "g_evac", 16)
                if k >= 8 and k % 4 == 0:
                    once(pe, "g_trow_ready", k // 4 - 1)
                last = pe.transpose(psum[0:27, (k // 4) % 2, (k % 4) * P:(k % 4 + 1) * P], tail[:, k, :], ident)
                if k % 4 == 3:
                    last.then_inc(sem("g_tail_turned"), 1)
            once(pe, "g_rows", 1)
            once(pe, "g_root", 8)
            for c, cs in enumerate(CHUNKS):
                last = pe.transpose(psum[0:cs.stop - cs.start, 4, c * HG:(c + 1) * HG], rows8(GG)[:, cs],
                                    ident[0:HG, 0:HG])
            last.then_inc(sem("g_col_turned"), 1)
            once(pe, "g_trow_ready", 6)
            once(pe, "g_ncol", 1)
            once(pe, "g_qk_unit", 8)
            flat = qkv[:].rearrange("p k t -> p (k t)")
            for p in range(GP):
                hh = [2 * p, 2 * p + 1]
                for s in range(2):
                    if p > 0:
                        once(pe, "g_o_split", hh[s] - 1)
                    for r in range(4):
                        last = pe.matmul(psum[:, 4 * s + r, 0:T], gt("select")[:, (2 * p + s) * P:(2 * p + s + 1) * P],
                                         rows8(r), start=True, stop=True)
                    last.then_inc(sem("g_bc_done"), 1)
                for s in range(2):
                    once(pe, "g_bc", hh[s] + 1)
                    kh, qh = (HG + 2 * p + s) * T, (2 * p + s) * T
                    for c, cs in enumerate(CHUNKS):
                        keys = flat[:, kh + cs.start:kh + cs.start + P]
                        pe.matmul(psum[:, 4 * s, cs], keys, flat[:, kh + cs.start:kh + cs.stop], start=True, stop=True)
                        last = pe.matmul(psum[:, 4 * s + 1, cs], keys, flat[:, qh + cs.start:qh + cs.stop],
                                         start=True, stop=True)
                    last.then_inc(sem("g_kk"), 1)
                for l in range(LV):
                    ch = CHUNKS if l < 2 else CHUNKS[0:2]
                    e = lambda s: (p * LV + l) * 2 + s + 1
                    for s in range(2):
                        once(pe, "g_ao", e(s))
                        if l > 0:
                            once(pe, "g_xupd", e(s) - 2)
                        for cs in ch:
                            m = cs.stop - cs.start
                            rhs = ident[0:m, 0:m] if l == 0 else X[0:m, s, cs]
                            last = pe.matmul(psum[0:m, 4 * s + 2, cs], AO[0:m, s, cs], rhs, start=True, stop=True)
                        last.then_inc(sem("g_p_done"), 1)
                    for s in range(2):
                        if l == 0:
                            continue
                        once(pe, "g_pc", (p * (LV - 1) + l - 1) * 2 + s + 1)
                        for cs in ch:
                            m = cs.stop - cs.start
                            if l < LV - 1:
                                pe.matmul(psum[0:m, 4 * s, cs], XT[0:m, s, cs], PC[0:m, s, cs], start=True, stop=True)
                            last = pe.matmul(psum[0:m, 4 * s + 3, cs], PC[0:m, s, cs], XT[0:m, s, cs],
                                             start=True, stop=True)
                        last.then_inc(sem("g_xp_done"), 1)
                B = lambda s, b: psum[:, 4 * s + b, :]
                for s in range(2):
                    once(pe, "g_kq", hh[s] + 1)
                    once(pe, f"g_s_in{s}", 16 * (p + 1))
                    for b in range(NB):
                        last = pe.matmul(B(s, 0)[:, 8 * b:8 * b + 8], Sin[:, s, b, :],
                                         kq[:, s, b].rearrange("p a t -> p (a t)"), start=True, stop=True)
                    last.then_inc(sem("g_ks"), 1)
                for s in range(2):
                    once(pe, "g_kdt", hh[s] + 1)
                    for c, cs in enumerate(CHUNKS):
                        last = pe.transpose(B(s, 2)[0:cs.stop - cs.start, c * P:(c + 1) * P], AO[:, s, cs], ident)
                    last.then_inc(sem("g_kd_turned"), 1)
                    once(pe, "g_rt", hh[s] + 1)
                    pe.transpose(B(s, 1)[:, 0:P], X[:, s, CHUNKS[0]], ident)
                    pe.transpose(B(s, 1)[0:NS, P:2 * P], X[:, s, CHUNKS[2]], ident).then_inc(sem("g_r_turned"), 1)
                for s in range(2):
                    once(pe, "g_r", hh[s] + 1)
                    pe.matmul(B(s, 0)[:, 192:320], XT[:, s, CHUNKS[0]], RS[s][:, 0, :], start=True, stop=True)
                    pe.matmul(B(s, 0)[0:NS, 320:448], XT[0:NS, s, CHUNKS[2]], RS[s][0:NS, 2, :],
                              start=True, stop=True).then_inc(sem("g_vn_done"), 1)
                for s in range(2):
                    once(pe, "g_vn", hh[s] + 1)
                    once(pe, "g_kd", hh[s] + 1)
                    pe.matmul(B(s, 2)[:, 384:512], KS_[s][:, 0, :], VS[s][:, 0, :], start=True,
                              stop=True).then_inc(sem("g_s1_done"), 1)
                    pe.matmul(B(s, 3)[:, CHUNKS[0]], VS[s][:, 0, :], AN[:, s, CHUNKS[0]], start=True, stop=True)
                    pe.matmul(B(s, 3)[:, CHUNKS[2]], VS[s][0:NS, 2, :], AN[0:NS, s, CHUNKS[2]], start=True,
                              stop=True).then_inc(sem("g_o1_done"), 1)
                for s in range(2):
                    once(pe, "g_s1", hh[s] + 1)
                    kh = (HG + 2 * p + s)
                    pe.matmul(B(s, 0)[:, 64:192], Sp[:, s, :], qkv[:, kh, CHUNKS[1]], start=True,
                              stop=True).then_inc(sem("g_ks1"), 1)
                for s in range(2):
                    once(pe, "g_rt1", hh[s] + 1)
                    pe.transpose(B(s, 1)[:, 256:384], X[:, s, CHUNKS[1]], ident).then_inc(sem("g_r1_turned"), 1)
                for s in range(2):
                    once(pe, "g_r1", hh[s] + 1)
                    pe.matmul(B(s, 0)[:, 192:320], XT[:, s, CHUNKS[1]], RS[s][:, 1, :], start=True,
                              stop=True).then_inc(sem("g_vn1_done"), 1)
                for s in range(2):
                    once(pe, "g_vn1", hh[s] + 1)
                    pe.matmul(B(s, 1)[:, 384:512], KS_[s][:, 1, :], VS[s][:, 1, :], start=True, stop=True)
                    pe.matmul(B(s, 3)[:, CHUNKS[1]], Sp[:, s, :], PC[:, s, CHUNKS[1]], start=True, stop=False)
                    pe.matmul(B(s, 3)[:, CHUNKS[1]], VS[s][:, 1, :], AN[:, s, CHUNKS[1]], start=False,
                              stop=True).then_inc(sem("g_o_done"), 1)
                for s in range(2):
                    once(pe, "g_kdb", hh[s] + 1)
                    once(pe, "g_sp_new", hh[s] + 1)
                    for b in range(NB):
                        last = pe.matmul(B(s, b // 4)[:, (b % 4) * P:(b % 4 + 1) * P], KDB[:, b, :],
                                         VS[s][0:NS, 2, :], start=True, stop=True)
                    last.then_inc(sem("g_ds_done"), 1)
                for s in range(2):
                    once(pe, "g_osq", hh[s] + 1)
                    pe.matmul(B(s, 2)[:, 0:T], ones, sq[:, s, :], start=True, stop=True).then_inc(sem("g_oss"), 1)
            once(pe, "g_o_split", HG)
            pe_out(pe, n, u0 + 17, xn(xn_hi), xn(xn_lo), None)

        def act_gdn(act, n):
            gi, u0 = subs[n][2], ubase[n]
            seq = sem("g_act_seq")
            act_split(act, u0 + 1)
            for i in range(16):
                act_split(act, u0 + i + 2)
                act.wait_ge(unit_used, u0 + i + 2)
                b = 2 * (i % 2)
                src = psum[:, b:b + 2, :]
                if i < 12:
                    if i >= 2:
                        once(act, "g_tail", i - 1)
                        once(act, "g_conv", i - 1)
                    else:
                        once(act, "g_cbuf_set", 1)
                    act.activation(cbuf[:, i % 2, :, 3:3 + SEQ], src[:, :, 0:SEQ], ACT.Copy)
                    for k in range(2):
                        last = act.activation(
                            cbuf[:, i % 2, k, 3 + SEQ:CW].rearrange("p (b t) -> p b t", b=NB)[:, :, 3:7],
                            src[:, k, SEQ:T].rearrange("p (b t) -> p b t", b=NB), ACT.Copy)
                    last.then_inc(sem("g_evac"), 1)
                else:
                    z2 = 2 * (i - 12)
                    act.activation(gz[:, z2:z2 + 2, :], src[:, :, 0:T], ACT.Silu).then_inc(sem("g_evac"), 1)
                if i >= 1 and i <= 12:
                    conv_silu(act, i - 1)
            for q in range(8):
                if q >= 4:
                    once(act, "g_ss", q - 3)
                act.activation(sq[:, 2 * (q % 4):2 * (q % 4) + 2, :], qkv[:, 2 * q:2 * q + 2, :],
                               ACT.Square).then_inc(sem("g_sq"), 1)
                if q >= 1:
                    qk_root(act, q - 1)
            qk_root(act, 7)
            once(act, "g_tab_in", 48)
            act.activation(gsm[:, 2:3], gsm[:, 1:2], ACT.Exp).then_inc(sem("g_alog"), 1)
            once(act, "g_abs", 1)
            act.activation(rows8(T2), rows8(T2), ACT.Exp, scale=-1.0).then_inc(seq, 1)
            act.wait_ge(seq, before("g_act_seq") + 1)
            act.activation(rows8(T3), rows8(T2), ACT.Ln, bias=ones[0:HG, 0:1]).then_inc(sem("g_lnp"), 1)
            act.activation(rows8(BETA), rows8(BETA), ACT.Exp, scale=-1.0).then_inc(sem("g_eb"), 1)
            once(act, "g_gg", 1)
            act.activation(rows8(EG), rows8(GG), ACT.Exp).then_inc(seq, 1)
            act.activation(rows8(ED), rows8(ED), ACT.Exp).then_inc(seq, 1)
            act.wait_ge(seq, before("g_act_seq") + 3)
            once(act, "g_beta", 1)
            act.activation(gsm[:, 3:4], gsm[:, 2:3], ACT.Copy).then_inc(sem("g_rows"), 1)
            for q in range(6):
                once(act, "g_tail_turned", q + 1)
                act.activation(trow[:, 512 * q:512 * q + 512], psum[0:27, q % 2, :], ACT.Copy
                               ).then_inc(sem("g_trow_ready"), 1)
            for p in range(GP):
                hh = [2 * p, 2 * p + 1]
                for s in range(2):
                    once(act, "g_bc_done", hh[s] + 1)
                    if p == 0:
                        once(act, "g_conv_out", 32)
                    act.activation(bc[:, s], psum[:, 4 * s:4 * s + 4, 0:T], ACT.Copy).then_inc(sem("g_bc"), 1)
                for s in range(2):
                    once(act, "g_tm", hh[s] + 1)
                    for c, cs in enumerate(CHUNKS):
                        last = act.activation(X[:, s, cs], PC[:, s, cs], ACT.Exp, bias=ncol[:, c, 2 * p + s:2 * p + s + 1])
                    last.then_inc(sem("g_dt"), 1)
                for l in range(1, LV):
                    for s in range(2):
                        once(act, "g_p_done", (p * LV + l) * 2 + s + 1)
                        last = act.activation(PC[:, s, 0:SEQ], psum[:, 4 * s + 2, 0:SEQ], ACT.Copy)
                        if l < 2:
                            last = act.activation(PC[0:NS, s, SEQ:T], psum[0:NS, 4 * s + 2, SEQ:T], ACT.Copy)
                        last.then_inc(sem("g_pc"), 1)
                for s in range(2):
                    once(act, "g_qg", hh[s] + 1)
                    act.activation(kq[:, s, :, 0, :], smp(qkv[:, HG + 2 * p + s, :]).rearrange("p (b t) -> p b t", b=NB),
                                   ACT.Copy)
                    act.activation(kq[:, s, :, 1, :], smp(PC[:, s, :]).rearrange("p (b t) -> p b t", b=NB),
                                   ACT.Copy).then_inc(sem("g_kq"), 1)
                for s in range(2):
                    once(act, "g_kd_turned", hh[s] + 1)
                    act.activation(KS_[s][:, 0:2, :], psum[:, 4 * s + 2, 0:SEQ].rearrange("p (c e) -> p c e", c=2), ACT.Copy)
                    act.activation(KS_[s][0:NS, 2, :], psum[0:NS, 4 * s + 2, SEQ:SEQ + P], ACT.Copy
                                   ).then_inc(sem("g_kd"), 1)
                for s in range(2):
                    once(act, "g_vn_done", hh[s] + 1)
                    act.activation(VS[s][:, 0, :], psum[:, 4 * s, 192:320], ACT.Copy)
                    act.activation(VS[s][0:NS, 2, :], psum[0:NS, 4 * s, 320:448], ACT.Copy).then_inc(sem("g_vn"), 1)
                for s in range(2):
                    once(act, "g_s1_done", hh[s] + 1)
                    act.activation(Sp[:, s, :], psum[:, 4 * s + 2, 384:512], ACT.Copy).then_inc(sem("g_s1"), 1)
                for s in range(2):
                    once(act, "g_r1_turned", hh[s] + 1)
                    act.activation(RS[s][:, 1, :], psum[:, 4 * s + 1, 256:384], ACT.Copy).then_inc(sem("g_r1"), 1)
                for s in range(2):
                    once(act, "g_vn1_done", hh[s] + 1)
                    act.activation(VS[s][:, 1, :], psum[:, 4 * s, 192:320], ACT.Copy).then_inc(sem("g_vn1"), 1)
                for s in range(2):
                    once(act, "g_o", hh[s] + 1)
                    act.activation(sq[:, s, :], qkv[:, 2 * p + s, :], ACT.Square).then_inc(sem("g_osq"), 1)
                for s in range(2):
                    once(act, "g_oss", hh[s] + 1)
                    act.activation(sq[:, 2 + s, :], psum[:, 4 * s + 2, 0:T], ACT.Ln, scale=1.0 / P,
                                   bias=eps_t[:, 0:1]).then_inc(sem("g_oln"), 1)
                    once(act, "g_oln", hh[s] + 1)
                    act.activation(sq[:, 2 + s, :], sq[:, 2 + s, :], ACT.Exp, scale=-0.5).then_inc(sem("g_or"), 1)
                for s in range(2):
                    once(act, "g_on", hh[s] + 1)
                    act.activation(xn_hi[:, 2 * p + s, :], fbuf[:, s, 1, :], ACT.Copy).then_inc(sem("g_o_hi"), 1)
            for i in range(H):
                act_split(act, u0 + 17 + i + 1)
                act_square_y(act, n, i)

        def conv_silu(act, i):
            once(act, "g_conv", i + 1)
            act.activation(qkv[:, 2 * i:2 * i + 2, 0:SEQ], cacc[:, i % 2, :, 0:SEQ], ACT.Silu)
            for k in range(2):
                last = act.activation(smp(qkv[:, 2 * i + k, :]).rearrange("p (b t) -> p b t", b=NB),
                                      cacc[:, i % 2, k, 3 + SEQ:CW].rearrange("p (b t) -> p b t", b=NB)[:, :, 0:NT],
                                      ACT.Silu)
            last.then_inc(sem("g_silu"), 1)

        def qk_root(act, q):
            once(act, "g_ss", q + 1)
            if q >= 2:
                once(act, "g_qk_unit", q - 1)
            e = 1 if q < 4 else 0
            act.activation(fbuf[:, q % 2], psum[:, 4 + 2 * (q % 2):6 + 2 * (q % 2), 0:T], ACT.Ln,
                           scale=float(P) if e else 1.0, bias=eps_t[:, e:e + 1]).then_inc(sem("g_qln"), 1)
            once(act, "g_qln", q + 1)
            act.activation(fbuf[:, q % 2], fbuf[:, q % 2], ACT.Exp, scale=-0.5).then_inc(sem("g_root"), 1)

        def dve_gdn(dve, n):
            gi, u0 = subs[n][2], ubase[n]
            seq, cnt = sem("g_dve_seq"), [0]

            def step(ins):
                cnt[0] += 1
                ins.then_inc(seq, 1)
                dve.wait_ge(seq, before("g_dve_seq") + cnt[0])
            dve_split(dve, u0 + 1)
            if n > 0:
                dve.wait_ge(unit_used, u0)
            for s in range(2):
                last = dve.memset(cbuf[:, s, :, 0:3], 0.0)
            dve.memset(ncol[:], 0.0)
            dve.wait_ge(unit_used, u0 + 1)
            once(dve, "g_tab_in", 48)
            dve.tensor_copy(rows8(BETA), psum[0:HG, 4, 0:T]).then_inc(sem("g_gate_read"), 1)
            dve.tensor_scalar(rows8(T1), psum[0:HG, 5, 0:T], gsm[:, 0:1], None, ALU.add).then_inc(sem("g_gate_read"), 1)
            once(dve, "g_hist_turned", 1)
            step(dve.tensor_copy(chist[:].rearrange("p (a k) t -> p a (k t)", a=2), psum[:, 6:8, 0:288]))
            dve.tensor_copy(chist[:, 0, 0:1], chist[:, 0, 0:1]).then_inc(sem("g_hist"), 1)
            once(dve, "g_hist", 1)
            for s in range(2):
                hist(dve, s)
            for i in range(16):
                dve_split(dve, u0 + i + 2)
                if i < 12:
                    once(dve, "g_evac", i + 1)
                    if i >= 2:
                        once(dve, "g_silu", i - 1)
                    for j in range(4):
                        for k in range(2):
                            r = V_CONV + (gi * 4 + j) * 3 * HG + 2 * i + k
                            src, dst = cbuf[:, i % 2, k, j:j + CW - 3], cacc[:, i % 2, k, 0:CW - 3]
                            if j == 0:
                                last = dve.tensor_scalar(dst, src, vec[:, r:r + 1], None, ALU.mult)
                            else:
                                last = dve.scalar_tensor_tensor(out=dst, in0=src, scalar=vec[:, r:r + 1], in1=dst,
                                                                op0=ALU.mult, op1=ALU.add)
                        if j < 3:
                            step(last)
                    last.then_inc(sem("g_conv"), 1)
                    for k in range(2):
                        dve.tensor_copy(tail[:, 2 * i + k, 0:3], cbuf[:, i % 2, k, SEQ:SEQ + 3])
                        last = dve.tensor_copy(
                            tail[:, 2 * i + k, 3:27].rearrange("p (b t) -> p b t", b=NB),
                            cbuf[:, i % 2, k, 3 + SEQ:CW].rearrange("p (b t) -> p b t", b=NB)[:, :, 4:7])
                    step(last)
                    if i + 2 < 12:
                        hist(dve, i + 2)
                    step(dve.tensor_copy(eps_t[:, 1:2], eps_t[:, 1:2]))
                    dve.tensor_copy(chist[0:1, 0, 0:1], chist[0:1, 0, 0:1]).then_inc(sem("g_tail"), 1)
            for q in range(8):
                once(dve, "g_root", q + 1)
                dve.tensor_tensor(qkv[:, 2 * q:2 * q + 2, :], qkv[:, 2 * q:2 * q + 2, :], fbuf[:, q % 2], ALU.mult
                                  ).then_inc(sem("g_qk_unit"), 1)
            step(dve.scalar_tensor_tensor(out=rows8(T2), in0=rows8(T1), scalar=-1.0, in1=rows8(T1),
                                          op0=ALU.mult, op1=ALU.max))
            dve.tensor_copy(gsm[:, 3:4], gsm[:, 0:1]).then_inc(sem("g_abs"), 1)
            once(dve, "g_lnp", 1)
            once(dve, "g_alog", 1)
            once(dve, "g_eb", 1)
            step(dve.scalar_tensor_tensor(out=rows8(T1), in0=rows8(T1), scalar=0.0, in1=rows8(T3),
                                          op0=ALU.max, op1=ALU.add))
            step(dve.tensor_scalar(rows8(T1), rows8(T1), gsm[:, 2:3], -1.0, ALU.mult, ALU.mult))
            step(dve.tensor_tensor_scan(rows8(GG), gt("keep"), rows8(T1), 0.0, ALU.mult, ALU.add))
            for c in range(2):
                cs = CHUNKS[c]
                dve.tensor_tensor(rows8(ED)[:, cs], rows8(GG)[:, cs.stop - 1:cs.stop].to_broadcast([HG, CH]),
                                  rows8(GG)[:, cs], ALU.subtract)
            g4 = smp(rows8(GG)).rearrange("p (b t) -> p b t", b=NB)
            dve.tensor_tensor(smp(rows8(ED)).rearrange("p (b t) -> p b t", b=NB),
                              g4[:, :, NT - 1:NT].to_broadcast([HG, NB, NT]), g4, ALU.subtract).then_inc(sem("g_gg"), 1)
            step(dve.tensor_scalar(rows8(BETA), rows8(BETA), 1.0, None, ALU.add))
            dve.reciprocal(rows8(BETA), rows8(BETA)).then_inc(sem("g_beta"), 1)
            once(dve, "g_col_turned", 1)
            dve.tensor_scalar(ncol[:, 0:2, :], psum[:, 4, 0:2 * HG].rearrange("p (c h) -> p c h", c=2), -1.0, None, ALU.mult)
            dve.tensor_scalar(ncol[0:NS, 2, :], psum[0:NS, 4, 2 * HG:3 * HG], -1.0, None, ALU.mult).then_inc(sem("g_ncol"), 1)
            id3 = ident[:, None, :].to_broadcast([P, 2, P])
            two = lambda v: v[:, 0:SEQ].rearrange("p (c i) -> p c i", c=2)
            for p in range(GP):
                hh = [2 * p, 2 * p + 1]
                for s in range(2):
                    once(dve, "g_bc", hh[s] + 1)
                    dve.tensor_tensor(PC[:, s], bc[:, s, GG, :], gt("mask"), ALU.add).then_inc(sem("g_tm"), 1)
                    step(dve.tensor_tensor(AO[:, s], bc[:, s, BETA, :], gt("strict"), ALU.mult))
                for s in range(2):
                    once(dve, "g_dt", hh[s] + 1)
                    once(dve, "g_kk", hh[s] + 1)
                    dve.tensor_tensor(AN[:, s], psum[:, 4 * s + 1, 0:T], X[:, s], ALU.mult)
                    step(dve.tensor_tensor(AO[:, s], AO[:, s], X[:, s], ALU.mult))
                    step(dve.tensor_tensor(AT[:, s], psum[:, 4 * s, 0:T], AO[:, s], ALU.mult))
                for l in range(LV):
                    e = lambda s: (p * LV + l) * 2 + s + 1
                    lev = gt(f"level{l}")
                    for s in range(2):
                        if l > 0:
                            once(dve, "g_p_done", e(s) - 2)
                            once(dve, "g_xupd", e(s) - 2)
                        last = dve.tensor_tensor(two(AO[:, s]), two(AT[:, s]), lev[:, None, :].to_broadcast([P, 2, P]), ALU.mult)
                        if l < 2:
                            last = dve.tensor_tensor(AO[0:NS, s, SEQ:T], AT[0:NS, s, SEQ:T], lev[0:NS, 0:NS], ALU.mult)
                        last.then_inc(sem("g_ao"), 1)
                    for s in range(2):
                        if l == 0:
                            once(dve, "g_ao", e(s))
                            dve.tensor_tensor(two(XT[:, s]), id3, two(AO[:, s]), ALU.subtract)
                            dve.tensor_tensor(XT[0:NS, s, SEQ:T], ident[0:NS, 0:NS], AO[0:NS, s, SEQ:T], ALU.subtract)
                            once(dve, "g_p_done", e(s))
                            dve.tensor_tensor(two(X[:, s]), id3, two(psum[:, 4 * s + 2, :]), ALU.subtract)
                            last = dve.tensor_tensor(X[0:NS, s, SEQ:T], ident[0:NS, 0:NS], psum[0:NS, 4 * s + 2, SEQ:T],
                                                     ALU.subtract)
                        else:
                            once(dve, "g_xp_done", (p * (LV - 1) + l - 1) * 2 + s + 1)
                            for dst, b in ((X, 0), (XT, 3)):
                                if b == 0 and l == LV - 1:
                                    continue
                                last = dve.tensor_tensor(dst[:, s, 0:SEQ], dst[:, s, 0:SEQ], psum[:, 4 * s + b, 0:SEQ],
                                                         ALU.subtract)
                                if l < 2:
                                    last = dve.tensor_tensor(dst[0:NS, s, SEQ:T], dst[0:NS, s, SEQ:T],
                                                             psum[0:NS, 4 * s + b, SEQ:T], ALU.subtract)
                        last.then_inc(sem("g_xupd"), 1)
                for s in range(2):
                    h = 2 * p + s
                    once(dve, "g_xupd", (p * LV + LV - 1) * 2 + s + 1)
                    dve.tensor_tensor(PC[:, s], qkv[:, h, :], bc[:, s, EG, :], ALU.mult).then_inc(sem("g_qg"), 1)
                    dve.tensor_tensor(AO[:, s], qkv[:, HG + h, :], bc[:, s, ED, :], ALU.mult).then_inc(sem("g_kdt"), 1)
                for s in range(2):
                    h = 2 * p + s
                    v = qkv[:, 2 * HG + h, :]
                    dve.tensor_tensor(X[:, s, CHUNKS[0]], v[:, CHUNKS[0]], bc[:, s, BETA, CHUNKS[0]], ALU.mult)
                    once(dve, "g_ks", hh[s] + 1)
                    seq3 = lambda t: smp(t).rearrange("p (b t) -> p b t", b=NB)
                    ks4 = psum[:, 4 * s, 0:64].rearrange("p (b a t) -> p b a t", b=NB, a=2)
                    step(dve.tensor_tensor(seq3(X[:, s]), ks4[:, :, 0, :], seq3(bc[:, s, EG, :]), ALU.mult))
                    step(dve.tensor_tensor(smp(X[:, s]), smp(v), smp(X[:, s]), ALU.subtract))
                    dve.tensor_tensor(smp(X[:, s]), smp(X[:, s]), smp(bc[:, s, BETA, :]), ALU.mult).then_inc(sem("g_rt"), 1)
                for s in range(2):
                    once(dve, "g_r_turned", hh[s] + 1)
                    dve.tensor_copy(RS[s][:, 0, :], psum[:, 4 * s + 1, 0:P])
                    dve.tensor_copy(RS[s][0:NS, 2, :], psum[0:NS, 4 * s + 1, P:2 * P]).then_inc(sem("g_r"), 1)
                for s in range(2):
                    h = 2 * p + s
                    once(dve, "g_ks1", hh[s] + 1)
                    c1 = CHUNKS[1]
                    step(dve.tensor_tensor(X[:, s, c1], psum[:, 4 * s, 64:192], bc[:, s, EG, c1], ALU.mult))
                    step(dve.tensor_tensor(X[:, s, c1], qkv[:, 2 * HG + h, c1], X[:, s, c1], ALU.subtract))
                    dve.tensor_tensor(X[:, s, c1], X[:, s, c1], bc[:, s, BETA, c1], ALU.mult).then_inc(sem("g_rt1"), 1)
                for s in range(2):
                    h = 2 * p + s
                    once(dve, "g_o_done", hh[s] + 1)
                    ks4 = psum[:, 4 * s, 0:64].rearrange("p (b a t) -> p b a t", b=NB, a=2)
                    o = qkv[:, h, :]
                    dve.tensor_copy(o[:, 0:SEQ], psum[:, 4 * s + 3, 0:SEQ])
                    step(dve.tensor_copy(smp(o), psum[:, 4 * s + 3, SEQ:T]))
                    dve.tensor_tensor(seq3(o), seq3(o), ks4[:, :, 1, :], ALU.add).then_inc(sem("g_o"), 1)
                    dve.scalar_tensor_tensor(out=Sp[:, s, :], in0=Sp[:, s, :], scalar=bc[:, s, EG, SEQ - 1:SEQ],
                                             in1=psum[:, 4 * s + 1, 384:512], op0=ALU.mult, op1=ALU.add
                                             ).then_inc(sem("g_sp_new"), 1)
                for s in range(2):
                    if s == 1:
                        once(dve, "g_ds_done", hh[0] + 1)
                    dve.tensor_tensor(KDB, KS_[s][0:NS, 2:3, :].to_broadcast([NS, NB, P]),
                                      gt("seqcol")[:, :, None].to_broadcast([NS, NB, P]), ALU.mult).then_inc(sem("g_kdb"), 1)
                for s in range(2):
                    once(dve, "g_ds_done", hh[s] + 1)
                    for b in range(NB):
                        e_ = SEQ + NT * b + NT - 1
                        last = dve.scalar_tensor_tensor(
                            out=Sin[:, s, b, :], in0=Sin[:, s, b, :], scalar=bc[:, s, EG, e_:e_ + 1],
                            in1=psum[:, 4 * s + b // 4, (b % 4) * P:(b % 4 + 1) * P], op0=ALU.mult, op1=ALU.add)
                    last.then_inc(sem("g_s_new"), 1)
                for s in range(2):
                    h = 2 * p + s
                    once(dve, "g_or", hh[s] + 1)
                    step(dve.scalar_tensor_tensor(out=fbuf[:, s, 0, :], in0=qkv[:, h, :],
                                                  scalar=vec[:, V_GN + gi:V_GN + gi + 1], in1=sq[:, 2 + s, :],
                                                  op0=ALU.mult, op1=ALU.mult))
                    dve.tensor_tensor(fbuf[:, s, 1, :], fbuf[:, s, 0, :], gz[:, h, :], ALU.mult).then_inc(sem("g_on"), 1)
                    once(dve, "g_o_hi", hh[s] + 1)
                    dve.tensor_tensor(xn_lo[:, h, :], fbuf[:, s, 1, :], xn_hi[:, h, :].bitcast(F32), ALU.subtract
                                      ).then_inc(sem("g_o_split"), 1)
            for i in range(H):
                dve_split(dve, u0 + 17 + i + 1)
                dve_take_y(dve, n, i, u0 + 17 + i)

        def hist(dve, i):
            for k in range(2):
                last = dve.tensor_copy(cbuf[:, i % 2, k, 3 + SEQ:CW].rearrange("p (b t) -> p b t", b=NB)[:, :, 0:3],
                                       chist[:, 2 * i + k, :].rearrange("p (b t) -> p b t", b=NB))
            if i < 2:
                last.then_inc(sem("g_cbuf_half"), 1)
                if i == 1:
                    once(dve, "g_cbuf_half", 2)
                    dve.memset(cbuf[:, 1, 1, 0:3], 0.0).then_inc(sem("g_cbuf_set"), 1)
        SP["gdn"], PE["gdn"], ACTE["gdn"], DVE["gdn"] = sp_gdn, pe_gdn, act_gdn, dve_gdn

        if any(q[0] == "mlstm" for q in subs):
            w[0] = 0
            LC = 256
            lkq = carve("l_kq", [P, 2 * LH, T])
            lv = carve("l_v", [P, 3, LH * LC])
            lo = carve("l_o", [P, 2 * LH, T])
            ltab = carve("l_tab", [P, TAB["c_mlstm"][0].shape[1]])
            lbc = carve("l_bc", [P, 2, 4, T])
            Cin = carve("l_c", [P, 2, NB, LC])
            Cp = carve("l_cp", [P, 2, LC])
            WS, ST = carve("l_w", [P, 2, 416]), carve("l_st", [P, 2, 416])
            LKD = carve("l_kd", [P, 2, 3, P])
            kdT, den = carve("l_kdt", [P, 2, T]), carve("l_den", [P, 2, T])
            nrow, n0 = carve("l_nrow", [NB * LH, P]), carve("l_n0", [P, NB, LH])
            nall, nout = carve("l_nall", [P, LH + NB * LH]), carve("l_nout", [LH + NB * LH, P])
            qw, qn = carve("l_qw", [P, 2, NS]), carve("l_qn", [P, 2, NS])
            acol = carve("l_acol", [P, 3, LH])
            gb = carve("l_gb", [LH, 2])
            m0, mnew = carve("l_m0", [LH, NB]), carve("l_mnew", [LH, 1 + NB])
            ncar = carve("l_ncar", [P, 2, NB])

        def lt(name):
            o, _, r = table["c_mlstm"][name]
            n_ = table["c_mlstm"][name][1]
            return ltab[0:r, o:o + n_]
        rows4 = lambda r: y[0:LH, r, :]
        LM, LWI, LEM, LWJ, LI, LB, LA, LMT = range(8)
        tmp4 = lambda r: fbuf[0:LH, r // 2, r % 2, :]
        sq3 = lambda v: smp(v).rearrange("p (b t) -> p b t", b=NB)
        LP = LH // 2
        BL = lambda s, b: psum[:, 4 * s + b, :]

        def sp_mlstm(sp, n):
            g, u0 = subs[n][2], ubase[n]
            if n > 0:
                once(sp, "unit_used", u0)
            sp.dma_start(ltab[:], a["c_mlstm"]).then_inc(sem("l_tab_in"), 16)
            sp.dma_start(gb[:, 0:1], a["mlstm_i_bias"][g].rearrange("(h o) -> h o", o=1)).then_inc(sem("l_tab_in"), 16)
            sp.dma_start(gb[:, 1:2], a["mlstm_f_bias"][g].rearrange("(h o) -> h o", o=1)).then_inc(sem("l_tab_in"), 16)
            with nc.allow_non_contiguous_dma(reason="32 stabilisers"):
                sp.dma_start(m0[:], a["state_mlstm_m"][g].rearrange("b h -> h b")).then_inc(sem("l_tab_in"), 16)
            sp.dma_start(nrow[:], a["state_mlstm_n"][g].rearrange("b h d -> (b h) d")).then_inc(sem("l_tab_in"), 16)
            for u in range(u0, u0 + 13):
                sp_unit(sp, u)
            out = 0
            for h in range(LH + 2):
                if h >= 2:
                    once(sp, "l_c_new", h - 1)
                    sp.dma_start(a["ml_C_s"][g, :, h - 2].rearrange("b d e -> d b e"), Cin[:, h % 2]
                                 ).then_inc(sem(f"l_c_out{h % 2}"), 16)
                    sp.dma_start(a["ml_C_p"][g, 0, h - 2], Cp[:, h % 2]).then_inc(sem(f"l_c_out{h % 2}"), 16)
                    once(sp, f"l_c_out{h % 2}", 32 * (h // 2))
                if h < LH:
                    sp.dma_start(Cin[:, h % 2], a["state_mlstm_C"][g, :, h].rearrange("b d e -> d b e")
                                 ).then_inc(sem(f"l_c_in{h % 2}"), 16)
                if h == 1:
                    for u in range(u0 + 13, uend[n]):
                        sp_unit(sp, u)
            once(sp, "l_m_new", 1)
            sp.dma_start(a["ml_m_p"][g, 0].rearrange("(h o) -> h o", o=1), mnew[:, 0:1]).then_inc(sem("l_rows_out"), 16)
            with nc.allow_non_contiguous_dma(reason="32 stabilisers"):
                sp.dma_start(a["ml_m_s"][g].rearrange("b h -> h b"), mnew[:, 1:]).then_inc(sem("l_rows_out"), 16)
            once(sp, "l_n_out", 1)
            sp.dma_start(a["ml_n_p"][g, 0], nout[0:LH, :]).then_inc(sem("l_rows_out"), 16)
            sp.dma_start(a["ml_n_s"][g].rearrange("b h d -> (b h) d"), nout[LH:, :]).then_inc(sem("l_rows_out"), 16)
            once(sp, "l_rows_out", 64)

        def pe_mlstm(pe, n):
            u0 = ubase[n]
            gates = [psum[0:LH, 4, 0:T], psum[0:LH, 5, 0:T]]
            pe.wait_ge(lo_ready, u0 + 1)
            wh, wl = wview(w_hi[u0 % NSPL], u0), wview(w_lo[u0 % NSPL], u0)
            ready = x_chunks(pe, n)
            for m in range(2):
                for k in range(KC):
                    if m == 0:
                        ready(k)
                    c = slice(m * LH, (m + 1) * LH)
                    pe.matmul(gates[m], wh[:, k, c], xn_hi[:, k, :], start=k == 0, stop=False)
                    pe.matmul(gates[m], wh[:, k, c], xn_lo[:, k, :], start=False, stop=False)
                    last = pe.matmul(gates[m], wl[:, k, c], xn_hi[:, k, :], start=False, stop=k == KC - 1)
            last.then_inc(unit_used, 1)
            once(pe, "l_tab_in", 80)
            pe.transpose(psum[:, 6, 0:NB * LH], nrow[:], ident[0:NB * LH, 0:NB * LH]).then_inc(sem("l_n_turned"), 1)
            for i in range(12):
                if i >= 2:
                    once(pe, "l_evac", i - 1)
                u, b = u0 + 1 + i, 2 * (i % 2)
                if not 4 <= i < 8:
                    pe_unit(pe, u, [psum[:, b, 0:T], psum[:, b + 1, 0:T]], xn(xn_hi), xn(xn_lo), True, True)
                    continue
                pe.wait_ge(lo_ready, u + 1)
                wh, wl = wview(w_hi[u % NSPL], u), wview(w_lo[u % NSPL], u)
                for t, (cols, _, _) in enumerate(token_tiles):
                    out = psum[0:cols.stop - cols.start, b + t // 2, (t % 2) * LC:(t % 2 + 1) * LC]
                    for k in range(KC):
                        pe.matmul(out, xn_hi[:, k, cols], wh[:, k, :], start=k == 0, stop=False)
                        pe.matmul(out, xn_hi[:, k, cols], wl[:, k, :], start=False, stop=False)
                        last = pe.matmul(out, xn_lo[:, k, cols], wh[:, k, :], start=False, stop=k == KC - 1)
                last.then_inc(unit_used, 1)
            once(pe, "l_rows", 1)
            for t, (cols, _, _) in enumerate(token_tiles):
                last = pe.transpose(psum[0:cols.stop - cols.start, 6, 64 + t * LH:64 + (t + 1) * LH],
                                    rows4(LA)[:, cols], ident[0:LH, 0:LH])
            last.then_inc(sem("l_col_turned"), 1)
            once(pe, "l_evac", 12)
            once(pe, "l_acol", 1)
            flat = lkq[:].rearrange("p k t -> p (k t)")
            for p in range(LP):
                for s in range(2):
                    h = 2 * p + s
                    if p > 0:
                        once(pe, "l_c_new", h - 1)
                    for r in range(4):
                        last = pe.matmul(BL(s, r)[:, 0:T], lt("select")[0:LH, h * P:(h + 1) * P], rows4(r),
                                         start=True, stop=True)
                    last.then_inc(sem("l_bc_done"), 1)
                for s in range(2):
                    h = 2 * p + s
                    once(pe, "l_bc", h + 1)
                    k0, q0 = h * T, (LH + h) * T
                    pe.matmul(BL(s, 0)[:, 0:SEQ], flat[:, k0:k0 + P], flat[:, q0:q0 + SEQ], start=True, stop=True)
                    pe.matmul(BL(s, 0)[:, SEQ:384], flat[:, k0 + P:k0 + SEQ], flat[:, q0 + P:q0 + SEQ], start=True,
                              stop=True)
                    pe.matmul(BL(s, 0)[:, 384:416], flat[:, k0 + SEQ:k0 + SEQ + P], flat[:, q0 + SEQ:q0 + T],
                              start=True, stop=True).then_inc(sem("l_kk"), 1)
                for s in range(2):
                    h = 2 * p + s
                    once(pe, "l_st", h + 1)
                    once(pe, "l_qn", h + 1)
                    once(pe, f"l_c_in{s}", 16 * (p + 1))
                    for e in range(3):
                        val = lambda t: lv[:, t, h * LC + e * P:h * LC + (e + 1) * P] if e < 2 else ones
                        out = BL(s, 1 + e)
                        pe.matmul(out[:, SEQ:T], val(2)[0:NS], ST[0:NS, s, 384:416], start=True, stop=False)
                        if e < 2:
                            for b in range(NB):
                                cs = slice(SEQ + NT * b, SEQ + NT * (b + 1))
                                pe.matmul(out[:, cs], Cin[:, s, b, e * P:(e + 1) * P], qw[:, s, NT * b:NT * (b + 1)],
                                          start=False, stop=b == NB - 1)
                        else:
                            pe.matmul(out[:, SEQ:T], ones, qn[:, s, :], start=False, stop=True)
                        pe.matmul(out[:, 0:SEQ], val(0), ST[:, s, 0:SEQ], start=True, stop=False)
                        last = pe.matmul(out[:, P:SEQ], val(1), ST[:, s, SEQ:384], start=False, stop=True)
                    last.then_inc(sem("l_num"), 1)
                for s in range(2):
                    h = 2 * p + s
                    once(pe, "l_kdt", h + 1)
                    for t, (cols, _, _) in enumerate(token_tiles):
                        last = pe.transpose(BL(s, 0)[0:cols.stop - cols.start, t * P:(t + 1) * P], kdT[:, s, cols], ident)
                    last.then_inc(sem("l_kd_turned"), 1)
                for s in range(2):
                    h = 2 * p + s
                    once(pe, "l_kd", h + 1)
                    for t in range(2):
                        last = pe.matmul(BL(s, 0)[:, 0:LC], LKD[:, s, t, :], lv[:, t, h * LC:(h + 1) * LC],
                                         start=t == 0, stop=t == 1)
                    last.then_inc(sem("l_cp_done"), 1)
                for s in range(2):
                    h = 2 * p + s
                    once(pe, "l_kdb", h + 1)
                    once(pe, "l_cp", h + 1)
                    once(pe, "l_h", h + 1)
                    for b in range(NB):
                        last = pe.matmul(BL(s, b // 2)[:, (b % 2) * LC:(b % 2 + 1) * LC], KDB[:, b, :],
                                         lv[0:NS, 2, h * LC:(h + 1) * LC], start=True, stop=True)
                    last.then_inc(sem("l_dc_done"), 1)
            once(pe, "l_nall", LH)
            once(pe, "l_c_new", LH)
            pe.transpose(psum[0:LH + NB * LH, 7, 0:P], nall[:], ident).then_inc(sem("l_n_turned"), 1)
            once(pe, "l_o_split", LH)
            once(pe, "l_n_out", 1)
            pe_out(pe, n, u0 + 13, xn(xn_hi), xn(xn_lo), None)

        def act_mlstm(act, n):
            u0 = ubase[n]
            seq = sem("l_act_seq")
            act_split(act, u0 + 1)
            for i in range(12):
                act_split(act, u0 + i + 2)
                act.wait_ge(unit_used, u0 + i + 2)
                b = 2 * (i % 2)
                if i < 2:
                    act.activation(lkq[:, LH + 2 * i:LH + 2 * i + 2, :], psum[:, b:b + 2, 0:T], ACT.Copy,
                                   scale=P ** -0.5).then_inc(sem("l_evac"), 1)
                elif i < 4:
                    act.activation(lkq[:, 2 * i - 4:2 * i - 2, :], psum[:, b:b + 2, 0:T], ACT.Copy).then_inc(sem("l_evac"), 1)
                elif i < 8:
                    c = slice((i - 4) * LC, (i - 3) * LC)
                    act.activation(lv[:, 0:2, c], psum[:, b, :].rearrange("p (t e) -> p t e", t=2), ACT.Copy)
                    act.activation(lv[0:NS, 2, c], psum[0:NS, b + 1, 0:LC], ACT.Copy).then_inc(sem("l_evac"), 1)
                else:
                    act.activation(lo[:, 2 * i - 16:2 * i - 14, :], psum[:, b:b + 2, 0:T], ACT.Exp,
                                   scale=-1.0).then_inc(sem("l_evac"), 1)
                if i == 1:
                    once(act, "l_abs", 1)
                    act.activation(tmp4(1), tmp4(1), ACT.Exp, scale=-1.0).then_inc(seq, 1)
                    act.wait_ge(seq, before("l_act_seq") + 1)
                    act.activation(tmp4(2), tmp4(1), ACT.Ln, bias=ones[0:LH, 0:1]).then_inc(sem("l_lnp"), 1)
            once(act, "l_pre_rows", 1)
            act.activation(rows4(LWI), rows4(LWI), ACT.Exp)
            act.activation(rows4(LEM), rows4(LMT), ACT.Exp, scale=-1.0)
            act.activation(rows4(LWJ), rows4(LWJ), ACT.Exp).then_inc(sem("l_rows"), 1)
            for p in range(LP):
                for s in range(2):
                    h = 2 * p + s
                    once(act, "l_bc_done", h + 1)
                    act.activation(lbc[:, s], psum[:, 4 * s:4 * s + 4, 0:T], ACT.Copy).then_inc(sem("l_bc"), 1)
                for s in range(2):
                    h = 2 * p + s
                    once(act, "l_tm", h + 1)
                    for t, cs in enumerate((slice(0, SEQ), slice(SEQ, 384), slice(384, 416))):
                        last = act.activation(WS[:, s, cs], WS[:, s, cs], ACT.Exp, bias=acol[:, t, h:h + 1])
                    last.then_inc(sem("l_w_ready"), 1)
                for s in range(2):
                    h = 2 * p + s
                    once(act, "l_num", h + 1)
                    act.activation(den[:, s, :], BL(s, 3)[:, 0:T], ACT.Abs).then_inc(sem("l_den"), 1)
                for s in range(2):
                    h = 2 * p + s
                    once(act, "l_kd_turned", h + 1)
                    act.activation(LKD[:, s, 0:2, :], BL(s, 0)[:, 0:SEQ].rearrange("p (c e) -> p c e", c=2), ACT.Copy)
                    act.activation(LKD[0:NS, s, 2, :], BL(s, 0)[0:NS, SEQ:SEQ + P], ACT.Copy).then_inc(sem("l_kd"), 1)
                for s in range(2):
                    h = 2 * p + s
                    once(act, "l_cp_done", h + 1)
                    act.activation(Cp[:, s, :], BL(s, 0)[:, 0:LC], ACT.Copy).then_inc(sem("l_cp"), 1)
                for s in range(2):
                    h = 2 * p + s
                    once(act, "l_h", h + 1)
                    act.activation(xn_hi[:, 2 * h:2 * h + 2, :], fbuf[:, s], ACT.Copy).then_inc(sem("l_o_hi"), 1)
            once(act, "l_n_turned", 2)
            act.activation(nout[:], psum[0:LH + NB * LH, 7, 0:P], ACT.Copy).then_inc(sem("l_n_out"), 1)
            for i in range(H):
                act_split(act, u0 + 13 + i + 1)
                act_square_y(act, n, i)

        def dve_mlstm(dve, n):
            u0 = ubase[n]
            seq, cnt = sem("l_dve_seq"), [0]

            def step(ins):
                cnt[0] += 1
                ins.then_inc(seq, 1)
                dve.wait_ge(seq, before("l_dve_seq") + cnt[0])
            dve_split(dve, u0 + 1)
            if n > 0:
                dve.wait_ge(unit_used, u0)
            dve.memset(acol[:], 0.0)
            once(dve, "xlo_ready", H * (n + 1))
            dve.wait_ge(unit_used, u0 + 1)
            once(dve, "l_tab_in", 80)
            dve.tensor_scalar(rows4(LI), psum[0:LH, 4, 0:T], gb[:, 0:1], None, ALU.add)
            step(dve.tensor_scalar(tmp4(0), psum[0:LH, 5, 0:T], gb[:, 1:2], None, ALU.add))
            dve.scalar_tensor_tensor(out=tmp4(1), in0=tmp4(0), scalar=-1.0, in1=tmp4(0), op0=ALU.mult,
                                     op1=ALU.max).then_inc(sem("l_abs"), 1)
            once(dve, "l_n_turned", 1)
            step(dve.tensor_copy(n0[:].rearrange("p b h -> p (b h)"), psum[:, 6, 0:NB * LH]))
            for i in range(12):
                dve_split(dve, u0 + i + 2)
                if i == 1:
                    once(dve, "l_lnp", 1)
                    step(dve.scalar_tensor_tensor(out=tmp4(3), in0=tmp4(0), scalar=0.0, in1=tmp4(2), op0=ALU.min,
                                                  op1=ALU.subtract))
                    step(dve.tensor_tensor_scan(rows4(LB), lt("keep")[0:LH], tmp4(3), 0.0, ALU.mult, ALU.add))
                    step(dve.tensor_tensor(rows4(LA), rows4(LI), rows4(LB), ALU.subtract))
                    step(dve.tensor_copy(tmp4(3), rows4(LA)))
                    dve.tensor_scalar(tmp4(3)[:, 0:1], tmp4(3)[:, 0:1], 0.0, None, ALU.max)
                    step(dve.tensor_tensor(sq3(tmp4(3))[:, :, 0], sq3(tmp4(3))[:, :, 0], m0[:], ALU.max))
                    step(dve.tensor_tensor_scan(rows4(LM), lt("drop")[0:LH], tmp4(3), 0.0, ALU.add, ALU.max))
                    step(dve.tensor_tensor(rows4(LMT), rows4(LB), rows4(LM), ALU.add))
                    dve.tensor_copy(mnew[:, 0:1], rows4(LMT)[:, SEQ - 1:SEQ])
                    dve.tensor_copy(mnew[:, 1:], sq3(rows4(LMT))[:, :, NT - 1]).then_inc(sem("l_m_new"), 1)
                    dve.tensor_scalar(rows4(LWI)[:, 0:SEQ], rows4(LM)[:, 0:SEQ], -1.0, None, ALU.mult)
                    dve.tensor_tensor(sq3(rows4(LWI)), m0[:, :, None].to_broadcast([LH, NB, NT]), sq3(rows4(LM)), ALU.subtract)
                    dve.tensor_tensor(rows4(LWJ)[:, 0:SEQ], rows4(LA)[:, 0:SEQ],
                                      rows4(LM)[:, SEQ - 1:SEQ].to_broadcast([LH, SEQ]), ALU.subtract)
                    dve.tensor_tensor(sq3(rows4(LWJ)), sq3(rows4(LA)),
                                      sq3(rows4(LM))[:, :, NT - 1:NT].to_broadcast([LH, NB, NT]), ALU.subtract
                                      ).then_inc(sem("l_pre_rows"), 1)
                if i >= 9:
                    gate(dve, i - 9)
            gate(dve, 3)
            once(dve, "l_col_turned", 1)
            dve.tensor_copy(acol[:, 0:2, :], psum[:, 6, 64:64 + 2 * LH].rearrange("p (c h) -> p c h", c=2))
            dve.tensor_copy(acol[0:NS, 2, :], psum[0:NS, 6, 64 + 2 * LH:64 + 3 * LH]).then_inc(sem("l_acol"), 1)
            for p in range(LP):
                for s in range(2):
                    h = 2 * p + s
                    once(dve, "l_bc", h + 1)
                    if p > 0:
                        once(dve, "l_st", h - 1)
                    dve.tensor_tensor(WS[:, s, 0:SEQ], lt("mask")[:, 0:SEQ], lbc[:, s, LM, 0:SEQ], ALU.subtract)
                    dve.tensor_tensor(WS[:, s, SEQ:416], lt("mask")[:, SEQ:416], lbc[:, s, LM, P:T], ALU.subtract
                                      ).then_inc(sem("l_tm"), 1)
                    step(dve.tensor_tensor(qw[:, s, :], smp(lkq[:, LH + h, :]), smp(lbc[:, s, LWI, :]), ALU.mult))
                    qn3 = lambda v: v.rearrange("p (b t) -> p b t", b=NB)
                    dve.tensor_tensor(qn3(qn[:, s, :]), qn3(qw[:, s, :]), n0[:, :, h:h + 1].to_broadcast([P, NB, NT]),
                                      ALU.mult).then_inc(sem("l_qn"), 1)
                for s in range(2):
                    h = 2 * p + s
                    once(dve, "l_w_ready", h + 1)
                    once(dve, "l_kk", h + 1)
                    dve.tensor_tensor(ST[:, s, :], BL(s, 0)[:, 0:416], WS[:, s, :], ALU.mult).then_inc(sem("l_st"), 1)
                    dve.tensor_tensor(kdT[:, s, :], lkq[:, h, :], lbc[:, s, LWJ, :], ALU.mult).then_inc(sem("l_kdt"), 1)
                for s in range(2):
                    h = 2 * p + s
                    once(dve, "l_kdt", h + 1)
                    dve.tensor_reduce(nall[:, h:h + 1], kdT[:, s, 0:SEQ], AX.X, ALU.add)
                    step(dve.tensor_reduce(ncar[:, 0, :], sq3(kdT[:, s, :]), AX.X, ALU.add))
                    step(dve.tensor_tensor(ncar[:, 1, :], n0[:, :, h], sq3(lbc[:, s, LWI, :])[:, :, NT - 1], ALU.mult))
                    dve.tensor_tensor(nall[:, LH:].rearrange("p (b h) -> p b h", b=NB)[:, :, h], ncar[:, 0, :],
                                      ncar[:, 1, :], ALU.add).then_inc(sem("l_nall"), 1)
                    once(dve, "l_nall", h + 1)
                for s in range(2):
                    h = 2 * p + s
                    once(dve, "l_den", h + 1)
                    step(dve.tensor_tensor(den[:, s, :], den[:, s, :], lbc[:, s, LEM, :], ALU.max))
                    step(dve.reciprocal(den[:, s, :], den[:, s, :]))
                    if p > 0:
                        once(dve, "l_o_split", h - 1)
                    for e in range(2):
                        last = dve.tensor_tensor(fbuf[:, s, e, :], BL(s, 1 + e)[:, 0:T], den[:, s, :], ALU.mult)
                    step(last)
                    dve.tensor_tensor(fbuf[:, s], fbuf[:, s], lo[:, 2 * h:2 * h + 2, :], ALU.mult).then_inc(sem("l_h"), 1)
                for s in range(2):
                    h = 2 * p + s
                    once(dve, "l_kd", h + 1)
                    if h > 0:
                        once(dve, "l_dc_done", h)
                    dve.tensor_tensor(KDB, LKD[0:NS, s, 2:3, :].to_broadcast([NS, NB, P]),
                                      lt("seqcol")[:, :, None].to_broadcast([NS, NB, P]), ALU.mult).then_inc(sem("l_kdb"), 1)
                for s in range(2):
                    h = 2 * p + s
                    once(dve, "l_dc_done", h + 1)
                    once(dve, "l_cp", h + 1)
                    for b in range(NB):
                        e_ = SEQ + NT * b + NT - 1
                        last = dve.scalar_tensor_tensor(
                            out=Cin[:, s, b, :], in0=Cin[:, s, b, :], scalar=lbc[:, s, LWI, e_:e_ + 1],
                            in1=BL(s, b // 2)[:, (b % 2) * LC:(b % 2 + 1) * LC], op0=ALU.mult, op1=ALU.add)
                    last.then_inc(sem("l_c_new"), 1)
                for s in range(2):
                    h = 2 * p + s
                    once(dve, "l_o_hi", h + 1)
                    dve.tensor_tensor(xn_lo[:, 2 * h:2 * h + 2, :], fbuf[:, s],
                                      xn_hi[:, 2 * h:2 * h + 2, :].bitcast(F32), ALU.subtract).then_inc(sem("l_o_split"), 1)
            for i in range(H):
                dve_split(dve, u0 + 13 + i + 1)
                dve_take_y(dve, n, i, u0 + 13 + i)

        def gate(dve, i):
            o2 = lo[:, 2 * i:2 * i + 2, :]
            once(dve, "l_evac", 9 + i)
            dve.tensor_scalar(o2, o2, 1.0, None, ALU.add).then_inc(sem("l_gate_sum"), 1)
            once(dve, "l_gate_sum", i + 1)
            dve.reciprocal(o2, o2)
        SP["mlstm"], PE["mlstm"], ACTE["mlstm"], DVE["mlstm"] = sp_mlstm, pe_mlstm, act_mlstm, dve_mlstm

        if any(q[0] == "mla" for q in subs):
            w[0] = 0
            atab = carve("a_tab", [P, TAB["c_mla"][0].shape[1]])
            wkv = carve("a_wkv", [P, 2, MH * 256])
            ckvT = carve("a_ckvt", [P, 2, T])
            ctok, krtok = carve("a_ctok", [P, 3, KVR]), carve("a_krtok", [P, 3, ROPE])
            QL = carve("a_ql", [P, 2, NB, MH, NT])
            QRS = carve("a_qrs", [ROPE, NB, MH, NT])
            OL = carve("a_ol", [P, 2, NB, MH, NT])
            krT = carve("a_krt", [ROPE, T])
            pages = nc.alloc_sbuf_tensor_at("a_pages", [1, NB * NP], I32, offset=free_at + 4 * w[0])
            w[0] += NB * NP
            stat = carve("a_stat", [P, 2, 8])
            w2 = w[0]
            WkT = carve("a_wkt", [P, MH, KVR])
            qnT = carve("a_qn", [P, MH, T])
            qrT = carve("a_qr", [ROPE, MH, T])
            kT = carve("a_kt", [P, MH, SEQ])
            vP = carve("a_v", [P, 2, MH * P])
            krr = y[0:ROPE, 5:7, :]
            qrr = sq[0:ROPE, 0:4, :].rearrange("p (i j) t -> p i j t", i=2)
            yflat = y[:].rearrange("p k t -> p (k t)")
            pm = yflat[:, 0:768].rearrange("p (s k) -> p s k", s=2)
            pT = yflat[:, 768:1536].rearrange("p (s k) -> p s k", s=2)
            cq_hi = nc.alloc_sbuf_tensor_at("a_cqh", [P, 3, T], F32R, offset=free_at + 4 * w[0])
            w[0] += 3 * T
            cq_lo = nc.alloc_sbuf_tensor_at("a_cql", [P, 3, T], F32R, offset=free_at + 4 * w[0])
            w[0] += 3 * T
            assert w[0] <= mix_words, (w[0], mix_words)
            w[0] = w2
            lat = carve("a_lat", [P, 2, NP, KVR])
            rop = carve("a_rop", [P, 2, NP, ROPE])
            latT = carve("a_latt", [P, 2, 2, 512])
            ropT = carve("a_ropt", [ROPE, 2, 512])
        craw = y[:, 0:5, :]
        sc = [v[0:NS].rearrange("p k t -> p (k t)") for v in (y, sq)]
        spT = fbuf[:].rearrange("p a b t -> p (a b t)")[:, 0:2 * (512 + NS)].rearrange("p (s k) -> p s k", s=2)
        NK = PAST + NS

        def at_(name):
            o, n_, r = table["c_mla"][name]
            return atab[0:r, o:o + n_]
        bt = lambda v: v.rearrange("p (b t) -> p b t", b=NB)

        def sp_mla(sp, n):
            g, u0 = subs[n][2], ubase[n]
            if n > 0:
                once(sp, "unit_used", u0)
            sp.dma_start(atab[:], a["c_mla"]).then_inc(sem("a_tab_in"), 16)
            sp.dma_start(wkv[:], a["mla_w_ukv"][g].rearrange("(k p) n -> p k n", p=P)).then_inc(sem("a_tab_in"), 16)
            sp.dma_start(pages[:], a["page_table"].rearrange("(o b) n -> o (b n)", o=1)).then_inc(sem("a_pages_in"), 16)
            for u in range(u0, u0 + 7 + NRAW):
                sp_unit(sp, u)
            once(sp, "a_tok", 1)
            for t in range(2):
                sp.dma_start(a["mla_lat_p"][g, t], ctok[:, t, :]).then_inc(sem("a_tok_out"), 16)
                sp.dma_start(a["mla_rope_p"][g, t], krtok[:, t, :]).then_inc(sem("a_tok_out"), 16)
            sp.dma_start(a["mla_lat_s"][g].rearrange("b t r -> (b t) r"), ctok[0:NS, 2, :]).then_inc(sem("a_tok_out"), 16)
            sp.dma_start(a["mla_rope_s"][g].rearrange("b t r -> (b t) r"), krtok[0:NS, 2, :]).then_inc(sem("a_tok_out"), 16)
            once(sp, "a_pages_in", 16)
            once(sp, "a_pv_done", MH)
            once(sp, "a_o_split", 1)
            for b in range(NB):
                if b >= 2:
                    once(sp, "a_spv_done", b - 1)
                with sp.Fori(0, NP) as q:
                    page = sp.value_load(pages[0:1, bass.ds(q + b * NP, 1)], min_val=0, max_val=N_PHYS - 1)
                    sp.dma_start(lat[:, b % 2, bass.ds(q, 1), :],
                                 a["cache_mla_latent"][g, bass.ds(page, 1)].rearrange("o p r -> p o r")
                                 ).then_inc(sem(f"a_lat_in{b % 2}"), 16)
                    sp.dma_start(rop[:, b % 2, bass.ds(q, 1), :],
                                 a["cache_mla_rope"][g, bass.ds(page, 1)].rearrange("o p r -> p o r")
                                 ).then_inc(sem(f"a_lat_in{b % 2}"), 16)
            assert u0 + 7 + NRAW == uend[n]
            once(sp, "a_tok_out", 96)

        def pe_mla(pe, n):
            u0 = ubase[n]
            ready = x_chunks(pe, n)
            for i in range(3):
                m2 = P if i < 2 else ROPE
                pe_unit(pe, u0 + i, [psum[:, 2 * i, 0:T], psum[0:m2, 2 * i + 1, 0:T]], xn(xn_hi), xn(xn_lo),
                        True, True, ready=ready if i == 0 else None)
            once(pe, "a_tab_in", 32)
            for q in range(4):
                if q >= 2:
                    once(pe, "a_wkt", q - 1)
                for j in range(4):
                    h, rc = 2 * q + j // 2, j % 2
                    last = pe.transpose(psum[:, 6 + q % 2, j * P:(j + 1) * P], wkv[:, rc, h * 256:h * 256 + P], ident)
                last.then_inc(sem("a_wk_turned"), 1)
            once(pe, "a_csq", 2)
            once(pe, "a_craw", 3)
            for k in range(5):
                last = pe.matmul(psum[:, k // 3, 0:T], ones, sq[:, k, :], start=k in (0, 3), stop=k in (2, 4))
            last.then_inc(sem("a_css"), 1)
            pe.matmul(psum[0:ROPE, 2, 0:T], at_("rot"), krr[:, 0, :], start=True, stop=True).then_inc(sem("a_krot"), 1)
            once(pe, "a_cq_split", 1)
            once(pe, "a_kr", 1)
            for i in range(4):
                b = 4 * (i % 2)
                u = u0 + 3 + i
                if i >= 2:
                    once(pe, "a_q", i - 1)
                elif i == 1:
                    once(pe, "a_wkt", 4)
                pe.wait_ge(lo_ready, u + 1)
                wh, wl = wview(w_hi[u % NSPL], u), wview(w_lo[u % NSPL], u)
                for j, (c0, m) in enumerate(((0, P), (P, ROPE), (192, P), (192 + P, ROPE))):
                    out = psum[0:m, b + j, 0:T]
                    for k in range(3):
                        c = slice(c0, c0 + m)
                        pe.matmul(out, wh[:, k, c], cq_hi[:, k, :], start=k == 0, stop=False)
                        pe.matmul(out, wh[:, k, c], cq_lo[:, k, :], start=False, stop=False)
                        last = pe.matmul(out, wl[:, k, c], cq_hi[:, k, :], start=False, stop=k == 2)
                last.then_inc(unit_used, 1)
                once(pe, "a_q_evac", i + 1)
                for j in range(2):
                    last = pe.matmul(psum[0:ROPE, b + 2 * j, 0:T], at_("rot"), qrr[:, i % 2, j, :], start=True, stop=True)
                last.then_inc(sem("a_qrot"), 1)
            once(pe, "a_q", 4)
            once(pe, "a_ckv", 1)
            for q in range(4):
                for j in range(2):
                    for k in range(2):
                        h = 2 * q + j
                        last = pe.matmul(psum[:, q, j * SEQ:(j + 1) * SEQ], wkv[:, k, h * 256:h * 256 + P],
                                         ckvT[:, k, 0:SEQ], start=k == 0, stop=k == 1)
                last.then_inc(sem("a_k_done"), 1)
            v4 = wkv[:].rearrange("p k (h c e) -> p k h c e", h=MH, c=2)
            for q in range(4):
                for k in range(2):
                    last = pe.matmul(psum[:, 4 + q, :], ckvT[:, k, (q // 2) * P:(q // 2 + 1) * P],
                                     v4[:, k, 4 * (q % 2):4 * (q % 2) + 4, 1, :], start=k == 0, stop=k == 1)
                last.then_inc(sem("a_v_done"), 1)
            once(pe, "a_k", 2)
            for rc in range(2):
                for h in range(MH):
                    last = pe.matmul(psum[:, rc, h * NS:(h + 1) * NS], WkT[:, h, rc * P:(rc + 1) * P],
                                     smp(qnT[:, h, :]), start=True, stop=True)
            last.then_inc(sem("a_ql_done"), 1)
            once(pe, "a_k", 4)
            for t, (cols, _, _) in enumerate(token_tiles):
                m = cols.stop - cols.start
                for k in range(2):
                    pe.transpose(psum[0:m, 2 + k, t * P:(t + 1) * P], ckvT[:, k, cols], ident)
            once(pe, "a_v", 1)
            for t, (cols, _, _) in enumerate(token_tiles):
                last = pe.transpose(psum[0:cols.stop - cols.start, 4, t * ROPE:(t + 1) * ROPE], krT[:, cols],
                                    ident[0:ROPE, 0:ROPE])
            last.then_inc(sem("a_tok_turned"), 1)
            once(pe, "a_v", 4)
            once(pe, "a_tok", 1)
            once(pe, "a_ql", 1)

            def scores(h):
                bank = psum[:, 4 * (h % 2), :]
                if h >= 2:
                    once(pe, "a_pm", h - 1)
                for i in range(2):
                    out = bank[:, i * P:i * P + (i + 1) * P]
                    qs = slice(i * P, (i + 1) * P)
                    pe.matmul(out, qnT[:, h, qs], kT[:, h, 0:(i + 1) * P], start=True, stop=False)
                    last = pe.matmul(out, qrT[:, h, qs], krT[:, 0:(i + 1) * P], start=False, stop=True)
                last.then_inc(sem("a_sc_done"), 1)

            def attend(h):
                s = h % 2
                once(pe, "a_pn", h + 1)
                if h >= 2:
                    once(pe, "a_o_pair", h // 2)
                for j in range(3):
                    last = pe.transpose(psum[:, 4 * s + 1, j * P:(j + 1) * P], pm[:, s, j * P:(j + 1) * P], ident)
                last.then_inc(sem("a_p_turned"), 1)
                once(pe, "a_pt", h + 1)
                out = psum[:, 4 * s + 2, :]
                vh = slice(h * P, (h + 1) * P)
                pe.matmul(out[:, 0:P], vP[:, 0, vh], pT[:, s, 0:P], start=True, stop=True)
                pe.matmul(out[:, P:SEQ], vP[:, 0, vh], pT[:, s, P:SEQ], start=True, stop=False)
                pe.matmul(out[:, P:SEQ], vP[:, 1, vh], pT[:, s, SEQ:384], start=False,
                          stop=True).then_inc(sem("a_pv_done"), 1)
            scores(0)
            for h in range(MH):
                if h + 1 < MH:
                    scores(h + 1)
                attend(h)
            once(pe, "a_o_pair", MH // 2)
            for b in range(NB):
                s = b % 2
                once(pe, f"a_lat_in{s}", 16 * 2 * NP * (b // 2 + 1))
                for q in range(NP // 4):
                    e = 4 * b + q
                    bk = 3 * (e % 2)
                    if e >= 2:
                        once(pe, "a_latt", e - 1)
                    for j in range(4):
                        for rc in range(2):
                            pe.transpose(psum[:, bk + rc, j * P:(j + 1) * P], lat[:, s, 4 * q + j, rc * P:(rc + 1) * P], ident)
                        last = pe.transpose(psum[0:ROPE, bk + 2, j * P:(j + 1) * P], rop[:, s, 4 * q + j, :], ident)
                    last.then_inc(sem("a_lat_turned"), 1)
                    if q > 0:
                        sample_scores(pe, b, q - 1)
                sample_scores(pe, b, NP // 4 - 1)
                once(pe, "a_ssc", 5 * b + 4)
                for rc in range(2):
                    pe.matmul(psum[0:NS, 6, 0:NS], QL[:, rc, b].rearrange("p h t -> p (h t)"), smp(ckvT[:, rc, :]),
                              start=rc == 0, stop=False)
                pe.matmul(psum[0:NS, 6, 0:NS], QRS[:, b].rearrange("p h t -> p (h t)"), smp(krT[:]), start=False,
                          stop=True).then_inc(sem("a_ssc_done"), 1)
                if b > 0:
                    sample_attend(pe, b - 1)
            sample_attend(pe, NB - 1)
            once(pe, "a_sol", NB)
            for h in range(MH):
                for rc in range(2):
                    last = pe.matmul(psum[:, 0, h * NS:(h + 1) * NS].rearrange("p (b t) -> p b t", b=NB),
                                     wkv[:, rc, h * 256 + P:(h + 1) * 256], OL[:, rc, :, h, :], start=rc == 0, stop=rc == 1)
            last.then_inc(sem("a_so_done"), 1)
            once(pe, "a_o_split", 2)
            pe_out(pe, n, u0 + 7, xn(xn_hi), xn(xn_lo), None)

        def sample_scores(pe, b, q):
            e = 4 * b + q
            once(pe, "a_latt", e + 1)
            if e > 0:
                once(pe, "a_ssc", 5 * b + q)
            if b > 0 and q == 0 and b > 1:
                once(pe, "a_spt", b - 1)
            for rc in range(2):
                pe.matmul(psum[0:NS, 6, :], QL[:, rc, b].rearrange("p h t -> p (h t)"), latT[:, e % 2, rc, :],
                          start=rc == 0, stop=False)
            pe.matmul(psum[0:NS, 6, :], QRS[:, b].rearrange("p h t -> p (h t)"), ropT[:, e % 2, :], start=False,
                      stop=True).then_inc(sem("a_ssc_done"), 1)

        def sample_attend(pe, b):
            s = b % 2
            once(pe, "a_spn", b + 1)
            if b > 0:
                once(pe, "a_sol", b)
            once(pe, "a_ssc", 5 * (b + 1) if b == NB - 1 else 5 * (b + 2))
            for j in range(NP):
                pe.transpose(psum[:, 7, j * NS:(j + 1) * NS], sc[s][:, j * P:(j + 1) * P], ident[0:NS, 0:NS])
            pe.transpose(psum[0:NS, 6, 0:NS], sc[s][:, PAST:NK], ident[0:NS, 0:NS]).then_inc(sem("a_sp_turned"), 1)
            once(pe, "a_spt", b + 1)
            for rc in range(2):
                out = psum[:, 7, rc * NS:(rc + 1) * NS]
                for j in range(NP):
                    pe.matmul(out, lat[:, s, j, rc * P:(rc + 1) * P], spT[:, s, j * NS:(j + 1) * NS], start=j == 0,
                              stop=False)
                last = pe.matmul(out, ctok[0:NS, 2, rc * P:(rc + 1) * P], spT[0:NS, s, 512:512 + NS], start=False,
                                 stop=True)
            last.then_inc(sem("a_spv_done"), 1)

        def act_mla(act, n):
            u0 = ubase[n]
            seq, cnt = sem("a_act_seq"), [0]

            def step(ins):
                cnt[0] += 1
                ins.then_inc(seq, 1)
                act.wait_ge(seq, before("a_act_seq") + cnt[0])
            for i in range(3):
                act_split(act, u0 + i + 1)
                act.wait_ge(unit_used, u0 + i + 1)
                if i < 2:
                    act.activation(craw[:, 2 * i:2 * i + 2, :], psum[:, 2 * i:2 * i + 2, 0:T], ACT.Copy
                                   ).then_inc(sem("a_craw"), 1)
                else:
                    act.activation(craw[:, 4, :], psum[:, 4, 0:T], ACT.Copy)
                    act.activation(krr[:, 0, :], psum[0:ROPE, 5, 0:T], ACT.Copy).then_inc(sem("a_craw"), 1)
            once(act, "a_craw", 3)
            act.activation(sq[:, 0:3, :], craw[:, 0:3, :], ACT.Square).then_inc(sem("a_csq"), 1)
            act.activation(sq[:, 3:5, :], craw[:, 3:5, :], ACT.Square).then_inc(sem("a_csq"), 1)
            once(act, "a_css", 1)
            act.activation(sq[:, 5, :], psum[:, 0, 0:T], ACT.Ln, scale=1.0 / QR, bias=eps_t[:, 0:1])
            step(act.activation(sq[:, 6, :], psum[:, 1, 0:T], ACT.Ln, scale=1.0 / KVR, bias=eps_t[:, 0:1]))
            act.activation(sq[:, 5:7, :], sq[:, 5:7, :], ACT.Exp, scale=-0.5).then_inc(sem("a_croot"), 1)
            once(act, "a_cqn", 1)
            act.activation(cq_hi[:], craw[:, 0:3, :], ACT.Copy).then_inc(sem("a_cq_hi"), 1)
            for i in range(4):
                act_split(act, u0 + 3 + i + 1)
                act.wait_ge(unit_used, u0 + 3 + i + 1)
                b = 4 * (i % 2)
                if i >= 2:
                    once(act, "a_q", i - 1)
                for j in range(2):
                    act.activation(qnT[:, 2 * i + j, :], psum[:, b + 2 * j, 0:T], ACT.Copy)
                    last = act.activation(qrr[:, i % 2, j, :], psum[0:ROPE, b + 2 * j + 1, 0:T], ACT.Copy)
                last.then_inc(sem("a_q_evac"), 1)
            for q in range(4):
                once(act, "a_v_done", q + 1)
                act.activation(vP[:, q // 2, 512 * (q % 2):512 * (q % 2) + 512], psum[:, 4 + q, :], ACT.Copy
                               ).then_inc(sem("a_v"), 1)
            once(act, "a_ql_done", 1)
            for rc in range(2):
                for h in range(MH):
                    last = act.activation(QL[:, rc, :, h, :], bt(psum[:, rc, h * NS:(h + 1) * NS]), ACT.Copy)
            for h in range(MH):
                last = act.activation(QRS[:, :, h, :], bt(smp(qrT[:, h, :])), ACT.Copy)
            last.then_inc(sem("a_ql"), 1)
            for h in range(MH):
                s = h % 2
                once(act, "a_max", h + 1)
                act.activation(pm[:, s, 0:P], pm[:, s, 0:P], ACT.Exp, scale=SCALE, bias=stat[:, s, 0:1],
                               accum_out=stat[:, s, 2:3])
                act.activation(pm[:, s, P:384], pm[:, s, P:384], ACT.Exp, scale=SCALE, bias=stat[:, s, 1:2],
                               accum_out=stat[:, s, 3:4]).then_inc(sem("a_p"), 1)
                once(act, "a_p_turned", h + 1)
                act.activation(pT[:, s, :], psum[:, 4 * s + 1, 0:384], ACT.Copy).then_inc(sem("a_pt"), 1)
                if s == 1:
                    once(act, "a_o_pair", h // 2 + 1)
                    act.activation(xn_hi[:, h - 1:h + 1, 0:SEQ], fbuf[:, 0, :, 0:SEQ], ACT.Copy).then_inc(sem("a_o_hi"), 1)
            for b in range(NB):
                for q in range(4):
                    e = 4 * b + q
                    once(act, "a_lat_turned", e + 1)
                    if e >= 2:
                        once(act, "a_ssc_done", 5 * ((e - 2) // 4) + (e - 2) % 4 + 1)
                    bk = 3 * (e % 2)
                    act.activation(latT[:, e % 2, 0, :], psum[:, bk, :], ACT.Copy)
                    act.activation(ropT[:, e % 2, :], psum[0:ROPE, bk + 2, :], ACT.Copy).then_inc(sem("a_latt_a"), 1)
                    if q == 1 and b > 0:
                        sample_exp(act, b - 1)
            sample_exp(act, NB - 1)
            once(act, "a_so", 1)
            act.activation(xn_hi[:, :, SEQ:T], fbuf8(), ACT.Copy).then_inc(sem("a_o_hi"), 1)
            for i in range(H):
                act_split(act, u0 + 7 + i + 1)
                act_square_y(act, n, i)

        def fbuf8():
            return fbuf[:].rearrange("p a b t -> p (a b t)")[:, 0:MH * NS].rearrange("p (h q) -> p h q", h=MH)

        def sample_exp(act, b):
            s = b % 2
            once(act, "a_smax", b + 1)
            act.activation(sc[s][:, 0:NK], sc[s][:, 0:NK], ACT.Exp, scale=SCALE, bias=stat[0:NS, s, 4:5],
                           accum_out=stat[0:NS, s, 5:6]).then_inc(sem("a_sp"), 1)

        def dve_mla(dve, n):
            u0 = ubase[n]
            seq, cnt = sem("a_dve_seq"), [0]

            def step(ins):
                cnt[0] += 1
                ins.then_inc(seq, 1)
                dve.wait_ge(seq, before("a_dve_seq") + cnt[0])
            for i in range(3):
                dve_split(dve, u0 + i + 1)
            for q in range(4):
                once(dve, "a_wk_turned", q + 1)
                dve.tensor_copy(WkT[:, 2 * q:2 * q + 2, :].rearrange("p h r -> p (h r)"), psum[:, 6 + q % 2, :]
                                ).then_inc(sem("a_wkt"), 1)
            once(dve, "a_croot", 1)
            for k in range(3):
                last = dve.scalar_tensor_tensor(out=craw[:, k, :], in0=craw[:, k, :], scalar=vec[:, V_QN + k:V_QN + k + 1],
                                                in1=sq[:, 5, :], op0=ALU.mult, op1=ALU.mult)
            last.then_inc(sem("a_cqn"), 1)
            for k in range(2):
                last = dve.scalar_tensor_tensor(out=ckvT[:, k, :], in0=craw[:, 3 + k, :],
                                                scalar=vec[:, V_KVN + k:V_KVN + k + 1], in1=sq[:, 6, :],
                                                op0=ALU.mult, op1=ALU.mult)
            last.then_inc(sem("a_ckv"), 1)
            once(dve, "a_cq_hi", 1)
            dve.tensor_tensor(cq_lo[:], craw[:, 0:3, :], cq_hi[:].bitcast(F32), ALU.subtract).then_inc(sem("a_cq_split"), 1)
            once(dve, "a_krot", 1)
            dve.tensor_tensor(krr[:, 1, :], psum[0:ROPE, 2, 0:T], at_("sin"), ALU.mult)
            step(dve.tensor_tensor(krT[:], krr[:, 0, :], at_("cos"), ALU.mult))
            dve.tensor_tensor(krT[:], krT[:], krr[:, 1, :], ALU.add).then_inc(sem("a_kr"), 1)
            two_ = lambda v: v[:, None, :].to_broadcast([ROPE, 2, T])
            for i in range(4):
                dve_split(dve, u0 + 3 + i + 1)
                once(dve, "a_qrot", i + 1)
                b = 4 * (i % 2)
                r2 = qrT[:, 2 * i:2 * i + 2, :]
                rotated = psum[0:ROPE, b:b + 4:2, 0:T]
                dve.tensor_tensor(qrr[:, i % 2], qrr[:, i % 2], two_(at_("cos")), ALU.mult)
                step(dve.tensor_tensor(r2, rotated, two_(at_("sin")), ALU.mult))
                dve.tensor_tensor(r2, r2, qrr[:, i % 2], ALU.add).then_inc(sem("a_q"), 1)
            for q in range(4):
                once(dve, "a_k_done", q + 1)
                dve.tensor_copy(kT[:, 2 * q:2 * q + 2, :].rearrange("p h t -> p (h t)"), psum[:, q, :]).then_inc(sem("a_k"), 1)
            once(dve, "a_tok_turned", 1)
            for k in range(2):
                rs = slice(k * P, (k + 1) * P)
                dve.tensor_copy(ctok[:, 0:2, rs], psum[:, 2 + k, 0:SEQ].rearrange("p (t r) -> p t r", t=2))
                dve.tensor_copy(ctok[0:NS, 2, rs], psum[0:NS, 2 + k, SEQ:384])
            dve.tensor_copy(krtok[:, 0:2, :], psum[:, 4, 0:2 * ROPE].rearrange("p (t r) -> p t r", t=2))
            dve.tensor_copy(krtok[0:NS, 2, :], psum[0:NS, 4, 2 * ROPE:3 * ROPE]).then_inc(sem("a_tok"), 1)

            def masked(h):
                s = h % 2
                once(dve, "a_sc_done", h + 1)
                if h >= 2:
                    once(dve, "a_p_turned", h - 1)
                dve.tensor_tensor(pm[:, s, :], psum[:, 4 * s, 0:384], at_("causal"), ALU.add).then_inc(sem("a_pm"), 1)
                once(dve, "a_pm", h + 1)
                dve.tensor_reduce(stat[:, s, 6:7], pm[:, s, 0:P], AX.X, ALU.max)
                step(dve.tensor_reduce(stat[:, s, 7:8], pm[:, s, P:384], AX.X, ALU.max))
                dve.tensor_scalar(stat[:, s, 0:2], stat[:, s, 6:8], -SCALE, None, ALU.mult).then_inc(sem("a_max"), 1)

            def head_out(h):
                s = h % 2
                once(dve, "a_pv_done", h + 1)
                if s == 0 and h >= 2:
                    once(dve, "a_o_low", h // 2)
                last = dve.tensor_copy(fbuf[:, 0, s, 0:SEQ], psum[:, 4 * s + 2, 0:SEQ])
                if s == 1:
                    last.then_inc(sem("a_o_pair"), 1)
                    once(dve, "a_o_hi", h // 2 + 1)
                    dve.tensor_tensor(xn_lo[:, h - 1:h + 1, 0:SEQ], fbuf[:, 0, :, 0:SEQ],
                                      xn_hi[:, h - 1:h + 1, 0:SEQ].bitcast(F32), ALU.subtract).then_inc(sem("a_o_low"), 1)
            masked(0)
            for h in range(MH):
                s = h % 2
                once(dve, "a_p", h + 1)
                step(dve.reciprocal(stat[:, s, 2:4], stat[:, s, 2:4]))
                dve.tensor_scalar(pm[:, s, 0:P], pm[:, s, 0:P], stat[:, s, 2:3], None, ALU.mult)
                dve.tensor_scalar(pm[:, s, P:384], pm[:, s, P:384], stat[:, s, 3:4], None, ALU.mult).then_inc(sem("a_pn"), 1)
                if h + 1 < MH:
                    masked(h + 1)
                head_out(h)
            dve.tensor_copy(stat[:, 0, 6:7], stat[:, 0, 7:8]).then_inc(sem("a_o_split"), 1)

            def sample_softmax(b):
                s = b % 2
                step(dve.tensor_reduce(stat[0:NS, s, 6:7], sc[s][:, 0:NK], AX.X, ALU.max))
                dve.tensor_scalar(stat[0:NS, s, 4:5], stat[0:NS, s, 6:7], -SCALE, None, ALU.mult).then_inc(sem("a_smax"), 1)

            def sample_rest(b):
                s = b % 2
                once(dve, "a_sp", b + 1)
                step(dve.reciprocal(stat[0:NS, s, 5:6], stat[0:NS, s, 5:6]))
                dve.tensor_scalar(sc[s][:, 0:NK], sc[s][:, 0:NK], stat[0:NS, s, 5:6], None, ALU.mult).then_inc(sem("a_spn"), 1)

            def sample_out(b):
                s = b % 2
                once(dve, "a_sp_turned", b + 1)
                dve.tensor_copy(spT[:, s, 0:512], psum[:, 7, :])
                dve.tensor_copy(spT[0:NS, s, 512:512 + NS], psum[0:NS, 6, 0:NS]).then_inc(sem("a_spt"), 1)
                once(dve, "a_spv_done", b + 1)
                dve.tensor_copy(OL[:, :, b].rearrange("p c h t -> p c (h t)"),
                                psum[:, 7, 0:2 * NS].rearrange("p (c q) -> p c q", c=2)).then_inc(sem("a_sol"), 1)
            for b in range(NB):
                s = b % 2
                if b >= 2:
                    once(dve, "a_sp_turned", b - 1)
                for q in range(4):
                    e = 4 * b + q
                    once(dve, "a_latt_a", e + 1)
                    bk = 3 * (e % 2)
                    dve.tensor_copy(latT[:, e % 2, 1, :], psum[:, bk + 1, :]).then_inc(sem("a_latt"), 1)
                    if q > 0:
                        once(dve, "a_ssc_done", 5 * b + q)
                        dve.tensor_copy(sc[s][:, (q - 1) * 512:q * 512], psum[0:NS, 6, :]).then_inc(sem("a_ssc"), 1)
                    if q == 3 and b > 0:
                        sample_rest(b - 1)
                once(dve, "a_ssc_done", 5 * b + 4)
                dve.tensor_copy(sc[s][:, 1536:2048], psum[0:NS, 6, :]).then_inc(sem("a_ssc"), 1)
                once(dve, "a_ssc_done", 5 * b + 5)
                dve.tensor_tensor(sc[s][:, PAST:NK], psum[0:NS, 6, 0:NS], at_("own")[:, b * NS:(b + 1) * NS], ALU.add
                                  ).then_inc(sem("a_ssc"), 1)
                once(dve, "a_ssc", 5 * b + 5)
                sample_softmax(b)
                if b > 0:
                    sample_out(b - 1)
            sample_rest(NB - 1)
            sample_out(NB - 1)
            once(dve, "a_so_done", 1)
            dve.tensor_copy(fbuf8(), psum[:, 0, 0:MH * NS].rearrange("p (h q) -> p h q", h=MH)).then_inc(sem("a_so"), 1)
            once(dve, "a_o_hi", MH // 2 + 1)
            dve.tensor_tensor(xn_lo[:, :, SEQ:T], fbuf8(), xn_hi[:, :, SEQ:T].bitcast(F32), ALU.subtract
                              ).then_inc(sem("a_o_split"), 1)
            for i in range(H):
                dve_split(dve, u0 + 7 + i + 1)
                dve_take_y(dve, n, i, u0 + 7 + i)
        SP["mla"], PE["mla"], ACTE["mla"], DVE["mla"] = sp_mla, pe_mla, act_mla, dve_mla


        vec_ready, out_rows = sem("vec_ready"), sem("out_rows")
        vec_rows = []
        for src, r0, cnt in ((a["norm_gains"].rearrange("l n (k p) -> (l n k) p", p=P), V_GAIN, NGAIN),
                             (a["gdn_conv_w"].rearrange("g j (k p) -> (g j k) p", p=P), V_CONV, NCONV),
                             (a["gdn_norm_w"], V_GN, 2),
                             (a["mla_q_norm"].rearrange("g (k p) -> (g k) p", p=P), V_QN, QR // P),
                             (a["mla_kv_norm"].rearrange("g (k p) -> (g k) p", p=P), V_KVN, KVR // P)):
            r = 0
            while r < cnt:
                q = r0 + r
                m = min(cnt - r, P - q % P)
                vec_rows.append((vt[q % P:q % P + m, q // P, :], src[r:r + m, :]))
                r += m

        @block.sync
        def _(sp):
            sp.dma_start(base[:], a["c_base"]).then_inc(sem("base_in"), 16)
            for t, (cols, src, _) in enumerate(token_tiles):
                sp.dma_start(xin(t)[0:cols.stop - cols.start], src).then_inc(sem("x_in"), 16)
            for dst, src in vec_rows:
                sp.dma_start(dst, src).then_inc(sem("vec_in"), 16)
            for n, sub in enumerate(subs):
                here[0] = n
                SP[sub[0]](sp, n)
            for t, (cols, _, dst) in enumerate(token_tiles):
                sp.wait_ge(out_rows, 2 * t + 2)
                sp.dma_start(dst, xin(t)[0:cols.stop - cols.start]).then_inc(sem("y_stored"), 16)
            sp.wait_ge(sem("y_stored"), 16 * len(token_tiles))

        @block.tensor
        def _(pe):
            pe.wait_ge(sem("base_in"), 16)
            pe.wait_ge(sem("x_in"), 48)
            for k in range(KC):
                for t, (cols, _, _) in enumerate(token_tiles):
                    m = cols.stop - cols.start
                    last = pe.transpose(psum[:, k, cols], xin(t)[0:m, k * P:(k + 1) * P], ident[0:m, 0:m])
                last.then_inc(sem("x_turned"), 1)
            pe.wait_ge(sem("vec_in"), 16 * len(vec_rows))
            pe.wait_ge(x_ready, 2)
            for c in range(4):
                m = min(P, V_ALL - c * P)
                last = pe.transpose(psum[:, 2, c * P:c * P + m], vt[0:m, c, :], ident[0:m, 0:m])
            last.then_inc(sem("vec_turned"), 1)
            for n, sub in enumerate(subs):
                here[0] = n
                pe_sum_squares(pe, 2 * n)
                PE[sub[0]](pe, n)
                pe_sum_squares(pe, 2 * n + 1)
            pe.wait_ge(x_ready, H * (NSUB + 1))
            for t, (cols, _, _) in enumerate(token_tiles):
                m = cols.stop - cols.start
                for half in range(2):
                    for q in range(4):
                        last = pe.transpose(psum[0:m, 2 * t + half + 2, q * P:(q + 1) * P], x[:, 4 * half + q, cols],
                                            ident)
                    last.then_inc(sem("rows_turned"), 1)

        @block.scalar
        def _(act):
            act_split(act, 0)
            act.wait_ge(sem("eps_set"), 2)
            act.wait_ge(sem("x_turned"), KC)
            for n, sub in enumerate(subs):
                here[0] = n
                act_pre(act, n)
                ACTE[sub[0]](act, n)
                act_root(act, 2 * n + 1)

        @block.vector
        def _(dve):
            dve.memset(eps_t[:, 0:1], EPS).then_inc(sem("eps_set"), 1)
            dve.memset(eps_t[:, 1:2], P * EPS).then_inc(sem("eps_set"), 1)
            dve_split(dve, 0)
            for i in range(H):
                dve.wait_ge(sem("x_turned"), 2 * i + 2)
                dve.tensor_copy(x[:, 2 * i:2 * i + 2, :], psum[:, 2 * i:2 * i + 2, 0:T]).then_inc(x_ready, 1)
            dve.wait_ge(sem("vec_turned"), 1)
            dve.tensor_copy(vec[:], psum[:, 2, 0:V_ALL]).then_inc(vec_ready, 1)
            dve.wait_ge(vec_ready, 1)
            gains = vec[:, V_GAIN:V_GAIN + NGAIN].rearrange("p (l n k) -> p l n k", l=DEPTH, n=6)
            for n in (1, 5):
                dve.tensor_scalar(gains[:, :, n, :], gains[:, :, n, :], 0.5, None, ALU.mult).then_inc(vec_ready, 1)
            for n, sub in enumerate(subs):
                here[0] = n
                dve_pre(dve, n)
                DVE[sub[0]](dve, n)
                dve_update(dve, n)
            for t, (cols, _, _) in enumerate(token_tiles):
                m = cols.stop - cols.start
                for half in range(2):
                    dve.wait_ge(sem("rows_turned"), 2 * t + half + 1)
                    dve.tensor_copy(xin(t)[0:m, 512 * half:512 * half + 512],
                                    psum[0:m, 2 * t + half + 2, :]).then_inc(out_rows, 1)

        @block.gpsimd
        def _(pool):
            for n, sub in enumerate(subs):
                if sub[0] in POOL:
                    POOL[sub[0]](pool, n)


INS = ["x_prompt", "x_sample", "state_gdn_S", "state_gdn_conv", "cache_mla_latent", "cache_mla_rope",
       "state_mlstm_C", "state_mlstm_n", "state_mlstm_m", "page_table", "norm_gains", "w_ffn_up", "w_ffn_down",
       "gdn_w_in", "gdn_conv_w", "gdn_a_log", "gdn_dt_bias", "gdn_norm_w", "gdn_w_out", "mla_w_in", "mla_q_norm",
       "mla_kv_norm", "mla_w_uq", "mla_w_ukv", "mla_w_out", "mlstm_w_in", "mlstm_i_bias", "mlstm_f_bias",
       "mlstm_w_out"]
OUTS = [("y_prompt", (1, SEQ, D)), ("y_sample", (NB, NT, D)),
        ("gdn_S_p", (2, 1, HG, P, P)), ("gdn_S_s", (2, NB, HG, P, P)),
        ("gdn_conv_p", (2, 1, 3, GQKV)), ("gdn_conv_s", (2, NB, 3, GQKV)),
        ("mla_lat_p", (1, SEQ // PAGE, PAGE, KVR)), ("mla_lat_s", (1, NB, NT, KVR)),
        ("mla_rope_p", (1, SEQ // PAGE, PAGE, ROPE)), ("mla_rope_s", (1, NB, NT, ROPE)),
        ("ml_C_p", (1, 1, LH, P, 256)), ("ml_C_s", (1, NB, LH, P, 256)),
        ("ml_n_p", (1, 1, LH, P)), ("ml_n_s", (1, NB, LH, P)), ("ml_m_p", (1, 1, LH)), ("ml_m_s", (1, NB, LH))]


def kernel(**inputs):
    import concourse.bacc as bacc
    from concourse.bass_utils import run_bass_kernel_spmd

    nc = bacc.Bacc("TRN2", target_bir_lowering=False, num_devices=1)
    arrays = {name: np.ascontiguousarray(inputs[name]) for name in INS}
    arrays.update({name: np.ascontiguousarray(t[0]) for name, t in tables().items()})
    aps = {name: nc.dram_tensor(name, v.shape, mybir.dt.from_np(v.dtype), kind="ExternalInput").ap()
           for name, v in arrays.items()}
    for name, shape in OUTS:
        aps[name] = nc.dram_tensor(name, shape, F32, kind="ExternalOutput").ap()
    trunk(nc, aps, sublayers())
    r = run_bass_kernel_spmd(nc, [arrays], core_ids=[0])
    return tuple(r.results[0][name] for name, _ in OUTS)
```

```python
from contextlib import ExitStack

import numpy as np

import concourse.bass as bass
from concourse import mybir

F32 = mybir.dt.float32
F32R = mybir.dt.float32r
I32 = mybir.dt.int32
ALU = mybir.AluOpType
ACT = mybir.ActivationFunctionType
AX = mybir.AxisListType

P = 128
D = 1024
KC = D // P
SEQ = 256
NB, NT = 8, 4
NS = NB * NT
T = SEQ + NS
DFF = ((8 * D // 3 + 127) // 128) * 128
FC = DFF // P
PAIRS = FC // 2
DEPTH = 4
MIXER = [i % 3 for i in range(DEPTH)]
EPS = 1e-6
CH = 128
HG = 8
MH = 8
LH = 4
GQKV = 3 * HG * P
PAST, PAGE = 2048, 128
NP = PAST // PAGE
N_PHYS = (5 * NB * NP + 3) // 4
QR, KVR, ROPE = 384, 256, 64
SCALE = (128 + 64) ** -0.5
LV = 7
NEG = -1e30

UNIT = 2048
NRAW = 4
NSPL = 2




def tables():
    def pack(items):
        cols, at, n = [], {}, 0
        for name, a in items:
            full = np.zeros((P, a.shape[1]), np.float32)
            full[:a.shape[0]] = a
            at[name] = (n, a.shape[1], a.shape[0])
            n += a.shape[1]
            cols.append(full)
        return np.concatenate(cols, axis=1), at

    j, i = np.arange(P)[:, None], np.arange(P)[None, :]
    js, si = np.arange(P)[:, None], np.arange(NS)[None, :]
    same = (js // NT == si // NT) & (js < NS)
    incl = np.concatenate([j <= i, j <= i, same & (js <= si)], axis=1)
    strict = np.concatenate([j < i, j < i, same & (js < si)], axis=1)
    tok = np.arange(T)
    start_s = (tok >= SEQ) & ((tok - SEQ) % NT == 0)
    start_g = start_s | ((tok < SEQ) & (tok % CH == 0))
    start_m = start_s | (tok == 0)
    rows = lambda a: np.tile(a.astype(np.float32), (8, 1))
    select = np.repeat(np.eye(8, dtype=np.float32), P, axis=1)
    mask = np.where(incl, 0.0, NEG).astype(np.float32)
    gdn = [("mask", mask), ("strict", strict.astype(np.float32))]
    for l in range(LV):
        b = 2 ** l
        gdn.append((f"level{l}", ((j // (2 * b) == i // (2 * b)) & (j // b < i // b)).astype(np.float32)))
    seqcol = (np.arange(NS)[:, None] // NT == np.arange(NB)[None, :]).astype(np.float32)
    gdn += [("keep", rows(~start_g)), ("select", select), ("seqcol", seqcol)]
    wide = np.concatenate([mask[:, 0:P], np.zeros((P, P), np.float32), mask[:, P:]], axis=1)
    mls = [("mask", wide), ("keep", rows(~start_m)), ("drop", rows(np.where(start_m, NEG, 0.0))),
           ("select", select), ("seqcol", seqcol)]
    half = ROPE // 2
    inv = (10000.0 ** (-np.arange(half, dtype=np.float32) / half)).astype(np.float32)
    pos = np.where(tok < SEQ, tok, PAST + (tok - SEQ) % NT).astype(np.float32)
    ang = (inv[:, None] * pos[None, :]).astype(np.float32)
    rot = np.zeros((ROPE, ROPE), np.float32)
    for m in range(half):
        rot[m + half, m] = -1.0
        rot[m, m + half] = 1.0
    causal = np.where(i <= j, 0.0, NEG).astype(np.float32)
    own = np.full((NS, NB, NS), NEG, np.float32)
    for b in range(NB):
        for r in range(NS):
            own[r, b, b * NT:b * NT + r % NT + 1] = 0.0
    mla = [("cos", np.concatenate([np.cos(ang)] * 2)), ("sin", np.concatenate([np.sin(ang)] * 2)),
           ("rot", rot), ("own", own.reshape(NS, NB * NS)), ("causal", np.concatenate([causal, 0 * causal, causal], axis=1))]
    base = [("ident", np.eye(P, dtype=np.float32)), ("ones", np.ones((P, P), np.float32))]
    return {"c_base": pack(base), "c_gdn": pack(gdn), "c_mla": pack(mla), "c_mlstm": pack(mls)}



SIGNALS = {
    "gdn": dict(
        g_tab_in=48, g_conv_in=16, g_conv_out=32, g_s_in0=64, g_s_in1=64, g_s_out0=128, g_s_out1=128,
        g_hist_turned=1, g_ss=8, g_tail_turned=6, g_col_turned=1, g_bc_done=8, g_kk=8, g_p_done=56,
        g_xp_done=48, g_ks=8, g_kd_turned=8, g_r_turned=8, g_vn_done=8, g_s1_done=8, g_o1_done=8, g_ks1=8,
        g_r1_turned=8, g_vn1_done=8, g_o_done=8, g_ds_done=8, g_oss=8, g_evac=16, g_silu=12, g_sq=8, g_qln=8,
        g_root=8, g_alog=1, g_act_seq=3, g_lnp=1, g_eb=1, g_rows=1, g_trow_ready=6, g_bc=8, g_dt=8, g_pc=48,
        g_kq=8, g_kd=8, g_vn=8, g_s1=8, g_r1=8, g_vn1=8, g_osq=8, g_oln=8, g_or=8, g_o_hi=8, g_gate_read=2,
        g_dve_seq=120, g_hist=1, g_cbuf_half=2, g_cbuf_set=1, g_conv=12, g_tail=12, g_qk_unit=8, g_abs=1,
        g_gg=1, g_beta=1, g_ncol=1, g_tm=8, g_ao=56, g_xupd=56, g_qg=8, g_kdt=8, g_rt=8, g_r=8, g_rt1=8, g_o=8,
        g_sp_new=8, g_kdb=8, g_s_new=8, g_on=8, g_o_split=8,
    ),
    "mla": dict(
        a_tab_in=32, a_pages_in=16, a_tok_out=96, a_lat_in0=512, a_lat_in1=512, a_lat_in2=512, a_lat_in3=512, a_wk_turned=4, a_css=1,
        a_krot=1, a_qrot=4, a_k_done=4, a_v_done=4, a_ql_done=1, a_tok_turned=1, a_sc_done=8, a_p_turned=8,
        a_pv_done=8, a_lat_turned=32, a_ssc_done=40, a_sp_turned=8, a_spv_done=8, a_so_done=1, a_ol_turned=1, a_olf=1, a_craw=3,
        a_csq=2, a_act_seq=1, a_croot=1, a_cq_hi=1, a_q_evac=4, a_v=4, a_ql=1, a_p=8, a_pt=8, a_o_hi=5,
        a_latt_a=32, a_sp=8, a_wkt=4, a_cqn=1, a_ckv=1, a_cq_split=1, a_dve_seq=37, a_kr=1, a_q=4, a_k=4,
        a_tok=1, a_pm=8, a_max=8, a_pn=8, a_o_pair=4, a_o_low=4, a_o_split=2, a_latt=32, a_ssc=40, a_smax=8,
        a_spn=8, a_spt=8, a_sol=8, a_so=1,
    ),
    "mlstm": dict(
        l_tab_in=80, l_c_in0=32, l_c_in1=32, l_c_out0=64, l_c_out1=64, l_rows_out=64, l_n_turned=2,
        l_col_turned=1, l_bc_done=4, l_kk=4, l_num=4, l_kd_turned=4, l_cp_done=4, l_dc_done=4, l_evac=12,
        l_act_seq=1, l_lnp=1, l_rows=1, l_bc=4, l_w_ready=4, l_den=4, l_kd=4, l_cp=4, l_o_hi=4, l_n_out=1,
        l_dve_seq=33, l_abs=1, l_m_new=1, l_pre_rows=1, l_gate_sum=4, l_acol=1, l_tm=4, l_qn=4, l_st=4,
        l_kdt=4, l_nall=4, l_h=4, l_kdb=4, l_c_new=4, l_o_split=4,
    ),
}


MIXERS = ("gdn", "mla", "mlstm")
DOWN_K = (6, 6, 5, 5)
NGAIN = DEPTH * 6 * KC
NCONV = 2 * 4 * (GQKV // P)
V_GAIN, V_CONV, V_GN = 0, NGAIN, NGAIN + NCONV
V_QN, V_KVN, V_ALL = V_GN + 2, V_GN + 2 + QR // P, V_GN + 2 + QR // P + KVR // P


def sublayers():
    subs, seen = [], {}
    for l in range(DEPTH):
        kind = MIXERS[MIXER[l]]
        n = seen.get(kind, 0)
        seen[kind] = n + 1
        subs += [("ffn", l, 0), (kind, l, n), ("ffn", l, 1)]
    return subs


def cols_units(w, k, start, stop, group=256):
    v = w.rearrange("(k p) n -> p k n", p=P)
    return [(v[:, 0:k, c:min(c + group, stop)], k, min(group, stop - c)) for c in range(start, stop, group)]


def units_of(sub, a):
    kind, l, n = sub
    if kind == "ffn":
        up = a["w_ffn_up"][l, n].rearrange("(k p) n -> p k n", p=P)
        down = a["w_ffn_down"][l, n].rearrange("(k p) n -> p k n", p=P)
        out = []
        for j in range(PAIRS):
            for half in range(2):
                c = half * DFF + j * 256
                out.append((up[:, :, c:c + 256], KC, 256))
        for i in range(KC // 2):
            k = 0
            for nk in DOWN_K:
                out.append((down[:, k:k + nk, i * 256:(i + 1) * 256], nk, 256))
                k += nk
        return out
    if kind == "gdn":
        w = a["gdn_w_in"][n]
        return (cols_units(w, KC, GQKV + HG * P, GQKV + HG * P + 2 * HG) + cols_units(w, KC, 0, GQKV + HG * P)
                + cols_units(a["gdn_w_out"][n], KC, 0, D))
    if kind == "mla":
        w = a["mla_w_in"][n]
        return (cols_units(w, KC, 0, QR + KVR + ROPE) + cols_units(a["mla_w_uq"][n], QR // P, 0, MH * 192, 384)
                + cols_units(a["mla_w_out"][n], KC, 0, D))
    w = a["mlstm_w_in"][n]
    return (cols_units(w, KC, 3072, 3080) + cols_units(w, KC, 0, 3072) + cols_units(a["mlstm_w_out"][n], KC, 0, D))


def trunk(nc, a, subs):
    ctx = ExitStack()
    sems = {}
    TAB = tables()

    def sb(name, shape, dt=F32):
        return ctx.enter_context(nc.sbuf_tensor(name, shape, dt))

    place, counted = {}, {}
    for n, sub in enumerate(subs):
        place[n], used = {}, {}
        for name, count in SIGNALS.get(sub[0], {}).items():
            kind = "mix_dma" if count % 16 == 0 and name.endswith(("_in", "_in0", "_in1", "_in2", "_in3", "_out", "_out0", "_out1")) else "mix"
            used[kind] = used.get(kind, -1) + 1
            pool = f"{kind}{used[kind]}"
            place[n][name] = (pool, counted.get(pool, 0))
            counted[pool] = counted.get(pool, 0) + count
    here = [0]

    def sem(name):
        name = place[here[0]][name][0] if name in place.get(here[0], {}) else name
        if name not in sems:
            sems[name] = ctx.enter_context(nc.semaphore(name))
        return sems[name]

    def before(name):
        return place[here[0]][name][1] if name in place.get(here[0], {}) else 0

    def once(eng, name, v):
        eng.wait_ge(sem(name), v + before(name))

    with ctx:
        raw = [sb(f"raw{s}", [P, UNIT]) for s in range(NRAW)]
        w_hi = [sb(f"w_hi{s}", [P, UNIT], F32R) for s in range(NSPL)]
        w_lo = [sb(f"w_lo{s}", [P, UNIT], F32R) for s in range(NSPL)]
        x = sb("x", [P, KC, T])
        xn_hi = sb("xn_hi", [P, KC, T], F32R)
        xn_lo = sb("xn_lo", [P, KC, T], F32R)
        base = sb("base", [P, 2 * P])
        ident, ones = base[:, 0:P], base[:, P:2 * P]
        vec = sb("vec", [P, V_ALL])
        eps_t = sb("eps_t", [P, 2])
        rr = sb("rr", [P, 2, T])
        y = sb("y", [P, KC, T])
        sq = sb("sq", [P, KC, T])
        fbuf = sb("fbuf", [P, 2, 2, T])
        psum = ctx.enter_context(nc.psum_tensor("psum", [P, 8, 512], F32))
        free_at = -(-nc.sbuf_base // 64) * 64
        mix_words = (nc.sbuf_usable_end - free_at) // 4

        def at(name, shape, word, dt=F32):
            assert word + int(np.prod(shape[1:])) <= mix_words, (name, mix_words)
            return nc.alloc_sbuf_tensor_at(name, shape, dt, offset=free_at + 4 * word)
        h_hi = at("h_hi", [P, FC, T], 0, F32R)
        h_lo = at("h_lo", [P, FC, T], FC * T, F32R)
        sg = at("sg", [P, 2, 2, T], 2 * FC * T)

        raw_in = [sem(f"raw_in{s}") for s in range(NRAW)]
        hi_ready, lo_ready, unit_used = sem("hi_ready"), sem("lo_ready"), sem("unit_used")
        ln_done = sem("ln_done")
        block = ctx.enter_context(nc.Block())

        units, ubase, uend = [], [], []
        for sub in subs:
            ubase.append(len(units))
            units += units_of(sub, a)
            uend.append(len(units))
        NU = len(units)
        NSUB = len(subs)
        nffn = [sum(q[0] == "ffn" for q in subs[:n]) for n in range(NSUB)]
        nmix = [n - nffn[n] for n in range(NSUB)]

        def gain(l, n, k):
            r = V_GAIN + (l * 6 + n) * KC + k
            return vec[:, r:r + 1]

        def post_gain(sub):
            return 3 if sub[0] != "ffn" else (1, 5)[sub[2]]

        def pre_gain(sub):
            return 2 if sub[0] != "ffn" else (0, 4)[sub[2]]

        def wview(buf, u):
            _, k, n = units[u]
            return buf[:, 0:k * n].rearrange("p (k n) -> p k n", k=k)

        def xin(t):
            return (y, sq, fbuf)[t][:].rearrange(("p k t -> p (k t)", "p a b t -> p (a b t)")[t == 2])[:, 0:D]

        vt = at("vt", [P, 4, P], (mix_words - 4 * P) // 8 * 8)

        def sp_unit(sp, u):
            if u >= NRAW:
                sp.wait_ge(lo_ready, u - NRAW + 1)
            sp.dma_start(wview(raw[u % NRAW], u), units[u][0]).then_inc(raw_in[u % NRAW], 16)

        def act_split(act, u, i=0):
            if u >= NU:
                return
            act.wait_ge(raw_in[u % NRAW], 16 * i + 16 * (u // NRAW + 1))
            if u >= NSPL:
                act.wait_ge(unit_used, 4 * i + u - NSPL + 1)
            act.activation(wview(w_hi[u % NSPL], u), wview(raw[u % NRAW], u), ACT.Copy).then_inc(hi_ready, 1)

        def dve_split(dve, u, i=0):
            if u >= NU:
                return
            dve.wait_ge(hi_ready, 4 * i + u + 1)
            dve.tensor_tensor(wview(w_lo[u % NSPL], u), wview(raw[u % NRAW], u),
                              wview(w_hi[u % NSPL], u).bitcast(F32), ALU.subtract).then_inc(lo_ready, 1)

        def pe_unit(pe, u, outs, hi, lo, start, stop, i=0, ready=None, late=0):
            _, nk, n = units[u]
            pe.wait_ge(lo_ready, 4 * i + u + 1)
            wh, wl = wview(w_hi[u % NSPL], u), wview(w_lo[u % NSPL], u)
            for m, out in list(enumerate(outs))[::-1 if late else 1]:
                if late and m == 0:
                    pe.wait_ge(ln_done, late)
                c = slice(m * P, min((m + 1) * P, n))
                for k in range(nk):
                    if ready is not None and m == 0:
                        ready(k)
                    st, sp_ = start and k == 0, stop and k == nk - 1
                    pe.matmul(out, wh[:, k, c], hi(k), start=st, stop=False)
                    pe.matmul(out, wh[:, k, c], lo(k), start=False, stop=False)
                    last = pe.matmul(out, wl[:, k, c], hi(k), start=False, stop=sp_)
            last.then_inc(unit_used, 1)

        y_copied, sq_ready, ss_done, r_ready = sem("y_copied"), sem("sq_ready"), sem("ss_done"), sem("r_ready")
        x_ready, f_ready, xhi_ready, xlo_ready = sem("x_ready"), sem("f_ready"), sem("xhi_ready"), sem("xlo_ready")
        half_ready = sem("half_ready")
        H = KC // 2

        def pe_sum_squares(pe, q, i):
            pe.wait_ge(sq_ready, H * q + i + 1)
            if q % 2 == 1 and i == 0:
                pe.wait_ge(y_copied, H * (q // 2) + 1)
            for k in (2 * i, 2 * i + 1):
                last = pe.matmul(psum[:, q % 2, 0:T], ones, sq[:, k, :], start=k == 0, stop=k == KC - 1)
            if i == H - 1:
                last.then_inc(ss_done, 1)

        def act_root(act, q):
            act.wait_ge(ss_done, q + 1)
            act.activation(rr[:, q % 2, :], psum[:, q % 2, 0:T], ACT.Ln, scale=1.0 / D,
                           bias=eps_t[:, 0:1]).then_inc(ln_done, 1)
            act.wait_ge(ln_done, q + 1)
            act.activation(rr[:, q % 2, :], rr[:, q % 2, :], ACT.Exp, scale=-0.5).then_inc(r_ready, 1)

        def act_square_x(act, n, i):
            q = 2 * n
            if q > 0:
                act.wait_ge(ss_done, q)
            act.activation(sq[:, 2 * i:2 * i + 2, :], x[:, 2 * i:2 * i + 2, :], ACT.Square).then_inc(sq_ready, 1)

        def act_pre(act, n):
            for i in range(H):
                act.wait_ge(x_ready, H * n + i + 1)
                act_square_x(act, n, i)
            act_root(act, 2 * n)
            for i in range(H):
                act.wait_ge(f_ready, H * nmix[n] + i + 1)
                act.activation(xn_hi[:, 2 * i:2 * i + 2, :], fbuf[:, i % 2], ACT.Copy).then_inc(xhi_ready, 1)

        def act_pre_ffn(act, n):
            l, g = subs[n][1], pre_gain(subs[n])
            if n == 0:
                act.wait_ge(vec_ready, 3)
            for i in range(H):
                act.wait_ge(x_ready, H * n + i + 1)
                for k in (2 * i, 2 * i + 1):
                    last = act.activation(xn_hi[:, k, :], x[:, k, :], ACT.Copy, scale=gain(l, g, k))
                last.then_inc(xhi_ready, 1)
                if i == 0:
                    act_split(act, ubase[n] + 1)
                else:
                    if i == 1:
                        act_square_x(act, n, 0)
                    act_square_x(act, n, i)

        def dve_low_x(dve, n, i):
            l, g = subs[n][1], pre_gain(subs[n])
            dve.wait_ge(xhi_ready, H * n + i + 1)
            for k in (2 * i, 2 * i + 1):
                last = dve.scalar_tensor_tensor(out=xn_lo[:, k, :], in0=x[:, k, :], scalar=gain(l, g, k),
                                                in1=xn_hi[:, k, :].bitcast(F32), op0=ALU.mult, op1=ALU.subtract)
            last.then_inc(xlo_ready, 1)
            if i == 1:
                dve_split(dve, ubase[n] + 1)

        def dve_enter(dve, n, chunk):
            ffn = n < NSUB and subs[n][0] == "ffn"
            for i in range(H + 1):
                if i < H:
                    chunk(i)
                if i > 0 and ffn:
                    dve_low_x(dve, n, i - 1)

        def dve_pre(dve, n):
            l, g = subs[n][1], pre_gain(subs[n])
            if subs[n][0] == "ffn":
                return
            dve.wait_ge(r_ready, 2 * n + 1)
            if n == 0:
                dve.wait_ge(vec_ready, 3)
            for i in range(H + 1):
                if i < H:
                    if i >= 2:
                        dve.wait_ge(xlo_ready, H * n + i - 1)
                    for k in (2 * i, 2 * i + 1):
                        last = dve.scalar_tensor_tensor(out=fbuf[:, i % 2, k % 2], in0=x[:, k, :], scalar=gain(l, g, k),
                                                        in1=rr[:, 0, :], op0=ALU.mult, op1=ALU.mult)
                    last.then_inc(f_ready, 1)
                if i > 0:
                    dve.wait_ge(xhi_ready, H * n + i)
                    dve.tensor_tensor(xn_lo[:, 2 * i - 2:2 * i, :], fbuf[:, (i - 1) % 2],
                                      xn_hi[:, 2 * i - 2:2 * i, :].bitcast(F32), ALU.subtract).then_inc(xlo_ready, 1)

        def xn(part):
            return lambda k: part[:, k, :]

        def x_chunks(pe, n):
            return lambda k: pe.wait_ge(xlo_ready, H * n + k // 2 + 1) if k % 2 == 0 else None

        def dve_take_y(dve, n, i):
            l, g = subs[n][1], post_gain(subs[n])
            dve.wait_ge(sq_ready, H * (2 * n + 1) + i + 1)
            for k in (2 * i, 2 * i + 1):
                last = dve.tensor_scalar(y[:, k, :], psum[:, k, 0:T], gain(l, g, k), None, ALU.mult)
            last.then_inc(y_copied, 1)

        def act_square_y(act, n, i, u):
            act.wait_ge(unit_used, u + 1)
            act.activation(sq[:, 2 * i:2 * i + 2, :], psum[:, 2 * i:2 * i + 2, 0:T], ACT.Square).then_inc(sq_ready, 1)

        def dve_update(dve, n):
            dve.wait_ge(r_ready, 2 * n + 2)
            t = sem("x_term")

            def chunk(i):
                c = slice(2 * i, 2 * i + 2)
                dve.tensor_tensor(y[:, c, :], y[:, c, :], rr[:, 1:2, :].to_broadcast([P, 2, T]), ALU.mult).then_inc(t, 1)
                dve.wait_ge(t, H * n + i + 1)
                dve.tensor_tensor(x[:, c, :], x[:, c, :], y[:, c, :], ALU.add).then_inc(x_ready, 1)
            dve_enter(dve, n + 1, chunk)

        def pe_out(pe, n, u0, hi, lo, ready):
            for i in range(H):
                pe_unit(pe, u0 + i, [psum[:, 2 * i, 0:T], psum[:, 2 * i + 1, 0:T]], hi, lo, True, True,
                        ready=ready if i == 0 else None)
                if i > 0:
                    pe_sum_squares(pe, 2 * n + 1, i - 1)
            pe_sum_squares(pe, 2 * n + 1, H - 1)

        silu_done, h_done, hhi_done, hlo_done = sem("silu_done"), sem("h_done"), sem("hhi_done"), sem("hlo_done")
        gate_ready, pair_read = sem("gate_ready"), sem("pair_read")
        ROUNDS = PAIRS // 2
        DU = len(DOWN_K)

        def sp_ffn(sp, n):
            _, l, f = subs[n]
            up = a["w_ffn_up"][l, f].rearrange("(k p) n -> p k n", p=P)
            u0 = ubase[n]
            for q in range(4):
                sp_unit(sp, u0 + q)
            with sp.Fori(1, ROUNDS) as i:
                for q in range(4):
                    u = u0 + q
                    sp.wait_ge(lo_ready, 4 * i + u - NRAW + 1)
                    sp.dma_start(wview(raw[u % NRAW], u),
                                 up[:, :, bass.ds(512 * i + (q // 2) * 256 + (q % 2) * DFF, 256)]
                                 ).then_inc(raw_in[u % NRAW], 16)
            for u in range(u0 + 4 * ROUNDS, uend[n]):
                sp_unit(sp, u)

        def pe_ffn(pe, n):
            u0, f0 = ubase[n], nffn[n] * PAIRS

            def pair(j, i, jj):
                s = 4 * ((j + 1) % 2)
                if jj is None or jj >= 2:
                    pe.wait_ge(pair_read, 2 * i + f0 + j - 1)
                for g in range(2):
                    pe_unit(pe, u0 + 2 * j + g, [psum[:, s + 2 * g, 0:T], psum[:, s + 2 * g + 1, 0:T]],
                            xn(xn_hi), xn(xn_lo), True, True, i=i, late=2 * n + 1 if jj == 1 and g == 0 else 0)
            for k0 in (0, H):
                for g in range(2):
                    u = u0 + g
                    pe.wait_ge(lo_ready, u + 1)
                    wh, wl = wview(w_hi[u % NSPL], u), wview(w_lo[u % NSPL], u)
                    for k in range(k0, k0 + H):
                        if g == 0 and k % 2 == 0:
                            pe.wait_ge(xlo_ready, H * n + k // 2 + 1)
                        for m in range(2):
                            out, c = psum[:, 4 + 2 * g + m, 0:T], slice(m * P, (m + 1) * P)
                            pe.matmul(out, wh[:, k, c], xn_hi[:, k, :], start=k == 0, stop=False)
                            pe.matmul(out, wh[:, k, c], xn_lo[:, k, :], start=False, stop=False)
                            last = pe.matmul(out, wl[:, k, c], xn_hi[:, k, :], start=False, stop=k == KC - 1)
                    if k0 > 0:
                        last.then_inc(unit_used, 1)
            for i in range(H):
                pe_sum_squares(pe, 2 * n, i)
            pair(1, 0, 1)
            with pe.Fori(1, ROUNDS) as i:
                pair(0, i, None)
                pair(1, i, None)
            pair(PAIRS - 1, 0, PAIRS - 1)
            for i in range(H):
                if i in (0, 2):
                    pe.wait_ge(pair_read, f0 + PAIRS - 1 + i // 2)
                k0 = 0
                for q, nk in enumerate(DOWN_K):
                    if i == 0:
                        pe.wait_ge(hlo_done, f0 + -(-(k0 + nk) // 2))
                    pe_unit(pe, u0 + 2 * PAIRS + DU * i + q, [psum[:, 2 * i, 0:T], psum[:, 2 * i + 1, 0:T]],
                            lambda k: h_hi[:, k0 + k, :], lambda k: h_lo[:, k0 + k, :], q == 0, q == DU - 1)
                    k0 += nk
                    if q == 0 and i > 0:
                        pe_sum_squares(pe, 2 * n + 1, i - 1)
            pe_sum_squares(pe, 2 * n + 1, H - 1)

        def act_ffn(act, n):
            u0, f0 = ubase[n], nffn[n] * PAIRS

            def pair(j, i, first=False):
                act_split(act, u0 + 2 * j + 2, i)
                act_split(act, u0 + 2 * j + 3, i)
                if first:
                    act_root(act, 2 * n)
                    act.preload_act_table_set("silu_and_others")
                act.wait_ge(gate_ready, 2 * i + f0 + j + 1)
                act.activation(sg[:, j % 2], sg[:, j % 2], ACT.Silu).then_inc(silu_done, 1)
                act.wait_ge(h_done, 2 * i + f0 + j + 1)
                dst = h_hi[:, 2 * j:2 * j + 2, :] if isinstance(i, int) else h_hi[:, bass.ds(4 * i + 2 * j, 2), :]
                act.activation(dst, fbuf[:, j % 2], ACT.Copy).then_inc(hhi_done, 1)
            pair(0, 0, first=True)
            pair(1, 0)
            with act.Fori(1, ROUNDS) as i:
                pair(0, i)
                pair(1, i)
            pair(PAIRS - 1, 0)
            act.preload_act_table_set("natural_log_exp_and_others")
            for i in range(H):
                for q in range(DU):
                    if DU * i + q > 0:
                        act_split(act, u0 + 2 * PAIRS + DU * i + q + 1)
                    if i > 0 and q == 0:
                        act_square_y(act, n, i - 1, u0 + 2 * PAIRS + DU * i - 1)
            act_square_y(act, n, H - 1, uend[n] - 1)

        def dve_ffn(dve, n):
            u0, f0 = ubase[n], nffn[n] * PAIRS

            def pair(j, i, first=False):
                s = 4 * ((j + 1) % 2)
                dve_split(dve, u0 + 2 * j + 2, i)
                if first:
                    dve_split(dve, u0 + 2 * j + 3, i)
                dve.wait_ge(unit_used, 4 * i + u0 + 2 * j + 2)
                if first:
                    dve.wait_ge(r_ready, 2 * n + 1)
                r2 = rr[:, 0:1, :].to_broadcast([P, 2, T])
                dve.tensor_tensor(sg[:, j % 2], psum[:, s:s + 2, 0:T], r2, ALU.mult).then_inc(gate_ready, 1)
                dve.tensor_tensor(fbuf[:, j % 2], psum[:, s + 2:s + 4, 0:T], r2, ALU.mult).then_inc(pair_read, 1)
                if not first:
                    dve_split(dve, u0 + 2 * j + 3, i)
                dve.wait_ge(silu_done, 2 * i + f0 + j + 1)
                dve.wait_ge(pair_read, 2 * i + f0 + j + 1)
                dve.tensor_tensor(fbuf[:, j % 2], sg[:, j % 2], fbuf[:, j % 2], ALU.mult).then_inc(h_done, 1)
                dve.wait_ge(hhi_done, 2 * i + f0 + j + 1)
                sl = slice(2 * j, 2 * j + 2) if isinstance(i, int) else bass.ds(4 * i + 2 * j, 2)
                dve.tensor_tensor(h_lo[:, sl, :], fbuf[:, j % 2], h_hi[:, sl, :].bitcast(F32),
                                  ALU.subtract).then_inc(hlo_done, 1)
            pair(0, 0, first=True)
            pair(1, 0)
            with dve.Fori(1, ROUNDS) as i:
                pair(0, i)
                pair(1, i)
            pair(PAIRS - 1, 0)
            for i in range(H):
                for q in range(DU):
                    if DU * i + q > 0:
                        dve_split(dve, u0 + 2 * PAIRS + DU * i + q + 1)
                    if i > 0 and q == 0:
                        dve_take_y(dve, n, i - 1)
            dve_take_y(dve, n, H - 1)

        SP, PE, ACTE, DVE, POOL = {"ffn": sp_ffn}, {"ffn": pe_ffn}, {"ffn": act_ffn}, {"ffn": dve_ffn}, {}

        token_tiles = [(slice(0, P), a["x_prompt"][0, 0:P, :], a["y_prompt"][0, 0:P, :]),
                       (slice(P, 2 * P), a["x_prompt"][0, P:2 * P, :], a["y_prompt"][0, P:2 * P, :]),
                       (slice(SEQ, T), a["x_sample"].rearrange("b t d -> (b t) d"),
                        a["y_sample"].rearrange("b t d -> (b t) d"))]

        table = {k: v for k, (_, v) in TAB.items()}
        w = [0]

        def carve(name, shape):
            t = at(name, shape, w[0])
            w[0] += -(-int(np.prod(shape[1:])) // 8) * 8
            return t
        KDB = sq[0:NS, 4:8, :].rearrange("p k t -> p (k t)")[:, 0:NB * P].rearrange("p (b e) -> p b e", b=NB)
        KDBS = (KDB, y[0:NS, 4:8, :].rearrange("p k t -> p (k t)")[:, 0:NB * P].rearrange("p (b e) -> p b e", b=NB))
        if any(q[0] == "gdn" for q in subs):
            GN = TAB["c_gdn"][0].shape[1]
            qkv = carve("g_qkv", [P, 3 * HG, T])
            gz = carve("g_z", [P, HG, T])
            gtab = carve("g_tab", [P, GN])
            gsm = carve("g_small", [HG, 4])
            ncol = carve("g_ncol", [P, 3, HG])
            w1 = w[0]
            crow = carve("g_crow", [NB * 3, GQKV])
            trow = carve("g_trow", [NB * 3 + 3, GQKV])
            CW = 3 + SEQ + NB * 7
            cbuf = carve("g_cbuf", [P, 2, 2, CW])
            cacc = carve("g_cacc", [P, 2, 2, CW])
            chist = carve("g_chist", [P, 3 * HG, NB * 3])
            tail = carve("g_tail", [P, 3 * HG, NB * 3 + 3])
            w[0] = w1
            X, XT, AT, AN, AO, PC = (carve("g_" + q, [P, 2, T]) for q in ("x", "xt", "at", "an", "ao", "pc"))
            bc = carve("g_bc", [P, 2, 4, T])
            Sin = carve("g_sin", [P, 2, NB, P])
            Sp = carve("g_sp", [P, 2, P])
            R, VN, KD = (carve("g_" + q, [P, 3, P]) for q in ("r", "vn", "kd"))
            R2, VN2, KD2 = (carve("g_" + q, [P, 3, P]) for q in ("r2", "vn2", "kd2"))
            kq = carve("g_kq", [P, 2, NB, 2, NT])
            RS, VS, KS_ = (R, R2), (VN, VN2), (KD, KD2)

        def gt(name):
            o, n, r = table["c_gdn"][name]
            return gtab[0:r, o:o + n]

        CHUNKS = (slice(0, CH), slice(CH, SEQ), slice(SEQ, T))
        rows8 = lambda r: y[0:HG, r, :]
        BETA, EG, ED, GG, T1, T2, T3 = range(7)
        smp = lambda v: v[..., SEQ:T]
        GP = HG // 2

        def sp_gdn(sp, n):
            gi, u0 = subs[n][2], ubase[n]
            if n > 0:
                once(sp, "unit_used", u0)
            sp.dma_start(gtab[:], a["c_gdn"]).then_inc(sem("g_tab_in"), 16)
            sp.dma_start(gsm[:, 0:1], a["gdn_dt_bias"][gi].rearrange("(h o) -> h o", o=1)).then_inc(sem("g_tab_in"), 16)
            sp.dma_start(gsm[:, 1:2], a["gdn_a_log"][gi].rearrange("(h o) -> h o", o=1)).then_inc(sem("g_tab_in"), 16)
            sp.dma_start(crow[:], a["state_gdn_conv"][gi].rearrange("b j c -> (b j) c")).then_inc(sem("g_conv_in"), 16)
            for u in range(u0, uend[n]):
                sp_unit(sp, u)
                if u == u0 + 17 + 2:
                    heads_io(sp, gi)
        def heads_io(sp, gi):
            once(sp, "g_trow_ready", 6)
            sp.dma_start(a["gdn_conv_p"][gi, 0], trow[0:3, :]).then_inc(sem("g_conv_out"), 16)
            sp.dma_start(a["gdn_conv_s"][gi].rearrange("b j c -> (b j) c"), trow[3:27, :]).then_inc(sem("g_conv_out"), 16)
            once(sp, "g_conv_out", 32)
            for h in range(HG + 2):
                if h >= 2:
                    q = h - 2
                    once(sp, "g_s_new", q + 1)
                    sp.dma_start(a["gdn_S_s"][gi, :, h - 2].rearrange("b d e -> d b e"), Sin[:, h % 2]
                                 ).then_inc(sem(f"g_s_out{h % 2}"), 16)
                    once(sp, "g_sp_new", q + 1)
                    sp.dma_start(a["gdn_S_p"][gi, 0, h - 2], Sp[:, h % 2]).then_inc(sem(f"g_s_out{h % 2}"), 16)
                    once(sp, f"g_s_out{h % 2}", 32 * (h // 2))
                if h < HG:
                    sp.dma_start(Sin[:, h % 2], a["state_gdn_S"][gi, :, h].rearrange("b d e -> d b e")
                                 ).then_inc(sem(f"g_s_in{h % 2}"), 16)

        def pe_gdn(pe, n):
            gi, u0 = subs[n][2], ubase[n]
            gates = [psum[0:HG, 4, 0:T], psum[0:HG, 5, 0:T]]
            pe.wait_ge(lo_ready, u0 + 1)
            wh, wl = wview(w_hi[u0 % NSPL], u0), wview(w_lo[u0 % NSPL], u0)
            ready = x_chunks(pe, n)
            for m in range(2):
                for k in range(KC):
                    if m == 0:
                        ready(k)
                    c = slice(m * HG, (m + 1) * HG)
                    pe.matmul(gates[m], wh[:, k, c], xn_hi[:, k, :], start=k == 0, stop=False)
                    pe.matmul(gates[m], wh[:, k, c], xn_lo[:, k, :], start=False, stop=False)
                    last = pe.matmul(gates[m], wl[:, k, c], xn_hi[:, k, :], start=False, stop=k == KC - 1)
            last.then_inc(unit_used, 1)
            once(pe, "g_conv_in", 16)
            for k in range(3 * HG):
                last = pe.transpose(psum[:, 6 + k // 12, (k % 12) * 24:(k % 12) * 24 + 24],
                                    crow[:, k * P:(k + 1) * P], ident[0:24, 0:24])
            last.then_inc(sem("g_hist_turned"), 1)
            for i in range(16):
                if i >= 2:
                    once(pe, "g_evac", i - 1)
                pe_unit(pe, u0 + 1 + i, [psum[:, 2 * (i % 2), 0:T], psum[:, 2 * (i % 2) + 1, 0:T]],
                        xn(xn_hi), xn(xn_lo), True, True)
            for q in range(8):
                once(pe, "g_sq", q + 1)
                if q == 0:
                    once(pe, "g_hist", 1)
                    once(pe, "g_gate_read", 2)
                if q >= 2:
                    once(pe, "g_root", q - 1)
                for k in range(2):
                    last = pe.matmul(psum[:, 4 + 2 * (q % 2) + k, 0:T], ones, sq[:, 2 * (q % 4) + k, :],
                                     start=True, stop=True)
                last.then_inc(sem("g_ss"), 1)
            once(pe, "g_tail", 12)
            for k in range(3 * HG):
                if k == 0:
                    once(pe, "g_evac", 16)
                if k >= 8 and k % 4 == 0:
                    once(pe, "g_trow_ready", k // 4 - 1)
                last = pe.transpose(psum[0:27, (k // 4) % 2, (k % 4) * P:(k % 4 + 1) * P], tail[:, k, :], ident)
                if k % 4 == 3:
                    last.then_inc(sem("g_tail_turned"), 1)
            once(pe, "g_rows", 1)
            once(pe, "g_root", 8)
            for c, cs in enumerate(CHUNKS):
                last = pe.transpose(psum[0:cs.stop - cs.start, 4, c * HG:(c + 1) * HG], rows8(GG)[:, cs],
                                    ident[0:HG, 0:HG])
            last.then_inc(sem("g_col_turned"), 1)
            once(pe, "g_trow_ready", 6)
            once(pe, "g_ncol", 1)
            once(pe, "g_qk_unit", 8)
            flat = qkv[:].rearrange("p k t -> p (k t)")
            for p in range(GP):
                hh = [2 * p, 2 * p + 1]
                for s in range(2):
                    if p > 0:
                        once(pe, "g_o_split", hh[s] - 1)
                        once(pe, "g_s_new", hh[s] - 1)
                    for r in range(4):
                        last = pe.matmul(psum[:, 4 * s + r, 0:T], gt("select")[:, (2 * p + s) * P:(2 * p + s + 1) * P],
                                         rows8(r), start=True, stop=True)
                    last.then_inc(sem("g_bc_done"), 1)
                for s in range(2):
                    once(pe, "g_bc", hh[s] + 1)
                    kh, qh = (HG + 2 * p + s) * T, (2 * p + s) * T
                    for c, cs in enumerate(CHUNKS):
                        keys = flat[:, kh + cs.start:kh + cs.start + P]
                        pe.matmul(psum[:, 4 * s, cs], keys, flat[:, kh + cs.start:kh + cs.stop], start=True, stop=True)
                        last = pe.matmul(psum[:, 4 * s + 1, cs], keys, flat[:, qh + cs.start:qh + cs.stop],
                                         start=True, stop=True)
                    last.then_inc(sem("g_kk"), 1)
                for l in range(LV):
                    ch = CHUNKS if l < 2 else CHUNKS[0:2]
                    e = lambda s: (p * LV + l) * 2 + s + 1
                    for s in range(2):
                        once(pe, "g_ao", e(s))
                        if l > 0:
                            once(pe, "g_xupd", e(s) - 2)
                        for cs in ch:
                            m = cs.stop - cs.start
                            rhs = ident[0:m, 0:m] if l == 0 else X[0:m, s, cs]
                            last = pe.matmul(psum[0:m, 4 * s + 2, cs], AO[0:m, s, cs], rhs, start=True, stop=True)
                        last.then_inc(sem("g_p_done"), 1)
                    for s in range(2):
                        if l == 0:
                            continue
                        once(pe, "g_pc", (p * (LV - 1) + l - 1) * 2 + s + 1)
                        for cs in ch:
                            m = cs.stop - cs.start
                            if l < LV - 1:
                                pe.matmul(psum[0:m, 4 * s, cs], XT[0:m, s, cs], PC[0:m, s, cs], start=True, stop=True)
                            last = pe.matmul(psum[0:m, 4 * s + 3, cs], PC[0:m, s, cs], XT[0:m, s, cs],
                                             start=True, stop=True)
                        last.then_inc(sem("g_xp_done"), 1)
                B = lambda s, b: psum[:, 4 * s + b, :]
                for s in range(2):
                    once(pe, "g_kq", hh[s] + 1)
                    once(pe, f"g_s_in{s}", 16 * (p + 1))
                    for b in range(NB):
                        last = pe.matmul(B(s, 0)[:, 8 * b:8 * b + 8], Sin[:, s, b, :],
                                         kq[:, s, b].rearrange("p a t -> p (a t)"), start=True, stop=True)
                    last.then_inc(sem("g_ks"), 1)
                for s in range(2):
                    once(pe, "g_kdt", hh[s] + 1)
                    for c, cs in enumerate(CHUNKS):
                        last = pe.transpose(B(s, 2)[0:cs.stop - cs.start, c * P:(c + 1) * P], AO[:, s, cs], ident)
                    last.then_inc(sem("g_kd_turned"), 1)
                    once(pe, "g_rt", hh[s] + 1)
                    pe.transpose(B(s, 1)[:, 0:P], X[:, s, CHUNKS[0]], ident)
                    pe.transpose(B(s, 1)[0:NS, P:2 * P], X[:, s, CHUNKS[2]], ident).then_inc(sem("g_r_turned"), 1)
                for s in range(2):
                    once(pe, "g_r", hh[s] + 1)
                    pe.matmul(B(s, 0)[:, 192:320], XT[:, s, CHUNKS[0]], RS[s][:, 0, :], start=True, stop=True)
                    pe.matmul(B(s, 0)[0:NS, 320:448], XT[0:NS, s, CHUNKS[2]], RS[s][0:NS, 2, :],
                              start=True, stop=True).then_inc(sem("g_vn_done"), 1)
                for s in range(2):
                    once(pe, "g_vn", hh[s] + 1)
                    once(pe, "g_kd", hh[s] + 1)
                    pe.matmul(B(s, 2)[:, 384:512], KS_[s][:, 0, :], VS[s][:, 0, :], start=True,
                              stop=True).then_inc(sem("g_s1_done"), 1)
                    pe.matmul(B(s, 3)[:, CHUNKS[0]], VS[s][:, 0, :], AN[:, s, CHUNKS[0]], start=True, stop=True)
                    pe.matmul(B(s, 3)[:, CHUNKS[2]], VS[s][0:NS, 2, :], AN[0:NS, s, CHUNKS[2]], start=True,
                              stop=True).then_inc(sem("g_o1_done"), 1)
                for s in range(2):
                    once(pe, "g_s1", hh[s] + 1)
                    kh = (HG + 2 * p + s)
                    pe.matmul(B(s, 0)[:, 64:192], Sp[:, s, :], qkv[:, kh, CHUNKS[1]], start=True,
                              stop=True).then_inc(sem("g_ks1"), 1)
                for s in range(2):
                    once(pe, "g_rt1", hh[s] + 1)
                    pe.transpose(B(s, 1)[:, 256:384], X[:, s, CHUNKS[1]], ident).then_inc(sem("g_r1_turned"), 1)
                for s in range(2):
                    once(pe, "g_r1", hh[s] + 1)
                    pe.matmul(B(s, 0)[:, 192:320], XT[:, s, CHUNKS[1]], RS[s][:, 1, :], start=True,
                              stop=True).then_inc(sem("g_vn1_done"), 1)
                for s in range(2):
                    once(pe, "g_vn1", hh[s] + 1)
                    pe.matmul(B(s, 1)[:, 384:512], KS_[s][:, 1, :], VS[s][:, 1, :], start=True, stop=True)
                    pe.matmul(B(s, 3)[:, CHUNKS[1]], Sp[:, s, :], PC[:, s, CHUNKS[1]], start=True, stop=False)
                    pe.matmul(B(s, 3)[:, CHUNKS[1]], VS[s][:, 1, :], AN[:, s, CHUNKS[1]], start=False,
                              stop=True).then_inc(sem("g_o_done"), 1)
                for s in range(2):
                    once(pe, "g_osq", hh[s] + 1)
                    pe.matmul(B(s, 2)[:, 0:T], ones, sq[:, s, :], start=True, stop=True).then_inc(sem("g_oss"), 1)
                for s in range(2):
                    once(pe, "g_kdb", hh[s] + 1)
                    once(pe, "g_sp_new", hh[s] + 1)
                    for b in range(NB):
                        last = pe.matmul(B(s, b // 4)[:, (b % 4) * P:(b % 4 + 1) * P], KDBS[s][:, b, :],
                                         VS[s][0:NS, 2, :], start=True, stop=True)
                    last.then_inc(sem("g_ds_done"), 1)
            once(pe, "g_o_split", HG)
            once(pe, "g_s_new", HG)
            pe_out(pe, n, u0 + 17, xn(xn_hi), xn(xn_lo), None)

        def act_gdn(act, n):
            gi, u0 = subs[n][2], ubase[n]
            act_split(act, u0 + 1)
            for i in range(16):
                act_split(act, u0 + i + 2)
                if i < 2:
                    act_gates(act, i)
                act.wait_ge(unit_used, u0 + i + 2)
                b = 2 * (i % 2)
                src = psum[:, b:b + 2, :]
                if i < 12:
                    if i >= 2:
                        once(act, "g_tail", i - 1)
                        once(act, "g_conv", i - 1)
                    else:
                        once(act, "g_cbuf_set", 1)
                    act.activation(cbuf[:, i % 2, :, 3:3 + SEQ], src[:, :, 0:SEQ], ACT.Copy)
                    for k in range(2):
                        last = act.activation(
                            cbuf[:, i % 2, k, 3 + SEQ:CW].rearrange("p (b t) -> p b t", b=NB)[:, :, 3:7],
                            src[:, k, SEQ:T].rearrange("p (b t) -> p b t", b=NB), ACT.Copy)
                    last.then_inc(sem("g_evac"), 1)
                else:
                    z2 = 2 * (i - 12)
                    act.activation(gz[:, z2:z2 + 2, :], src[:, :, 0:T], ACT.Silu).then_inc(sem("g_evac"), 1)
                if i >= 1 and i <= 12:
                    conv_silu(act, i - 1)
            act.preload_act_table_set("natural_log_exp_and_others")
            for q in range(8):
                if q >= 4:
                    once(act, "g_ss", q - 3)
                act.activation(sq[:, 2 * (q % 4):2 * (q % 4) + 2, :], qkv[:, 2 * q:2 * q + 2, :],
                               ACT.Square).then_inc(sem("g_sq"), 1)
                if q >= 1:
                    qk_root(act, q - 1)
            qk_root(act, 7)
            for q in range(6):
                once(act, "g_tail_turned", q + 1)
                act.activation(trow[:, 512 * q:512 * q + 512], psum[0:27, q % 2, :], ACT.Copy
                               ).then_inc(sem("g_trow_ready"), 1)
            for p in range(GP):
                hh = [2 * p, 2 * p + 1]
                for s in range(2):
                    once(act, "g_bc_done", hh[s] + 1)
                    if p == 0:
                        once(act, "g_conv_out", 32)
                    act.activation(bc[:, s], psum[:, 4 * s:4 * s + 4, 0:T], ACT.Copy).then_inc(sem("g_bc"), 1)
                for s in range(2):
                    once(act, "g_tm", hh[s] + 1)
                    for c, cs in enumerate(CHUNKS):
                        last = act.activation(X[:, s, cs], PC[:, s, cs], ACT.Exp, bias=ncol[:, c, 2 * p + s:2 * p + s + 1])
                    last.then_inc(sem("g_dt"), 1)
                for l in range(1, LV):
                    for s in range(2):
                        once(act, "g_p_done", (p * LV + l) * 2 + s + 1)
                        last = act.activation(PC[:, s, 0:SEQ], psum[:, 4 * s + 2, 0:SEQ], ACT.Copy)
                        if l < 2:
                            last = act.activation(PC[0:NS, s, SEQ:T], psum[0:NS, 4 * s + 2, SEQ:T], ACT.Copy)
                        last.then_inc(sem("g_pc"), 1)
                for s in range(2):
                    once(act, "g_qg", hh[s] + 1)
                    act.activation(kq[:, s, :, 0, :], smp(qkv[:, HG + 2 * p + s, :]).rearrange("p (b t) -> p b t", b=NB),
                                   ACT.Copy)
                    act.activation(kq[:, s, :, 1, :], smp(PC[:, s, :]).rearrange("p (b t) -> p b t", b=NB),
                                   ACT.Copy).then_inc(sem("g_kq"), 1)
                for s in range(2):
                    once(act, "g_kd_turned", hh[s] + 1)
                    act.activation(KS_[s][:, 0:2, :], psum[:, 4 * s + 2, 0:SEQ].rearrange("p (c e) -> p c e", c=2), ACT.Copy)
                    act.activation(KS_[s][0:NS, 2, :], psum[0:NS, 4 * s + 2, SEQ:SEQ + P], ACT.Copy
                                   ).then_inc(sem("g_kd"), 1)
                for s in range(2):
                    once(act, "g_vn_done", hh[s] + 1)
                    act.activation(VS[s][:, 0, :], psum[:, 4 * s, 192:320], ACT.Copy)
                    act.activation(VS[s][0:NS, 2, :], psum[0:NS, 4 * s, 320:448], ACT.Copy).then_inc(sem("g_vn"), 1)
                for s in range(2):
                    once(act, "g_s1_done", hh[s] + 1)
                    act.activation(Sp[:, s, :], psum[:, 4 * s + 2, 384:512], ACT.Copy).then_inc(sem("g_s1"), 1)
                for s in range(2):
                    once(act, "g_r1_turned", hh[s] + 1)
                    act.activation(RS[s][:, 1, :], psum[:, 4 * s + 1, 256:384], ACT.Copy).then_inc(sem("g_r1"), 1)
                for s in range(2):
                    once(act, "g_vn1_done", hh[s] + 1)
                    act.activation(VS[s][:, 1, :], psum[:, 4 * s, 192:320], ACT.Copy).then_inc(sem("g_vn1"), 1)
                for s in range(2):
                    once(act, "g_o", hh[s] + 1)
                    act.activation(sq[:, s, :], qkv[:, 2 * p + s, :], ACT.Square).then_inc(sem("g_osq"), 1)
                for s in range(2):
                    once(act, "g_oss", hh[s] + 1)
                    act.activation(sq[:, 2 + s, :], psum[:, 4 * s + 2, 0:T], ACT.Ln, scale=1.0 / P,
                                   bias=eps_t[:, 0:1]).then_inc(sem("g_oln"), 1)
                    once(act, "g_oln", hh[s] + 1)
                    act.activation(sq[:, 2 + s, :], sq[:, 2 + s, :], ACT.Exp, scale=-0.5).then_inc(sem("g_or"), 1)
                for s in range(2):
                    once(act, "g_on", hh[s] + 1)
                    act.activation(xn_hi[:, 2 * p + s, :], fbuf[:, s, 1, :], ACT.Copy).then_inc(sem("g_o_hi"), 1)
            for i in range(H):
                act_split(act, u0 + 17 + i + 1)
                act_square_y(act, n, i, u0 + 17 + i)

        def act_gates(act, part):
            seq = sem("g_act_seq")
            if part == 0:
                once(act, "g_tab_in", 48)
                act.activation(gsm[:, 2:3], gsm[:, 1:2], ACT.Exp).then_inc(sem("g_alog"), 1)
                once(act, "g_abs", 1)
                act.activation(rows8(T2), rows8(T2), ACT.Exp, scale=-1.0).then_inc(seq, 1)
                act.wait_ge(seq, before("g_act_seq") + 1)
                act.activation(rows8(T3), rows8(T2), ACT.Ln, bias=ones[0:HG, 0:1]).then_inc(sem("g_lnp"), 1)
                act.activation(rows8(BETA), rows8(BETA), ACT.Exp, scale=-1.0).then_inc(sem("g_eb"), 1)
                return
            once(act, "g_gg", 1)
            act.activation(rows8(EG), rows8(GG), ACT.Exp).then_inc(seq, 1)
            act.activation(rows8(ED), rows8(ED), ACT.Exp).then_inc(seq, 1)
            act.wait_ge(seq, before("g_act_seq") + 3)
            once(act, "g_beta", 1)
            act.activation(gsm[:, 3:4], gsm[:, 2:3], ACT.Copy).then_inc(sem("g_rows"), 1)
            act.preload_act_table_set("silu_and_others")

        def conv_silu(act, i):
            once(act, "g_conv", i + 1)
            act.activation(qkv[:, 2 * i:2 * i + 2, 0:SEQ], cacc[:, i % 2, :, 0:SEQ], ACT.Silu)
            for k in range(2):
                last = act.activation(smp(qkv[:, 2 * i + k, :]).rearrange("p (b t) -> p b t", b=NB),
                                      cacc[:, i % 2, k, 3 + SEQ:CW].rearrange("p (b t) -> p b t", b=NB)[:, :, 0:NT],
                                      ACT.Silu)
            last.then_inc(sem("g_silu"), 1)

        def qk_root(act, q):
            once(act, "g_ss", q + 1)
            if q >= 2:
                once(act, "g_qk_unit", q - 1)
            e = 1 if q < 4 else 0
            act.activation(fbuf[:, q % 2], psum[:, 4 + 2 * (q % 2):6 + 2 * (q % 2), 0:T], ACT.Ln,
                           scale=float(P) if e else 1.0, bias=eps_t[:, e:e + 1]).then_inc(sem("g_qln"), 1)
            once(act, "g_qln", q + 1)
            act.activation(fbuf[:, q % 2], fbuf[:, q % 2], ACT.Exp, scale=-0.5).then_inc(sem("g_root"), 1)

        def dve_gdn(dve, n):
            gi, u0 = subs[n][2], ubase[n]
            seq, cnt = sem("g_dve_seq"), [0]

            def step(ins):
                cnt[0] += 1
                ins.then_inc(seq, 1)
                dve.wait_ge(seq, before("g_dve_seq") + cnt[0])
            dve_split(dve, u0 + 1)
            if n > 0:
                dve.wait_ge(unit_used, u0)
            for s in range(2):
                last = dve.memset(cbuf[:, s, :, 0:3], 0.0)
            dve.memset(ncol[:], 0.0)
            dve.wait_ge(unit_used, u0 + 1)
            once(dve, "g_tab_in", 48)
            dve.tensor_copy(rows8(BETA), psum[0:HG, 4, 0:T]).then_inc(sem("g_gate_read"), 1)
            dve.tensor_scalar(rows8(T1), psum[0:HG, 5, 0:T], gsm[:, 0:1], None, ALU.add).then_inc(sem("g_gate_read"), 1)
            once(dve, "g_gate_read", 2)
            step(dve.scalar_tensor_tensor(out=rows8(T2), in0=rows8(T1), scalar=-1.0, in1=rows8(T1),
                                          op0=ALU.mult, op1=ALU.max))
            dve.tensor_copy(gsm[:, 3:4], gsm[:, 0:1]).then_inc(sem("g_abs"), 1)
            once(dve, "g_hist_turned", 1)
            step(dve.tensor_copy(chist[:].rearrange("p (a k) t -> p a (k t)", a=2), psum[:, 6:8, 0:288]))
            dve.tensor_copy(chist[:, 0, 0:1], chist[:, 0, 0:1]).then_inc(sem("g_hist"), 1)
            once(dve, "g_hist", 1)
            for s in range(2):
                hist(dve, s)
            for i in range(16):
                dve_split(dve, u0 + i + 2)
                if i == 0:
                    gates(dve, step)
                if i < 12:
                    once(dve, "g_evac", i + 1)
                    if i >= 2:
                        once(dve, "g_silu", i - 1)
                    for j in range(4):
                        for k in range(2):
                            r = V_CONV + (gi * 4 + j) * 3 * HG + 2 * i + k
                            src, dst = cbuf[:, i % 2, k, j:j + CW - 3], cacc[:, i % 2, k, 0:CW - 3]
                            if j == 0:
                                last = dve.tensor_scalar(dst, src, vec[:, r:r + 1], None, ALU.mult)
                            else:
                                last = dve.scalar_tensor_tensor(out=dst, in0=src, scalar=vec[:, r:r + 1], in1=dst,
                                                                op0=ALU.mult, op1=ALU.add)
                        if j < 3:
                            step(last)
                    last.then_inc(sem("g_conv"), 1)
                    for k in range(2):
                        dve.tensor_copy(tail[:, 2 * i + k, 0:3], cbuf[:, i % 2, k, SEQ:SEQ + 3])
                        last = dve.tensor_copy(
                            tail[:, 2 * i + k, 3:27].rearrange("p (b t) -> p b t", b=NB),
                            cbuf[:, i % 2, k, 3 + SEQ:CW].rearrange("p (b t) -> p b t", b=NB)[:, :, 4:7])
                    if i + 2 < 12:
                        step(last)
                        last = hist(dve, i + 2)
                    last.then_inc(sem("g_tail"), 1)
            for q in range(8):
                once(dve, "g_root", q + 1)
                dve.tensor_tensor(qkv[:, 2 * q:2 * q + 2, :], qkv[:, 2 * q:2 * q + 2, :], fbuf[:, q % 2], ALU.mult
                                  ).then_inc(sem("g_qk_unit"), 1)
            once(dve, "g_col_turned", 1)
            dve.tensor_scalar(ncol[:, 0:2, :], psum[:, 4, 0:2 * HG].rearrange("p (c h) -> p c h", c=2), -1.0, None, ALU.mult)
            dve.tensor_scalar(ncol[0:NS, 2, :], psum[0:NS, 4, 2 * HG:3 * HG], -1.0, None, ALU.mult).then_inc(sem("g_ncol"), 1)
            id3 = ident[:, None, :].to_broadcast([P, 2, P])
            two = lambda v: v[:, 0:SEQ].rearrange("p (c i) -> p c i", c=2)
            for p in range(GP):
                hh = [2 * p, 2 * p + 1]
                for s in range(2):
                    once(dve, "g_bc", hh[s] + 1)
                    dve.tensor_tensor(PC[:, s], bc[:, s, GG, :], gt("mask"), ALU.add).then_inc(sem("g_tm"), 1)
                    step(dve.tensor_tensor(AO[:, s], bc[:, s, BETA, :], gt("strict"), ALU.mult))
                for s in range(2):
                    once(dve, "g_dt", hh[s] + 1)
                    once(dve, "g_kk", hh[s] + 1)
                    dve.tensor_tensor(AN[:, s], psum[:, 4 * s + 1, 0:T], X[:, s], ALU.mult)
                    step(dve.tensor_tensor(AO[:, s], AO[:, s], X[:, s], ALU.mult))
                    step(dve.tensor_tensor(AT[:, s], psum[:, 4 * s, 0:T], AO[:, s], ALU.mult))

                def level_blocks(l):
                    lev = gt(f"level{l}")
                    for s in range(2):
                        if l > 0:
                            once(dve, "g_p_done", (p * LV + l - 1) * 2 + s + 1)
                        if l == 1:
                            once(dve, "g_xupd", p * LV * 2 + s + 1)
                        last = dve.tensor_tensor(two(AO[:, s]), two(AT[:, s]), lev[:, None, :].to_broadcast([P, 2, P]), ALU.mult)
                        if l < 2:
                            last = dve.tensor_tensor(AO[0:NS, s, SEQ:T], AT[0:NS, s, SEQ:T], lev[0:NS, 0:NS], ALU.mult)
                        last.then_inc(sem("g_ao"), 1)
                level_blocks(0)
                for l in range(LV):
                    e = lambda s: (p * LV + l) * 2 + s + 1
                    if l > 0 and l + 1 < LV:
                        level_blocks(l + 1)
                    for s in range(2):
                        if l == 0:
                            once(dve, "g_ao", e(s))
                            dve.tensor_tensor(two(XT[:, s]), id3, two(AO[:, s]), ALU.subtract)
                            dve.tensor_tensor(XT[0:NS, s, SEQ:T], ident[0:NS, 0:NS], AO[0:NS, s, SEQ:T], ALU.subtract)
                            once(dve, "g_p_done", e(s))
                            dve.tensor_tensor(two(X[:, s]), id3, two(psum[:, 4 * s + 2, :]), ALU.subtract)
                            last = dve.tensor_tensor(X[0:NS, s, SEQ:T], ident[0:NS, 0:NS], psum[0:NS, 4 * s + 2, SEQ:T],
                                                     ALU.subtract)
                        else:
                            once(dve, "g_xp_done", (p * (LV - 1) + l - 1) * 2 + s + 1)
                            for dst, b in ((X, 0), (XT, 3)):
                                if b == 0 and l == LV - 1:
                                    continue
                                last = dve.tensor_tensor(dst[:, s, 0:SEQ], dst[:, s, 0:SEQ], psum[:, 4 * s + b, 0:SEQ],
                                                         ALU.subtract)
                                if l < 2:
                                    last = dve.tensor_tensor(dst[0:NS, s, SEQ:T], dst[0:NS, s, SEQ:T],
                                                             psum[0:NS, 4 * s + b, SEQ:T], ALU.subtract)
                        last.then_inc(sem("g_xupd"), 1)
                    if l == 0:
                        level_blocks(1)
                for s in range(2):
                    h = 2 * p + s
                    once(dve, "g_xupd", (p * LV + LV - 1) * 2 + s + 1)
                    dve.tensor_tensor(PC[:, s], qkv[:, h, :], bc[:, s, EG, :], ALU.mult).then_inc(sem("g_qg"), 1)
                    dve.tensor_tensor(AO[:, s], qkv[:, HG + h, :], bc[:, s, ED, :], ALU.mult).then_inc(sem("g_kdt"), 1)
                for s in range(2):
                    h = 2 * p + s
                    v = qkv[:, 2 * HG + h, :]
                    dve.tensor_tensor(X[:, s, CHUNKS[0]], v[:, CHUNKS[0]], bc[:, s, BETA, CHUNKS[0]], ALU.mult)
                    once(dve, "g_ks", hh[s] + 1)
                    seq3 = lambda t: smp(t).rearrange("p (b t) -> p b t", b=NB)
                    ks4 = psum[:, 4 * s, 0:64].rearrange("p (b a t) -> p b a t", b=NB, a=2)
                    step(dve.tensor_tensor(seq3(X[:, s]), ks4[:, :, 0, :], seq3(bc[:, s, EG, :]), ALU.mult))
                    step(dve.tensor_tensor(smp(X[:, s]), smp(v), smp(X[:, s]), ALU.subtract))
                    dve.tensor_tensor(smp(X[:, s]), smp(X[:, s]), smp(bc[:, s, BETA, :]), ALU.mult).then_inc(sem("g_rt"), 1)
                for s in range(2):
                    once(dve, "g_r_turned", hh[s] + 1)
                    dve.tensor_copy(RS[s][:, 0, :], psum[:, 4 * s + 1, 0:P])
                    dve.tensor_copy(RS[s][0:NS, 2, :], psum[0:NS, 4 * s + 1, P:2 * P]).then_inc(sem("g_r"), 1)
                for s in range(2):
                    once(dve, "g_kd", hh[s] + 1)
                    dve.tensor_tensor(KDBS[s], KS_[s][0:NS, 2:3, :].to_broadcast([NS, NB, P]),
                                      gt("seqcol")[:, :, None].to_broadcast([NS, NB, P]), ALU.mult).then_inc(sem("g_kdb"), 1)
                for s in range(2):
                    h = 2 * p + s
                    once(dve, "g_ks1", hh[s] + 1)
                    c1 = CHUNKS[1]
                    step(dve.tensor_tensor(X[:, s, c1], psum[:, 4 * s, 64:192], bc[:, s, EG, c1], ALU.mult))
                    step(dve.tensor_tensor(X[:, s, c1], qkv[:, 2 * HG + h, c1], X[:, s, c1], ALU.subtract))
                    dve.tensor_tensor(X[:, s, c1], X[:, s, c1], bc[:, s, BETA, c1], ALU.mult).then_inc(sem("g_rt1"), 1)
                for s in range(2):
                    h = 2 * p + s
                    once(dve, "g_o_done", hh[s] + 1)
                    ks4 = psum[:, 4 * s, 0:64].rearrange("p (b a t) -> p b a t", b=NB, a=2)
                    o = qkv[:, h, :]
                    dve.tensor_copy(o[:, 0:SEQ], psum[:, 4 * s + 3, 0:SEQ])
                    step(dve.tensor_copy(smp(o), psum[:, 4 * s + 3, SEQ:T]))
                    dve.tensor_tensor(seq3(o), seq3(o), ks4[:, :, 1, :], ALU.add).then_inc(sem("g_o"), 1)
                    dve.scalar_tensor_tensor(out=Sp[:, s, :], in0=Sp[:, s, :], scalar=bc[:, s, EG, SEQ - 1:SEQ],
                                             in1=psum[:, 4 * s + 1, 384:512], op0=ALU.mult, op1=ALU.add
                                             ).then_inc(sem("g_sp_new"), 1)
                for s in range(2):
                    once(dve, "g_or", hh[s] + 1)
                    last = dve.scalar_tensor_tensor(out=fbuf[:, s, 0, :], in0=qkv[:, 2 * p + s, :],
                                                    scalar=vec[:, V_GN + gi:V_GN + gi + 1], in1=sq[:, 2 + s, :],
                                                    op0=ALU.mult, op1=ALU.mult)
                step(last)
                for s in range(2):
                    dve.tensor_tensor(fbuf[:, s, 1, :], fbuf[:, s, 0, :], gz[:, 2 * p + s, :], ALU.mult).then_inc(sem("g_on"), 1)
                for s in range(2):
                    h = 2 * p + s
                    once(dve, "g_o_hi", hh[s] + 1)
                    dve.tensor_tensor(xn_lo[:, h, :], fbuf[:, s, 1, :], xn_hi[:, h, :].bitcast(F32), ALU.subtract
                                      ).then_inc(sem("g_o_split"), 1)
                for s in range(2):
                    once(dve, "g_ds_done", hh[s] + 1)
                    for b in range(NB):
                        e_ = SEQ + NT * b + NT - 1
                        last = dve.scalar_tensor_tensor(
                            out=Sin[:, s, b, :], in0=Sin[:, s, b, :], scalar=bc[:, s, EG, e_:e_ + 1],
                            in1=psum[:, 4 * s + b // 4, (b % 4) * P:(b % 4 + 1) * P], op0=ALU.mult, op1=ALU.add)
                    last.then_inc(sem("g_s_new"), 1)
            for i in range(H):
                dve_split(dve, u0 + 17 + i + 1)
                dve_take_y(dve, n, i)

        def gates(dve, step):
            once(dve, "g_lnp", 1)
            once(dve, "g_alog", 1)
            once(dve, "g_eb", 1)
            step(dve.scalar_tensor_tensor(out=rows8(T1), in0=rows8(T1), scalar=0.0, in1=rows8(T3),
                                          op0=ALU.max, op1=ALU.add))
            step(dve.tensor_scalar(rows8(T1), rows8(T1), gsm[:, 2:3], -1.0, ALU.mult, ALU.mult))
            step(dve.tensor_tensor_scan(rows8(GG), gt("keep"), rows8(T1), 0.0, ALU.mult, ALU.add))
            for c in range(2):
                cs = CHUNKS[c]
                dve.tensor_tensor(rows8(ED)[:, cs], rows8(GG)[:, cs.stop - 1:cs.stop].to_broadcast([HG, CH]),
                                  rows8(GG)[:, cs], ALU.subtract)
            g4 = smp(rows8(GG)).rearrange("p (b t) -> p b t", b=NB)
            dve.tensor_tensor(smp(rows8(ED)).rearrange("p (b t) -> p b t", b=NB),
                              g4[:, :, NT - 1:NT].to_broadcast([HG, NB, NT]), g4, ALU.subtract).then_inc(sem("g_gg"), 1)
            step(dve.tensor_scalar(rows8(BETA), rows8(BETA), 1.0, None, ALU.add))
            dve.reciprocal(rows8(BETA), rows8(BETA)).then_inc(sem("g_beta"), 1)

        def hist(dve, i):
            for k in range(2):
                last = dve.tensor_copy(cbuf[:, i % 2, k, 3 + SEQ:CW].rearrange("p (b t) -> p b t", b=NB)[:, :, 0:3],
                                       chist[:, 2 * i + k, :].rearrange("p (b t) -> p b t", b=NB))
            if i < 2:
                last.then_inc(sem("g_cbuf_half"), 1)
                if i == 1:
                    once(dve, "g_cbuf_half", 2)
                    dve.memset(cbuf[:, 1, 1, 0:3], 0.0).then_inc(sem("g_cbuf_set"), 1)
            return last
        SP["gdn"], PE["gdn"], ACTE["gdn"], DVE["gdn"] = sp_gdn, pe_gdn, act_gdn, dve_gdn

        if any(q[0] == "mlstm" for q in subs):
            w[0] = 0
            LC = 256
            lkq = carve("l_kq", [P, 2 * LH, T])
            lv = carve("l_v", [P, 3, LH * LC])
            lo = carve("l_o", [P, 2 * LH, T])
            ltab = carve("l_tab", [P, TAB["c_mlstm"][0].shape[1]])
            lbc = carve("l_bc", [P, 2, 4, T])
            Cin = carve("l_c", [P, 2, NB, LC])
            Cp = carve("l_cp", [P, 2, LC])
            WS, ST = carve("l_w", [P, 2, 416]), carve("l_st", [P, 2, 416])
            LKD = carve("l_kd", [P, 2, 3, P])
            kdT, den = carve("l_kdt", [P, 2, T]), carve("l_den", [P, 2, T])
            nrow, n0 = carve("l_nrow", [NB * LH, P]), carve("l_n0", [P, NB, LH])
            nall, nout = carve("l_nall", [P, LH + NB * LH]), carve("l_nout", [LH + NB * LH, P])
            qw, qn = carve("l_qw", [P, 2, NS]), carve("l_qn", [P, 2, NS])
            acol = carve("l_acol", [P, 3, LH])
            gb = carve("l_gb", [LH, 2])
            m0, mnew = carve("l_m0", [LH, NB]), carve("l_mnew", [LH, 1 + NB])
            ncar = carve("l_ncar", [P, 2, NB])

        def lt(name):
            o, _, r = table["c_mlstm"][name]
            n_ = table["c_mlstm"][name][1]
            return ltab[0:r, o:o + n_]
        rows4 = lambda r: y[0:LH, r, :]
        LM, LWI, LEM, LWJ, LI, LB, LA, LMT = range(8)
        tmp4 = lambda r: fbuf[0:LH, r // 2, r % 2, :]
        sq3 = lambda v: smp(v).rearrange("p (b t) -> p b t", b=NB)
        LP = LH // 2
        BL = lambda s, b: psum[:, 4 * s + b, :]

        def sp_mlstm(sp, n):
            g, u0 = subs[n][2], ubase[n]
            if n > 0:
                once(sp, "unit_used", u0)
            sp.dma_start(ltab[:], a["c_mlstm"]).then_inc(sem("l_tab_in"), 16)
            sp.dma_start(gb[:, 0:1], a["mlstm_i_bias"][g].rearrange("(h o) -> h o", o=1)).then_inc(sem("l_tab_in"), 16)
            sp.dma_start(gb[:, 1:2], a["mlstm_f_bias"][g].rearrange("(h o) -> h o", o=1)).then_inc(sem("l_tab_in"), 16)
            with nc.allow_non_contiguous_dma(reason="32 stabilisers"):
                sp.dma_start(m0[:], a["state_mlstm_m"][g].rearrange("b h -> h b")).then_inc(sem("l_tab_in"), 16)
            sp.dma_start(nrow[:], a["state_mlstm_n"][g].rearrange("b h d -> (b h) d")).then_inc(sem("l_tab_in"), 16)
            for u in range(u0, u0 + 13):
                sp_unit(sp, u)
            out = 0
            for h in range(LH + 2):
                if h >= 2:
                    once(sp, "l_c_new", h - 1)
                    sp.dma_start(a["ml_C_s"][g, :, h - 2].rearrange("b d e -> d b e"), Cin[:, h % 2]
                                 ).then_inc(sem(f"l_c_out{h % 2}"), 16)
                    sp.dma_start(a["ml_C_p"][g, 0, h - 2], Cp[:, h % 2]).then_inc(sem(f"l_c_out{h % 2}"), 16)
                    once(sp, f"l_c_out{h % 2}", 32 * (h // 2))
                if h < LH:
                    sp.dma_start(Cin[:, h % 2], a["state_mlstm_C"][g, :, h].rearrange("b d e -> d b e")
                                 ).then_inc(sem(f"l_c_in{h % 2}"), 16)
                if h == 1:
                    for u in range(u0 + 13, uend[n]):
                        sp_unit(sp, u)
            once(sp, "l_m_new", 1)
            sp.dma_start(a["ml_m_p"][g, 0].rearrange("(h o) -> h o", o=1), mnew[:, 0:1]).then_inc(sem("l_rows_out"), 16)
            with nc.allow_non_contiguous_dma(reason="32 stabilisers"):
                sp.dma_start(a["ml_m_s"][g].rearrange("b h -> h b"), mnew[:, 1:]).then_inc(sem("l_rows_out"), 16)
            once(sp, "l_n_out", 1)
            sp.dma_start(a["ml_n_p"][g, 0], nout[0:LH, :]).then_inc(sem("l_rows_out"), 16)
            sp.dma_start(a["ml_n_s"][g].rearrange("b h d -> (b h) d"), nout[LH:, :]).then_inc(sem("l_rows_out"), 16)
            once(sp, "l_rows_out", 64)

        def pe_mlstm(pe, n):
            u0 = ubase[n]
            gates = [psum[0:LH, 4, 0:T], psum[0:LH, 5, 0:T]]
            pe.wait_ge(lo_ready, u0 + 1)
            wh, wl = wview(w_hi[u0 % NSPL], u0), wview(w_lo[u0 % NSPL], u0)
            ready = x_chunks(pe, n)
            for m in range(2):
                for k in range(KC):
                    if m == 0:
                        ready(k)
                    c = slice(m * LH, (m + 1) * LH)
                    pe.matmul(gates[m], wh[:, k, c], xn_hi[:, k, :], start=k == 0, stop=False)
                    pe.matmul(gates[m], wh[:, k, c], xn_lo[:, k, :], start=False, stop=False)
                    last = pe.matmul(gates[m], wl[:, k, c], xn_hi[:, k, :], start=False, stop=k == KC - 1)
            last.then_inc(unit_used, 1)
            once(pe, "l_tab_in", 80)
            pe.transpose(psum[:, 6, 0:NB * LH], nrow[:], ident[0:NB * LH, 0:NB * LH]).then_inc(sem("l_n_turned"), 1)
            for i in range(12):
                if i >= 2:
                    once(pe, "l_evac", i - 1)
                u, b = u0 + 1 + i, 2 * (i % 2)
                if not 4 <= i < 8:
                    pe_unit(pe, u, [psum[:, b, 0:T], psum[:, b + 1, 0:T]], xn(xn_hi), xn(xn_lo), True, True)
                    continue
                pe.wait_ge(lo_ready, u + 1)
                wh, wl = wview(w_hi[u % NSPL], u), wview(w_lo[u % NSPL], u)
                for t, (cols, _, _) in enumerate(token_tiles):
                    out = psum[0:cols.stop - cols.start, b + t // 2, (t % 2) * LC:(t % 2 + 1) * LC]
                    for k in range(KC):
                        pe.matmul(out, xn_hi[:, k, cols], wh[:, k, :], start=k == 0, stop=False)
                        pe.matmul(out, xn_hi[:, k, cols], wl[:, k, :], start=False, stop=False)
                        last = pe.matmul(out, xn_lo[:, k, cols], wh[:, k, :], start=False, stop=k == KC - 1)
                last.then_inc(unit_used, 1)
            once(pe, "l_rows", 1)
            for t, (cols, _, _) in enumerate(token_tiles):
                last = pe.transpose(psum[0:cols.stop - cols.start, 6, 64 + t * LH:64 + (t + 1) * LH],
                                    rows4(LA)[:, cols], ident[0:LH, 0:LH])
            last.then_inc(sem("l_col_turned"), 1)
            once(pe, "l_evac", 12)
            once(pe, "l_acol", 1)
            flat = lkq[:].rearrange("p k t -> p (k t)")
            for p in range(LP):
                for s in range(2):
                    h = 2 * p + s
                    if p > 0:
                        once(pe, "l_c_new", h - 1)
                    for r in range(4):
                        last = pe.matmul(BL(s, r)[:, 0:T], lt("select")[0:LH, h * P:(h + 1) * P], rows4(r),
                                         start=True, stop=True)
                    last.then_inc(sem("l_bc_done"), 1)
                for s in range(2):
                    h = 2 * p + s
                    once(pe, "l_bc", h + 1)
                    k0, q0 = h * T, (LH + h) * T
                    pe.matmul(BL(s, 0)[:, 0:SEQ], flat[:, k0:k0 + P], flat[:, q0:q0 + SEQ], start=True, stop=True)
                    pe.matmul(BL(s, 0)[:, SEQ:384], flat[:, k0 + P:k0 + SEQ], flat[:, q0 + P:q0 + SEQ], start=True,
                              stop=True)
                    pe.matmul(BL(s, 0)[:, 384:416], flat[:, k0 + SEQ:k0 + SEQ + P], flat[:, q0 + SEQ:q0 + T],
                              start=True, stop=True).then_inc(sem("l_kk"), 1)
                for s in range(2):
                    h = 2 * p + s
                    once(pe, "l_st", h + 1)
                    once(pe, "l_qn", h + 1)
                    once(pe, f"l_c_in{s}", 16 * (p + 1))
                    for e in range(3):
                        val = lambda t: lv[:, t, h * LC + e * P:h * LC + (e + 1) * P] if e < 2 else ones
                        out = BL(s, 1 + e)
                        pe.matmul(out[:, SEQ:T], val(2)[0:NS], ST[0:NS, s, 384:416], start=True, stop=False)
                        if e < 2:
                            for b in range(NB):
                                cs = slice(SEQ + NT * b, SEQ + NT * (b + 1))
                                pe.matmul(out[:, cs], Cin[:, s, b, e * P:(e + 1) * P], qw[:, s, NT * b:NT * (b + 1)],
                                          start=False, stop=b == NB - 1)
                        else:
                            pe.matmul(out[:, SEQ:T], ones, qn[:, s, :], start=False, stop=True)
                        pe.matmul(out[:, 0:SEQ], val(0), ST[:, s, 0:SEQ], start=True, stop=False)
                        last = pe.matmul(out[:, P:SEQ], val(1), ST[:, s, SEQ:384], start=False, stop=True)
                    last.then_inc(sem("l_num"), 1)
                for s in range(2):
                    h = 2 * p + s
                    once(pe, "l_kdt", h + 1)
                    for t, (cols, _, _) in enumerate(token_tiles):
                        last = pe.transpose(BL(s, 0)[0:cols.stop - cols.start, t * P:(t + 1) * P], kdT[:, s, cols], ident)
                    last.then_inc(sem("l_kd_turned"), 1)
                for s in range(2):
                    h = 2 * p + s
                    once(pe, "l_kd", h + 1)
                    for t in range(2):
                        last = pe.matmul(BL(s, 0)[:, 0:LC], LKD[:, s, t, :], lv[:, t, h * LC:(h + 1) * LC],
                                         start=t == 0, stop=t == 1)
                    last.then_inc(sem("l_cp_done"), 1)
                for s in range(2):
                    h = 2 * p + s
                    once(pe, "l_kdb", h + 1)
                    once(pe, "l_cp", h + 1)
                    once(pe, "l_h", h + 1)
                    for b in range(NB):
                        last = pe.matmul(BL(s, b // 2)[:, (b % 2) * LC:(b % 2 + 1) * LC], KDB[:, b, :],
                                         lv[0:NS, 2, h * LC:(h + 1) * LC], start=True, stop=True)
                    last.then_inc(sem("l_dc_done"), 1)
            once(pe, "l_nall", LH)
            once(pe, "l_c_new", LH)
            pe.transpose(psum[0:LH + NB * LH, 7, 0:P], nall[:], ident).then_inc(sem("l_n_turned"), 1)
            once(pe, "l_o_split", LH)
            once(pe, "l_n_out", 1)
            pe_out(pe, n, u0 + 13, xn(xn_hi), xn(xn_lo), None)

        def act_mlstm(act, n):
            u0 = ubase[n]
            seq = sem("l_act_seq")
            act_split(act, u0 + 1)
            for i in range(12):
                act_split(act, u0 + i + 2)
                act.wait_ge(unit_used, u0 + i + 2)
                b = 2 * (i % 2)
                if i < 2:
                    act.activation(lkq[:, LH + 2 * i:LH + 2 * i + 2, :], psum[:, b:b + 2, 0:T], ACT.Copy,
                                   scale=P ** -0.5).then_inc(sem("l_evac"), 1)
                elif i < 4:
                    act.activation(lkq[:, 2 * i - 4:2 * i - 2, :], psum[:, b:b + 2, 0:T], ACT.Copy).then_inc(sem("l_evac"), 1)
                elif i < 8:
                    c = slice((i - 4) * LC, (i - 3) * LC)
                    act.activation(lv[:, 0:2, c], psum[:, b, :].rearrange("p (t e) -> p t e", t=2), ACT.Copy)
                    act.activation(lv[0:NS, 2, c], psum[0:NS, b + 1, 0:LC], ACT.Copy).then_inc(sem("l_evac"), 1)
                else:
                    act.activation(lo[:, 2 * i - 16:2 * i - 14, :], psum[:, b:b + 2, 0:T], ACT.Exp,
                                   scale=-1.0).then_inc(sem("l_evac"), 1)
                if i == 1:
                    once(act, "l_abs", 1)
                    act.activation(tmp4(1), tmp4(1), ACT.Exp, scale=-1.0).then_inc(seq, 1)
                    act.wait_ge(seq, before("l_act_seq") + 1)
                    act.activation(tmp4(2), tmp4(1), ACT.Ln, bias=ones[0:LH, 0:1]).then_inc(sem("l_lnp"), 1)
            once(act, "l_pre_rows", 1)
            act.activation(rows4(LWI), rows4(LWI), ACT.Exp)
            act.activation(rows4(LEM), rows4(LMT), ACT.Exp, scale=-1.0)
            act.activation(rows4(LWJ), rows4(LWJ), ACT.Exp).then_inc(sem("l_rows"), 1)
            for p in range(LP):
                for s in range(2):
                    h = 2 * p + s
                    once(act, "l_bc_done", h + 1)
                    act.activation(lbc[:, s], psum[:, 4 * s:4 * s + 4, 0:T], ACT.Copy).then_inc(sem("l_bc"), 1)
                for s in range(2):
                    h = 2 * p + s
                    once(act, "l_tm", h + 1)
                    for t, cs in enumerate((slice(0, SEQ), slice(SEQ, 384), slice(384, 416))):
                        last = act.activation(WS[:, s, cs], WS[:, s, cs], ACT.Exp, bias=acol[:, t, h:h + 1])
                    last.then_inc(sem("l_w_ready"), 1)
                for s in range(2):
                    h = 2 * p + s
                    once(act, "l_num", h + 1)
                    act.activation(den[:, s, :], BL(s, 3)[:, 0:T], ACT.Abs).then_inc(sem("l_den"), 1)
                for s in range(2):
                    h = 2 * p + s
                    once(act, "l_kd_turned", h + 1)
                    act.activation(LKD[:, s, 0:2, :], BL(s, 0)[:, 0:SEQ].rearrange("p (c e) -> p c e", c=2), ACT.Copy)
                    act.activation(LKD[0:NS, s, 2, :], BL(s, 0)[0:NS, SEQ:SEQ + P], ACT.Copy).then_inc(sem("l_kd"), 1)
                for s in range(2):
                    h = 2 * p + s
                    once(act, "l_cp_done", h + 1)
                    act.activation(Cp[:, s, :], BL(s, 0)[:, 0:LC], ACT.Copy).then_inc(sem("l_cp"), 1)
                for s in range(2):
                    h = 2 * p + s
                    once(act, "l_h", h + 1)
                    act.activation(xn_hi[:, 2 * h:2 * h + 2, :], fbuf[:, s], ACT.Copy).then_inc(sem("l_o_hi"), 1)
            once(act, "l_n_turned", 2)
            act.activation(nout[:], psum[0:LH + NB * LH, 7, 0:P], ACT.Copy).then_inc(sem("l_n_out"), 1)
            for i in range(H):
                act_split(act, u0 + 13 + i + 1)
                act_square_y(act, n, i, u0 + 13 + i)

        def dve_mlstm(dve, n):
            u0 = ubase[n]
            seq, cnt = sem("l_dve_seq"), [0]

            def step(ins):
                cnt[0] += 1
                ins.then_inc(seq, 1)
                dve.wait_ge(seq, before("l_dve_seq") + cnt[0])
            dve_split(dve, u0 + 1)
            if n > 0:
                dve.wait_ge(unit_used, u0)
            dve.memset(acol[:], 0.0)
            once(dve, "xlo_ready", H * (n + 1))
            dve.wait_ge(unit_used, u0 + 1)
            once(dve, "l_tab_in", 80)
            dve.tensor_scalar(rows4(LI), psum[0:LH, 4, 0:T], gb[:, 0:1], None, ALU.add)
            step(dve.tensor_scalar(tmp4(0), psum[0:LH, 5, 0:T], gb[:, 1:2], None, ALU.add))
            dve.scalar_tensor_tensor(out=tmp4(1), in0=tmp4(0), scalar=-1.0, in1=tmp4(0), op0=ALU.mult,
                                     op1=ALU.max).then_inc(sem("l_abs"), 1)
            once(dve, "l_n_turned", 1)
            step(dve.tensor_copy(n0[:].rearrange("p b h -> p (b h)"), psum[:, 6, 0:NB * LH]))
            for i in range(12):
                dve_split(dve, u0 + i + 2)
                if i == 1:
                    once(dve, "l_lnp", 1)
                    step(dve.scalar_tensor_tensor(out=tmp4(3), in0=tmp4(0), scalar=0.0, in1=tmp4(2), op0=ALU.min,
                                                  op1=ALU.subtract))
                    step(dve.tensor_tensor_scan(rows4(LB), lt("keep")[0:LH], tmp4(3), 0.0, ALU.mult, ALU.add))
                    step(dve.tensor_tensor(rows4(LA), rows4(LI), rows4(LB), ALU.subtract))
                    step(dve.tensor_copy(tmp4(3), rows4(LA)))
                    dve.tensor_scalar(tmp4(3)[:, 0:1], tmp4(3)[:, 0:1], 0.0, None, ALU.max)
                    step(dve.tensor_tensor(sq3(tmp4(3))[:, :, 0], sq3(tmp4(3))[:, :, 0], m0[:], ALU.max))
                    step(dve.tensor_tensor_scan(rows4(LM), lt("drop")[0:LH], tmp4(3), 0.0, ALU.add, ALU.max))
                    step(dve.tensor_tensor(rows4(LMT), rows4(LB), rows4(LM), ALU.add))
                    dve.tensor_copy(mnew[:, 0:1], rows4(LMT)[:, SEQ - 1:SEQ])
                    dve.tensor_copy(mnew[:, 1:], sq3(rows4(LMT))[:, :, NT - 1]).then_inc(sem("l_m_new"), 1)
                    dve.tensor_scalar(rows4(LWI)[:, 0:SEQ], rows4(LM)[:, 0:SEQ], -1.0, None, ALU.mult)
                    dve.tensor_tensor(sq3(rows4(LWI)), m0[:, :, None].to_broadcast([LH, NB, NT]), sq3(rows4(LM)), ALU.subtract)
                    dve.tensor_tensor(rows4(LWJ)[:, 0:SEQ], rows4(LA)[:, 0:SEQ],
                                      rows4(LM)[:, SEQ - 1:SEQ].to_broadcast([LH, SEQ]), ALU.subtract)
                    dve.tensor_tensor(sq3(rows4(LWJ)), sq3(rows4(LA)),
                                      sq3(rows4(LM))[:, :, NT - 1:NT].to_broadcast([LH, NB, NT]), ALU.subtract
                                      ).then_inc(sem("l_pre_rows"), 1)
                if i >= 9:
                    gate(dve, i - 9)
            gate(dve, 3)
            once(dve, "l_col_turned", 1)
            dve.tensor_copy(acol[:, 0:2, :], psum[:, 6, 64:64 + 2 * LH].rearrange("p (c h) -> p c h", c=2))
            dve.tensor_copy(acol[0:NS, 2, :], psum[0:NS, 6, 64 + 2 * LH:64 + 3 * LH]).then_inc(sem("l_acol"), 1)
            for p in range(LP):
                for s in range(2):
                    h = 2 * p + s
                    once(dve, "l_bc", h + 1)
                    if p > 0:
                        once(dve, "l_st", h - 1)
                    dve.tensor_tensor(WS[:, s, 0:SEQ], lt("mask")[:, 0:SEQ], lbc[:, s, LM, 0:SEQ], ALU.subtract)
                    dve.tensor_tensor(WS[:, s, SEQ:416], lt("mask")[:, SEQ:416], lbc[:, s, LM, P:T], ALU.subtract
                                      ).then_inc(sem("l_tm"), 1)
                    step(dve.tensor_tensor(qw[:, s, :], smp(lkq[:, LH + h, :]), smp(lbc[:, s, LWI, :]), ALU.mult))
                    qn3 = lambda v: v.rearrange("p (b t) -> p b t", b=NB)
                    dve.tensor_tensor(qn3(qn[:, s, :]), qn3(qw[:, s, :]), n0[:, :, h:h + 1].to_broadcast([P, NB, NT]),
                                      ALU.mult).then_inc(sem("l_qn"), 1)
                for s in range(2):
                    h = 2 * p + s
                    once(dve, "l_w_ready", h + 1)
                    once(dve, "l_kk", h + 1)
                    dve.tensor_tensor(ST[:, s, :], BL(s, 0)[:, 0:416], WS[:, s, :], ALU.mult).then_inc(sem("l_st"), 1)
                    dve.tensor_tensor(kdT[:, s, :], lkq[:, h, :], lbc[:, s, LWJ, :], ALU.mult).then_inc(sem("l_kdt"), 1)
                for s in range(2):
                    h = 2 * p + s
                    once(dve, "l_kdt", h + 1)
                    dve.tensor_reduce(nall[:, h:h + 1], kdT[:, s, 0:SEQ], AX.X, ALU.add)
                    step(dve.tensor_reduce(ncar[:, 0, :], sq3(kdT[:, s, :]), AX.X, ALU.add))
                    step(dve.tensor_tensor(ncar[:, 1, :], n0[:, :, h], sq3(lbc[:, s, LWI, :])[:, :, NT - 1], ALU.mult))
                    dve.tensor_tensor(nall[:, LH:].rearrange("p (b h) -> p b h", b=NB)[:, :, h], ncar[:, 0, :],
                                      ncar[:, 1, :], ALU.add).then_inc(sem("l_nall"), 1)
                    once(dve, "l_nall", h + 1)
                for s in range(2):
                    h = 2 * p + s
                    once(dve, "l_den", h + 1)
                    step(dve.tensor_tensor(den[:, s, :], den[:, s, :], lbc[:, s, LEM, :], ALU.max))
                    step(dve.reciprocal(den[:, s, :], den[:, s, :]))
                    if p > 0:
                        once(dve, "l_o_split", h - 1)
                    for e in range(2):
                        last = dve.tensor_tensor(fbuf[:, s, e, :], BL(s, 1 + e)[:, 0:T], den[:, s, :], ALU.mult)
                    step(last)
                    dve.tensor_tensor(fbuf[:, s], fbuf[:, s], lo[:, 2 * h:2 * h + 2, :], ALU.mult).then_inc(sem("l_h"), 1)
                for s in range(2):
                    h = 2 * p + s
                    once(dve, "l_kd", h + 1)
                    if h > 0:
                        once(dve, "l_dc_done", h)
                    dve.tensor_tensor(KDB, LKD[0:NS, s, 2:3, :].to_broadcast([NS, NB, P]),
                                      lt("seqcol")[:, :, None].to_broadcast([NS, NB, P]), ALU.mult).then_inc(sem("l_kdb"), 1)
                for s in range(2):
                    h = 2 * p + s
                    once(dve, "l_dc_done", h + 1)
                    once(dve, "l_cp", h + 1)
                    for b in range(NB):
                        e_ = SEQ + NT * b + NT - 1
                        last = dve.scalar_tensor_tensor(
                            out=Cin[:, s, b, :], in0=Cin[:, s, b, :], scalar=lbc[:, s, LWI, e_:e_ + 1],
                            in1=BL(s, b // 2)[:, (b % 2) * LC:(b % 2 + 1) * LC], op0=ALU.mult, op1=ALU.add)
                    last.then_inc(sem("l_c_new"), 1)
                for s in range(2):
                    h = 2 * p + s
                    once(dve, "l_o_hi", h + 1)
                    dve.tensor_tensor(xn_lo[:, 2 * h:2 * h + 2, :], fbuf[:, s],
                                      xn_hi[:, 2 * h:2 * h + 2, :].bitcast(F32), ALU.subtract).then_inc(sem("l_o_split"), 1)
            for i in range(H):
                dve_split(dve, u0 + 13 + i + 1)
                dve_take_y(dve, n, i)

        def gate(dve, i):
            o2 = lo[:, 2 * i:2 * i + 2, :]
            once(dve, "l_evac", 9 + i)
            dve.tensor_scalar(o2, o2, 1.0, None, ALU.add).then_inc(sem("l_gate_sum"), 1)
            once(dve, "l_gate_sum", i + 1)
            dve.reciprocal(o2, o2)
        SP["mlstm"], PE["mlstm"], ACTE["mlstm"], DVE["mlstm"] = sp_mlstm, pe_mlstm, act_mlstm, dve_mlstm

        if any(q[0] == "mla" for q in subs):
            w[0] = 0
            atab = carve("a_tab", [P, TAB["c_mla"][0].shape[1]])
            wkv = carve("a_wkv", [P, 2, MH * 256])
            ckvT = carve("a_ckvt", [P, 2, T])
            ctok, krtok = carve("a_ctok", [P, 3, KVR]), carve("a_krtok", [P, 3, ROPE])
            QL = carve("a_ql", [P, 2, NB, MH, NT])
            QRS = carve("a_qrs", [ROPE, NB, MH, NT])
            OL = carve("a_ol", [P, 2, NB, MH, NT])
            krT = carve("a_krt", [ROPE, T])
            pages = nc.alloc_sbuf_tensor_at("a_pages", [1, NB * NP], I32, offset=free_at + 4 * w[0])
            w[0] += NB * NP
            stat = carve("a_stat", [P, 2, 8])
            w2 = w[0]
            WkT = carve("a_wkt", [P, MH, KVR])
            qnT = carve("a_qn", [P, MH, T])
            qrT = carve("a_qr", [ROPE, MH, T])
            kT = carve("a_kt", [P, MH, SEQ])
            vP = carve("a_v", [P, 2, MH * P])
            krr = y[0:ROPE, 5:7, :]
            qrr = sq[0:ROPE, 0:4, :].rearrange("p (i j) t -> p i j t", i=2)
            yflat = y[:].rearrange("p k t -> p (k t)")
            pm = yflat[:, 0:768].rearrange("p (s k) -> p s k", s=2)
            pT = yflat[:, 768:1536].rearrange("p (s k) -> p s k", s=2)
            cq_hi = nc.alloc_sbuf_tensor_at("a_cqh", [P, 3, T], F32R, offset=free_at + 4 * w[0])
            w[0] += 3 * T
            cq_lo = nc.alloc_sbuf_tensor_at("a_cql", [P, 3, T], F32R, offset=free_at + 4 * w[0])
            w[0] += 3 * T
            assert w[0] <= mix_words, (w[0], mix_words)
            w3 = w[0] - 6 * T
            w[0] = w2
            latT = carve("a_latt", [P, 2, 2, 512])
            ropT = carve("a_ropt", [ROPE, 2, 512])
            rop3 = carve("a_rop3", [P, NP, ROPE])
            OLt = carve("a_olt", [NS, NB, KVR])
            w[0] = w3
            ropes = [carve(f"a_rop{s}", [P, NP, ROPE]) for s in range(3)] + [rop3]
            assert w[0] <= mix_words
            hb = (ubase[[q[0] for q in subs].index("mla")] + 7) % NSPL
            page_bufs = [raw[0:2], raw[2:4]] + [[w_hi[(hb + i) % 2].bitcast(F32), w_lo[(hb + i) % 2].bitcast(F32)]
                                                for i in range(2)]
        LSLOTS = 4

        def page_at(s, j):
            half, jj = j if isinstance(j, tuple) else (j // 8, j % 8)
            v = page_bufs[s][half][:].rearrange("p (j r) -> p j r", r=KVR)
            return v[:, jj, :] if isinstance(jj, int) else v[:, bass.ds(jj, 1), :]
        craw = y[:, 0:5, :]
        sc = [v[0:NS].rearrange("p k t -> p (k t)") for v in (y, sq)]
        spT = fbuf[:].rearrange("p a b t -> p (a b t)")[:, 0:2 * (512 + NS)].rearrange("p (s k) -> p s k", s=2)
        NK = PAST + NS

        def at_(name):
            o, n_, r = table["c_mla"][name]
            return atab[0:r, o:o + n_]
        bt = lambda v: v.rearrange("p (b t) -> p b t", b=NB)

        def sp_mla(sp, n):
            g, u0 = subs[n][2], ubase[n]
            if n > 0:
                once(sp, "unit_used", u0)
            sp.dma_start(atab[:], a["c_mla"]).then_inc(sem("a_tab_in"), 16)
            sp.dma_start(wkv[:], a["mla_w_ukv"][g].rearrange("(k p) n -> p k n", p=P)).then_inc(sem("a_tab_in"), 16)
            sp.dma_start(pages[:], a["page_table"].rearrange("(o b) n -> o (b n)", o=1)).then_inc(sem("a_pages_in"), 16)
            for u in range(u0, u0 + 7):
                sp_unit(sp, u)
            once(sp, "a_pages_in", 16)
            for b in range(NB):
                if b == 0:
                    sp.wait_ge(lo_ready, u0 + 7)
                elif b == 2:
                    sp.wait_ge(unit_used, u0 + 7)
                elif b >= LSLOTS:
                    once(sp, "a_spv_done", b - 3)
                for half in range(2):
                    with sp.Fori(0, NP // 8) as q:
                        for j in range(4):
                            page = sp.value_load(pages[0:1, bass.ds(4 * q + (b * NP + half * 8 + j), 1)], min_val=0,
                                                 max_val=N_PHYS - 1)
                            sp.dma_start(page_at(b % LSLOTS, (half, 4 * q + j)),
                                         a["cache_mla_latent"][g, bass.ds(page, 1)].rearrange("o p r -> p o r")
                                         ).then_inc(sem(f"a_lat_in{b % LSLOTS}"), 16)
                if b == 1:
                    tokens_out(sp, g)
            for u in range(u0 + 7, uend[n]):
                once(sp, "a_spv_done", 5 + u % NRAW // 2)
                sp_unit(sp, u)
            once(sp, "a_tok_out", 96)

        def tokens_out(sp, g):
            once(sp, "a_tok", 1)
            for t in range(2):
                sp.dma_start(a["mla_lat_p"][g, t], ctok[:, t, :]).then_inc(sem("a_tok_out"), 16)
                sp.dma_start(a["mla_rope_p"][g, t], krtok[:, t, :]).then_inc(sem("a_tok_out"), 16)
            sp.dma_start(a["mla_lat_s"][g].rearrange("b t r -> (b t) r"), ctok[0:NS, 2, :]).then_inc(sem("a_tok_out"), 16)
            sp.dma_start(a["mla_rope_s"][g].rearrange("b t r -> (b t) r"), krtok[0:NS, 2, :]).then_inc(sem("a_tok_out"), 16)

        def pool_mla(pool, n):
            g, u0 = subs[n][2], ubase[n]
            once(pool, "a_pages_in", 16)
            pool.wait_ge(unit_used, u0 + 7)
            for b in range(NB):
                if b == LSLOTS - 1:
                    once(pool, "a_pv_done", MH)
                elif b >= LSLOTS:
                    once(pool, "a_lat_turned", 4 * (b - 3))
                with pool.Fori(0, NP // 4) as q:
                    for j in range(4):
                        page = pool.value_load(pages[0:1, bass.ds(4 * q + (b * NP + j), 1)], min_val=0,
                                               max_val=N_PHYS - 1)
                        pool.dma_start(ropes[b % LSLOTS][:, bass.ds(4 * q + j, 1), :],
                                       a["cache_mla_rope"][g, bass.ds(page, 1)].rearrange("o p r -> p o r")
                                       ).then_inc(sem(f"rope_in{b % LSLOTS}"), 16)

        def pe_mla(pe, n):
            u0 = ubase[n]
            ready = x_chunks(pe, n)
            for i in range(3):
                m2 = P if i < 2 else ROPE
                pe_unit(pe, u0 + i, [psum[:, 2 * i, 0:T], psum[0:m2, 2 * i + 1, 0:T]], xn(xn_hi), xn(xn_lo),
                        True, True, ready=ready if i == 0 else None)
            once(pe, "a_tab_in", 32)
            for q in range(4):
                if q >= 2:
                    once(pe, "a_wkt", q - 1)
                for j in range(4):
                    h, rc = 2 * q + j // 2, j % 2
                    last = pe.transpose(psum[:, 6 + q % 2, j * P:(j + 1) * P], wkv[:, rc, h * 256:h * 256 + P], ident)
                last.then_inc(sem("a_wk_turned"), 1)
            once(pe, "a_csq", 2)
            once(pe, "a_craw", 3)
            for k in range(5):
                last = pe.matmul(psum[:, k // 3, 0:T], ones, sq[:, k, :], start=k in (0, 3), stop=k in (2, 4))
            last.then_inc(sem("a_css"), 1)
            pe.matmul(psum[0:ROPE, 2, 0:T], at_("rot"), krr[:, 0, :], start=True, stop=True).then_inc(sem("a_krot"), 1)
            once(pe, "a_cq_split", 1)
            once(pe, "a_kr", 1)
            for i in range(4):
                b = 4 * (i % 2)
                u = u0 + 3 + i
                if i >= 2:
                    once(pe, "a_q", i - 1)
                elif i == 1:
                    once(pe, "a_wkt", 4)
                pe.wait_ge(lo_ready, u + 1)
                wh, wl = wview(w_hi[u % NSPL], u), wview(w_lo[u % NSPL], u)
                for j, (c0, m) in enumerate(((0, P), (P, ROPE), (192, P), (192 + P, ROPE))):
                    out = psum[0:m, b + j, 0:T]
                    for k in range(3):
                        c = slice(c0, c0 + m)
                        pe.matmul(out, wh[:, k, c], cq_hi[:, k, :], start=k == 0, stop=False)
                        pe.matmul(out, wh[:, k, c], cq_lo[:, k, :], start=False, stop=False)
                        last = pe.matmul(out, wl[:, k, c], cq_hi[:, k, :], start=False, stop=k == 2)
                last.then_inc(unit_used, 1)
                once(pe, "a_q_evac", i + 1)
                for j in range(2):
                    last = pe.matmul(psum[0:ROPE, b + 2 * j, 0:T], at_("rot"), qrr[:, i % 2, j, :], start=True, stop=True)
                last.then_inc(sem("a_qrot"), 1)
            once(pe, "a_q", 4)
            once(pe, "a_ckv", 1)
            for q in range(4):
                for j in range(2):
                    for k in range(2):
                        h = 2 * q + j
                        last = pe.matmul(psum[:, q, j * SEQ:(j + 1) * SEQ], wkv[:, k, h * 256:h * 256 + P],
                                         ckvT[:, k, 0:SEQ], start=k == 0, stop=k == 1)
                last.then_inc(sem("a_k_done"), 1)
            v4 = wkv[:].rearrange("p k (h c e) -> p k h c e", h=MH, c=2)
            for q in range(4):
                for k in range(2):
                    last = pe.matmul(psum[:, 4 + q, :], ckvT[:, k, (q // 2) * P:(q // 2 + 1) * P],
                                     v4[:, k, 4 * (q % 2):4 * (q % 2) + 4, 1, :], start=k == 0, stop=k == 1)
                last.then_inc(sem("a_v_done"), 1)
            once(pe, "a_k", 2)
            for rc in range(2):
                for h in range(MH):
                    last = pe.matmul(psum[:, rc, h * NS:(h + 1) * NS], WkT[:, h, rc * P:(rc + 1) * P],
                                     smp(qnT[:, h, :]), start=True, stop=True)
            last.then_inc(sem("a_ql_done"), 1)
            once(pe, "a_k", 4)
            for t, (cols, _, _) in enumerate(token_tiles):
                m = cols.stop - cols.start
                for k in range(2):
                    pe.transpose(psum[0:m, 2 + k, t * P:(t + 1) * P], ckvT[:, k, cols], ident)
            once(pe, "a_v", 1)
            for t, (cols, _, _) in enumerate(token_tiles):
                last = pe.transpose(psum[0:cols.stop - cols.start, 4, t * ROPE:(t + 1) * ROPE], krT[:, cols],
                                    ident[0:ROPE, 0:ROPE])
            last.then_inc(sem("a_tok_turned"), 1)
            once(pe, "a_v", 4)
            once(pe, "a_tok", 1)
            once(pe, "a_ql", 1)

            def scores(h):
                bank = psum[:, 4 * (h % 2), :]
                if h >= 2:
                    once(pe, "a_pm", h - 1)
                for i in range(2):
                    out = bank[:, i * P:i * P + (i + 1) * P]
                    qs = slice(i * P, (i + 1) * P)
                    pe.matmul(out, qnT[:, h, qs], kT[:, h, 0:(i + 1) * P], start=True, stop=False)
                    last = pe.matmul(out, qrT[:, h, qs], krT[:, 0:(i + 1) * P], start=False, stop=True)
                last.then_inc(sem("a_sc_done"), 1)

            def attend(h):
                s = h % 2
                once(pe, "a_pn", h + 1)
                if h >= 2:
                    once(pe, "a_o_pair", h // 2)
                for j in range(3):
                    last = pe.transpose(psum[:, 4 * s + 1, j * P:(j + 1) * P], pm[:, s, j * P:(j + 1) * P], ident)
                last.then_inc(sem("a_p_turned"), 1)
                once(pe, "a_pt", h + 1)
                out = psum[:, 4 * s + 2, :]
                vh = slice(h * P, (h + 1) * P)
                pe.matmul(out[:, 0:P], vP[:, 0, vh], pT[:, s, 0:P], start=True, stop=True)
                pe.matmul(out[:, P:SEQ], vP[:, 0, vh], pT[:, s, P:SEQ], start=True, stop=False)
                pe.matmul(out[:, P:SEQ], vP[:, 1, vh], pT[:, s, SEQ:384], start=False,
                          stop=True).then_inc(sem("a_pv_done"), 1)
            scores(0)
            for h in range(MH):
                if h + 1 < MH:
                    scores(h + 1)
                attend(h)
            once(pe, "a_o_pair", MH // 2)
            pages_turned(pe, 0)
            for e in range(4 * NB):
                b, q = divmod(e, 4)
                if e + 1 < 4 * NB:
                    pages_turned(pe, e + 1)
                sample_scores(pe, b, q)
                if q == 2 and b > 0:
                    probs_turned(pe, b - 1)
                if q == 3:
                    own_tokens(pe, b)
                    if b > 0:
                        sample_attend(pe, b - 1)
            once(pe, "a_ssc", 5 * NB)
            once(pe, "a_spn", NB)
            pe.transpose(psum[0:NS, 6, NS:2 * NS], sc[(NB - 1) % 2][:, PAST:NK], ident[0:NS, 0:NS])
            probs_turned(pe, NB - 1)
            sample_attend(pe, NB - 1)
            once(pe, "a_sol", NB)
            for rc in range(2):
                for b in range(NB):
                    c = (rc * NB + b) * NS
                    last = pe.transpose(psum[:, 0, c:c + NS], OLt[:, b, rc * P:(rc + 1) * P], ident[0:NS, 0:NS])
            last.then_inc(sem("a_ol_turned"), 1)
            once(pe, "a_olf", 1)
            for h in range(MH):
                for rc in range(2):
                    last = pe.matmul(psum[:, 1, h * NS:(h + 1) * NS].rearrange("p (b t) -> p b t", b=NB),
                                     wkv[:, rc, h * 256 + P:(h + 1) * 256], OL[:, rc, :, h, :], start=rc == 0, stop=rc == 1)
            last.then_inc(sem("a_so_done"), 1)
            once(pe, "a_o_split", 2)
            pe_out(pe, n, u0 + 7, xn(xn_hi), xn(xn_lo), None)

        def pages_turned(pe, e):
            b, q = divmod(e, 4)
            if q == 0:
                once(pe, f"a_lat_in{b % LSLOTS}", 16 * NP * (b // LSLOTS + 1))
                pe.wait_ge(sem(f"rope_in{b % LSLOTS}"), 16 * NP * (b // LSLOTS + 1))
            bk = 3 * (e % 2)
            if e >= 2:
                once(pe, "a_latt", e - 1)
            for j in range(4):
                for rc in range(2):
                    pe.transpose(psum[:, bk + rc, j * P:(j + 1) * P], page_at(b % LSLOTS, 4 * q + j)[:, rc * P:(rc + 1) * P],
                                 ident)
                last = pe.transpose(psum[0:ROPE, bk + 2, j * P:(j + 1) * P], ropes[b % LSLOTS][:, 4 * q + j, :], ident)
            last.then_inc(sem("a_lat_turned"), 1)

        def sample_scores(pe, b, q):
            e = 4 * b + q
            once(pe, "a_latt", e + 1)
            if e > 0:
                once(pe, "a_ssc", 5 * b + q)
            for rc in range(2):
                pe.matmul(psum[0:NS, 6, :], QL[:, rc, b].rearrange("p h t -> p (h t)"), latT[:, e % 2, rc, :],
                          start=rc == 0, stop=False)
            pe.matmul(psum[0:NS, 6, :], QRS[:, b].rearrange("p h t -> p (h t)"), ropT[:, e % 2, :], start=False,
                      stop=True).then_inc(sem("a_ssc_done"), 1)

        def own_tokens(pe, b):
            once(pe, "a_ssc", 5 * b + 4)
            if b > 0:
                pe.transpose(psum[0:NS, 6, NS:2 * NS], sc[(b - 1) % 2][:, PAST:NK], ident[0:NS, 0:NS])
            for rc in range(2):
                pe.matmul(psum[0:NS, 6, 0:NS], QL[:, rc, b].rearrange("p h t -> p (h t)"), smp(ckvT[:, rc, :]),
                          start=rc == 0, stop=False)
            pe.matmul(psum[0:NS, 6, 0:NS], QRS[:, b].rearrange("p h t -> p (h t)"), smp(krT[:]), start=False,
                      stop=True).then_inc(sem("a_ssc_done"), 1)

        def probs_turned(pe, b):
            once(pe, "a_spn", b + 1)
            if b > 0:
                once(pe, "a_sol", b)
            for j in range(NP):
                last = pe.transpose(psum[:, 7, j * NS:(j + 1) * NS], sc[b % 2][:, j * P:(j + 1) * P], ident[0:NS, 0:NS])
            last.then_inc(sem("a_sp_turned"), 1)

        def sample_attend(pe, b):
            s = b % 2
            once(pe, "a_spt", b + 1)
            out = psum[0:NS, 7, 0:KVR]
            for j in range(NP):
                pe.matmul(out, spT[:, s, j * NS:(j + 1) * NS], page_at(b % LSLOTS, j), start=j == 0, stop=False)
            pe.matmul(out, spT[0:NS, s, 512:512 + NS], ctok[0:NS, 2, :], start=False, stop=True
                      ).then_inc(sem("a_spv_done"), 1)

        def act_mla(act, n):
            u0 = ubase[n]
            seq, cnt = sem("a_act_seq"), [0]

            def step(ins):
                cnt[0] += 1
                ins.then_inc(seq, 1)
                act.wait_ge(seq, before("a_act_seq") + cnt[0])
            for i in range(3):
                act_split(act, u0 + i + 1)
                act.wait_ge(unit_used, u0 + i + 1)
                if i < 2:
                    act.activation(craw[:, 2 * i:2 * i + 2, :], psum[:, 2 * i:2 * i + 2, 0:T], ACT.Copy
                                   ).then_inc(sem("a_craw"), 1)
                else:
                    act.activation(craw[:, 4, :], psum[:, 4, 0:T], ACT.Copy)
                    act.activation(krr[:, 0, :], psum[0:ROPE, 5, 0:T], ACT.Copy).then_inc(sem("a_craw"), 1)
            once(act, "a_craw", 3)
            act.activation(sq[:, 0:3, :], craw[:, 0:3, :], ACT.Square).then_inc(sem("a_csq"), 1)
            act.activation(sq[:, 3:5, :], craw[:, 3:5, :], ACT.Square).then_inc(sem("a_csq"), 1)
            once(act, "a_css", 1)
            act.activation(sq[:, 5, :], psum[:, 0, 0:T], ACT.Ln, scale=1.0 / QR, bias=eps_t[:, 0:1])
            step(act.activation(sq[:, 6, :], psum[:, 1, 0:T], ACT.Ln, scale=1.0 / KVR, bias=eps_t[:, 0:1]))
            act.activation(sq[:, 5:7, :], sq[:, 5:7, :], ACT.Exp, scale=-0.5).then_inc(sem("a_croot"), 1)
            once(act, "a_cqn", 1)
            act.activation(cq_hi[:], craw[:, 0:3, :], ACT.Copy).then_inc(sem("a_cq_hi"), 1)
            for i in range(4):
                if i < 3:
                    act_split(act, u0 + 3 + i + 1)
                act.wait_ge(unit_used, u0 + 3 + i + 1)
                b = 4 * (i % 2)
                if i >= 2:
                    once(act, "a_q", i - 1)
                for j in range(2):
                    act.activation(qnT[:, 2 * i + j, :], psum[:, b + 2 * j, 0:T], ACT.Copy)
                    last = act.activation(qrr[:, i % 2, j, :], psum[0:ROPE, b + 2 * j + 1, 0:T], ACT.Copy)
                last.then_inc(sem("a_q_evac"), 1)
            for q in range(4):
                once(act, "a_v_done", q + 1)
                act.activation(vP[:, q // 2, 512 * (q % 2):512 * (q % 2) + 512], psum[:, 4 + q, :], ACT.Copy
                               ).then_inc(sem("a_v"), 1)
            once(act, "a_ql_done", 1)
            for rc in range(2):
                for h in range(MH):
                    last = act.activation(QL[:, rc, :, h, :], bt(psum[:, rc, h * NS:(h + 1) * NS]), ACT.Copy)
            for h in range(MH):
                last = act.activation(QRS[:, :, h, :], bt(smp(qrT[:, h, :])), ACT.Copy)
            last.then_inc(sem("a_ql"), 1)
            for h in range(MH):
                s = h % 2
                once(act, "a_max", h + 1)
                act.activation(pm[:, s, 0:P], pm[:, s, 0:P], ACT.Exp, scale=SCALE, bias=stat[:, s, 0:1],
                               accum_out=stat[:, s, 2:3])
                act.activation(pm[:, s, P:384], pm[:, s, P:384], ACT.Exp, scale=SCALE, bias=stat[:, s, 1:2],
                               accum_out=stat[:, s, 3:4]).then_inc(sem("a_p"), 1)
                once(act, "a_p_turned", h + 1)
                act.activation(pT[:, s, :], psum[:, 4 * s + 1, 0:384], ACT.Copy).then_inc(sem("a_pt"), 1)
                if s == 1:
                    once(act, "a_o_pair", h // 2 + 1)
                    act.activation(xn_hi[:, h - 1:h + 1, 0:SEQ], fbuf[:, 0, :, 0:SEQ], ACT.Copy).then_inc(sem("a_o_hi"), 1)
            for b in range(NB):
                for q in range(4):
                    e = 4 * b + q
                    once(act, "a_lat_turned", e + 1)
                    if e >= 2:
                        once(act, "a_ssc_done", 5 * ((e - 2) // 4) + (e - 2) % 4 + 1)
                    bk = 3 * (e % 2)
                    act.activation(latT[:, e % 2, 0, :], psum[:, bk, :], ACT.Copy)
                    act.activation(ropT[:, e % 2, :], psum[0:ROPE, bk + 2, :], ACT.Copy).then_inc(sem("a_latt_a"), 1)
                    if q == 1 and b > 0:
                        sample_exp(act, b - 1)
            sample_exp(act, NB - 1)
            once(act, "a_spv_done", NB - 1)
            act_split(act, u0 + 7)
            once(act, "a_so", 1)
            act.activation(xn_hi[:, :, SEQ:T], fbuf8(), ACT.Copy).then_inc(sem("a_o_hi"), 1)
            once(act, "a_spv_done", NB)
            for i in range(H):
                act_split(act, u0 + 7 + i + 1)
                act_square_y(act, n, i, u0 + 7 + i)

        def fbuf8():
            return fbuf[:].rearrange("p a b t -> p (a b t)")[:, 0:MH * NS].rearrange("p (h q) -> p h q", h=MH)

        def sample_exp(act, b):
            s = b % 2
            once(act, "a_smax", b + 1)
            act.activation(sc[s][:, 0:NK], sc[s][:, 0:NK], ACT.Exp, scale=SCALE, bias=stat[0:NS, s, 4:5],
                           accum_out=stat[0:NS, s, 5:6]).then_inc(sem("a_sp"), 1)

        def dve_mla(dve, n):
            u0 = ubase[n]
            seq, cnt = sem("a_dve_seq"), [0]

            def step(ins):
                cnt[0] += 1
                ins.then_inc(seq, 1)
                dve.wait_ge(seq, before("a_dve_seq") + cnt[0])
            for i in range(3):
                dve_split(dve, u0 + i + 1)
            for q in range(4):
                once(dve, "a_wk_turned", q + 1)
                dve.tensor_copy(WkT[:, 2 * q:2 * q + 2, :].rearrange("p h r -> p (h r)"), psum[:, 6 + q % 2, :]
                                ).then_inc(sem("a_wkt"), 1)
            once(dve, "a_croot", 1)
            for k in range(3):
                last = dve.scalar_tensor_tensor(out=craw[:, k, :], in0=craw[:, k, :], scalar=vec[:, V_QN + k:V_QN + k + 1],
                                                in1=sq[:, 5, :], op0=ALU.mult, op1=ALU.mult)
            last.then_inc(sem("a_cqn"), 1)
            for k in range(2):
                last = dve.scalar_tensor_tensor(out=ckvT[:, k, :], in0=craw[:, 3 + k, :],
                                                scalar=vec[:, V_KVN + k:V_KVN + k + 1], in1=sq[:, 6, :],
                                                op0=ALU.mult, op1=ALU.mult)
            last.then_inc(sem("a_ckv"), 1)
            once(dve, "a_cq_hi", 1)
            dve.tensor_tensor(cq_lo[:], craw[:, 0:3, :], cq_hi[:].bitcast(F32), ALU.subtract).then_inc(sem("a_cq_split"), 1)
            once(dve, "a_krot", 1)
            dve.tensor_tensor(krr[:, 1, :], psum[0:ROPE, 2, 0:T], at_("sin"), ALU.mult)
            step(dve.tensor_tensor(krT[:], krr[:, 0, :], at_("cos"), ALU.mult))
            dve.tensor_tensor(krT[:], krT[:], krr[:, 1, :], ALU.add).then_inc(sem("a_kr"), 1)
            two_ = lambda v: v[:, None, :].to_broadcast([ROPE, 2, T])
            for i in range(4):
                if i < 3:
                    dve_split(dve, u0 + 3 + i + 1)
                once(dve, "a_qrot", i + 1)
                b = 4 * (i % 2)
                r2 = qrT[:, 2 * i:2 * i + 2, :]
                rotated = psum[0:ROPE, b:b + 4:2, 0:T]
                dve.tensor_tensor(qrr[:, i % 2], qrr[:, i % 2], two_(at_("cos")), ALU.mult)
                step(dve.tensor_tensor(r2, rotated, two_(at_("sin")), ALU.mult))
                dve.tensor_tensor(r2, r2, qrr[:, i % 2], ALU.add).then_inc(sem("a_q"), 1)
            for q in range(4):
                once(dve, "a_k_done", q + 1)
                dve.tensor_copy(kT[:, 2 * q:2 * q + 2, :].rearrange("p h t -> p (h t)"), psum[:, q, :]).then_inc(sem("a_k"), 1)
            once(dve, "a_tok_turned", 1)
            for k in range(2):
                rs = slice(k * P, (k + 1) * P)
                dve.tensor_copy(ctok[:, 0:2, rs], psum[:, 2 + k, 0:SEQ].rearrange("p (t r) -> p t r", t=2))
                dve.tensor_copy(ctok[0:NS, 2, rs], psum[0:NS, 2 + k, SEQ:384])
            dve.tensor_copy(krtok[:, 0:2, :], psum[:, 4, 0:2 * ROPE].rearrange("p (t r) -> p t r", t=2))
            dve.tensor_copy(krtok[0:NS, 2, :], psum[0:NS, 4, 2 * ROPE:3 * ROPE]).then_inc(sem("a_tok"), 1)

            def masked(h):
                s = h % 2
                once(dve, "a_sc_done", h + 1)
                if h >= 2:
                    once(dve, "a_p_turned", h - 1)
                dve.tensor_tensor(pm[:, s, :], psum[:, 4 * s, 0:384], at_("causal"), ALU.add).then_inc(sem("a_pm"), 1)
                once(dve, "a_pm", h + 1)
                dve.tensor_reduce(stat[:, s, 6:7], pm[:, s, 0:P], AX.X, ALU.max)
                step(dve.tensor_reduce(stat[:, s, 7:8], pm[:, s, P:384], AX.X, ALU.max))
                dve.tensor_scalar(stat[:, s, 0:2], stat[:, s, 6:8], -SCALE, None, ALU.mult).then_inc(sem("a_max"), 1)

            def head_out(h):
                s = h % 2
                once(dve, "a_pv_done", h + 1)
                if s == 0 and h >= 2:
                    once(dve, "a_o_low", h // 2)
                last = dve.tensor_copy(fbuf[:, 0, s, 0:SEQ], psum[:, 4 * s + 2, 0:SEQ])
                if s == 1:
                    last.then_inc(sem("a_o_pair"), 1)
                    once(dve, "a_o_hi", h // 2 + 1)
                    dve.tensor_tensor(xn_lo[:, h - 1:h + 1, 0:SEQ], fbuf[:, 0, :, 0:SEQ],
                                      xn_hi[:, h - 1:h + 1, 0:SEQ].bitcast(F32), ALU.subtract).then_inc(sem("a_o_low"), 1)
            masked(0)
            for h in range(MH):
                s = h % 2
                once(dve, "a_p", h + 1)
                step(dve.reciprocal(stat[:, s, 2:4], stat[:, s, 2:4]))
                dve.tensor_scalar(pm[:, s, 0:P], pm[:, s, 0:P], stat[:, s, 2:3], None, ALU.mult)
                dve.tensor_scalar(pm[:, s, P:384], pm[:, s, P:384], stat[:, s, 3:4], None, ALU.mult).then_inc(sem("a_pn"), 1)
                if h + 1 < MH:
                    masked(h + 1)
                head_out(h)
            dve.tensor_copy(stat[:, 0, 6:7], stat[:, 0, 7:8]).then_inc(sem("a_o_split"), 1)

            def sample_softmax(b):
                s = b % 2
                step(dve.tensor_reduce(stat[0:NS, s, 6:7], sc[s][:, 0:NK], AX.X, ALU.max))
                dve.tensor_scalar(stat[0:NS, s, 4:5], stat[0:NS, s, 6:7], -SCALE, None, ALU.mult).then_inc(sem("a_smax"), 1)

            def sample_rest(b):
                s = b % 2
                once(dve, "a_sp", b + 1)
                step(dve.reciprocal(stat[0:NS, s, 5:6], stat[0:NS, s, 5:6]))
                dve.tensor_scalar(sc[s][:, 0:NK], sc[s][:, 0:NK], stat[0:NS, s, 5:6], None, ALU.mult).then_inc(sem("a_spn"), 1)

            def probs_out(b):
                once(dve, "a_sp_turned", b + 1)
                dve.tensor_copy(spT[:, b % 2, 0:512], psum[:, 7, :])

            def own_out(b):
                dve.tensor_copy(spT[0:NS, b % 2, 512:512 + NS], psum[0:NS, 6, NS:2 * NS]).then_inc(sem("a_spt"), 1)

            def sample_out(b):
                once(dve, "a_spv_done", b + 1)
                dve.tensor_copy(OLt[:, b, :], psum[0:NS, 7, 0:KVR]).then_inc(sem("a_sol"), 1)
            for e in range(4 * NB + 1):
                if e < 4 * NB:
                    once(dve, "a_latt_a", e + 1)
                    bk = 3 * (e % 2)
                    dve.tensor_copy(latT[:, e % 2, 1, :], psum[:, bk + 1, :]).then_inc(sem("a_latt"), 1)
                if e == 0:
                    continue
                b, q = divmod(e - 1, 4)
                once(dve, "a_ssc_done", 5 * b + q + 1)
                dve.tensor_copy(sc[b % 2][:, q * 512:(q + 1) * 512], psum[0:NS, 6, :]).then_inc(sem("a_ssc"), 1)
                if q == 1 and b > 0:
                    sample_rest(b - 1)
                if q == 3:
                    if b > 0:
                        probs_out(b - 1)
                    once(dve, "a_ssc_done", 5 * b + 5)
                    dve.tensor_tensor(sc[b % 2][:, PAST:NK], psum[0:NS, 6, 0:NS], at_("own")[:, b * NS:(b + 1) * NS], ALU.add
                                      ).then_inc(sem("a_ssc"), 1)
                    if b > 0:
                        own_out(b - 1)
                    once(dve, "a_ssc", 5 * b + 5)
                    sample_softmax(b)
                    if b > 0:
                        sample_out(b - 1)
            sample_rest(NB - 1)
            probs_out(NB - 1)
            own_out(NB - 1)
            sample_out(NB - 1)
            once(dve, "a_ol_turned", 1)
            dve.tensor_copy(OL[:].rearrange("p c b h t -> p (c b h t)"), psum[:, 0, :]).then_inc(sem("a_olf"), 1)
            dve_split(dve, u0 + 7)
            once(dve, "a_so_done", 1)
            dve.tensor_copy(fbuf8(), psum[:, 1, 0:MH * NS].rearrange("p (h q) -> p h q", h=MH)).then_inc(sem("a_so"), 1)
            once(dve, "a_o_hi", MH // 2 + 1)
            dve.tensor_tensor(xn_lo[:, :, SEQ:T], fbuf8(), xn_hi[:, :, SEQ:T].bitcast(F32), ALU.subtract
                              ).then_inc(sem("a_o_split"), 1)
            for i in range(H):
                dve_split(dve, u0 + 7 + i + 1)
                dve_take_y(dve, n, i)
        SP["mla"], PE["mla"], ACTE["mla"], DVE["mla"], POOL["mla"] = sp_mla, pe_mla, act_mla, dve_mla, pool_mla


        vec_ready, out_rows = sem("vec_ready"), sem("out_rows")
        vec_rows = []
        for src, r0, cnt in ((a["norm_gains"].rearrange("l n (k p) -> (l n k) p", p=P), V_GAIN, NGAIN),
                             (a["gdn_conv_w"].rearrange("g j (k p) -> (g j k) p", p=P), V_CONV, NCONV),
                             (a["gdn_norm_w"], V_GN, 2),
                             (a["mla_q_norm"].rearrange("g (k p) -> (g k) p", p=P), V_QN, QR // P),
                             (a["mla_kv_norm"].rearrange("g (k p) -> (g k) p", p=P), V_KVN, KVR // P)):
            r = 0
            while r < cnt:
                q = r0 + r
                m = min(cnt - r, P - q % P)
                vec_rows.append((vt[q % P:q % P + m, q // P, :], src[r:r + m, :]))
                r += m

        @block.sync
        def _(sp):
            sp.dma_start(base[:], a["c_base"]).then_inc(sem("base_in"), 16)
            for t, (cols, src, _) in enumerate(token_tiles):
                sp.dma_start(xin(t)[0:cols.stop - cols.start], src).then_inc(sem("x_in"), 16)
            for dst, src in vec_rows:
                sp.dma_start(dst, src).then_inc(sem("vec_in"), 16)
            for n, sub in enumerate(subs):
                here[0] = n
                SP[sub[0]](sp, n)
            for t, (cols, _, dst) in enumerate(token_tiles):
                sp.wait_ge(out_rows, 2 * t + 2)
                sp.dma_start(dst, xin(t)[0:cols.stop - cols.start]).then_inc(sem("y_stored"), 16)
            sp.wait_ge(sem("y_stored"), 16 * len(token_tiles))

        @block.tensor
        def _(pe):
            pe.wait_ge(sem("base_in"), 16)
            pe.wait_ge(sem("x_in"), 48)
            for k in range(KC):
                for t, (cols, _, _) in enumerate(token_tiles):
                    m = cols.stop - cols.start
                    last = pe.transpose(psum[:, k, cols], xin(t)[0:m, k * P:(k + 1) * P], ident[0:m, 0:m])
                last.then_inc(sem("x_turned"), 1)
            pe.wait_ge(sem("vec_in"), 16 * len(vec_rows))
            pe.wait_ge(x_ready, H)
            for c in range(4):
                m = min(P, V_ALL - c * P)
                last = pe.transpose(psum[:, 2, c * P:c * P + m], vt[0:m, c, :], ident[0:m, 0:m])
            last.then_inc(sem("vec_turned"), 1)
            for n, sub in enumerate(subs):
                here[0] = n
                if sub[0] != "ffn":
                    for i in range(H):
                        pe_sum_squares(pe, 2 * n, i)
                PE[sub[0]](pe, n)
            pe.wait_ge(x_ready, H * (NSUB + 1))
            for t, (cols, _, _) in enumerate(token_tiles):
                m = cols.stop - cols.start
                for half in range(2):
                    for q in range(4):
                        last = pe.transpose(psum[0:m, 2 * t + half + 2, q * P:(q + 1) * P], x[:, 4 * half + q, cols],
                                            ident)
                    last.then_inc(sem("rows_turned"), 1)

        @block.scalar
        def _(act):
            act_split(act, 0)
            act.wait_ge(sem("eps_set"), 2)
            act.wait_ge(sem("x_turned"), KC)
            for n, sub in enumerate(subs):
                here[0] = n
                (act_pre_ffn if sub[0] == "ffn" else act_pre)(act, n)
                ACTE[sub[0]](act, n)
                act_root(act, 2 * n + 1)

        @block.vector
        def _(dve):
            dve.memset(eps_t[:, 0:1], EPS).then_inc(sem("eps_set"), 1)
            dve.memset(eps_t[:, 1:2], P * EPS).then_inc(sem("eps_set"), 1)
            dve_split(dve, 0)
            for i in range(H):
                dve.wait_ge(sem("x_turned"), 2 * i + 2)
                dve.tensor_copy(x[:, 2 * i:2 * i + 2, :], psum[:, 2 * i:2 * i + 2, 0:T]).then_inc(x_ready, 1)
            dve.wait_ge(sem("vec_turned"), 1)
            dve.tensor_copy(vec[:], psum[:, 2, 0:V_ALL]).then_inc(vec_ready, 1)
            dve.wait_ge(vec_ready, 1)
            gains = vec[:, V_GAIN:V_GAIN + NGAIN].rearrange("p (l n k) -> p l n k", l=DEPTH, n=6)
            for n in (1, 5):
                dve.tensor_scalar(gains[:, :, n, :], gains[:, :, n, :], 0.5, None, ALU.mult).then_inc(vec_ready, 1)
            dve_enter(dve, 0, lambda i: None)
            for n, sub in enumerate(subs):
                here[0] = n
                dve_pre(dve, n)
                DVE[sub[0]](dve, n)
                dve_update(dve, n)
            for t, (cols, _, _) in enumerate(token_tiles):
                m = cols.stop - cols.start
                for half in range(2):
                    dve.wait_ge(sem("rows_turned"), 2 * t + half + 1)
                    dve.tensor_copy(xin(t)[0:m, 512 * half:512 * half + 512],
                                    psum[0:m, 2 * t + half + 2, :]).then_inc(out_rows, 1)

        @block.gpsimd
        def _(pool):
            for n, sub in enumerate(subs):
                here[0] = n
                if sub[0] in POOL:
                    POOL[sub[0]](pool, n)


INS = ["x_prompt", "x_sample", "state_gdn_S", "state_gdn_conv", "cache_mla_latent", "cache_mla_rope",
       "state_mlstm_C", "state_mlstm_n", "state_mlstm_m", "page_table", "norm_gains", "w_ffn_up", "w_ffn_down",
       "gdn_w_in", "gdn_conv_w", "gdn_a_log", "gdn_dt_bias", "gdn_norm_w", "gdn_w_out", "mla_w_in", "mla_q_norm",
       "mla_kv_norm", "mla_w_uq", "mla_w_ukv", "mla_w_out", "mlstm_w_in", "mlstm_i_bias", "mlstm_f_bias",
       "mlstm_w_out"]
OUTS = [("y_prompt", (1, SEQ, D)), ("y_sample", (NB, NT, D)),
        ("gdn_S_p", (2, 1, HG, P, P)), ("gdn_S_s", (2, NB, HG, P, P)),
        ("gdn_conv_p", (2, 1, 3, GQKV)), ("gdn_conv_s", (2, NB, 3, GQKV)),
        ("mla_lat_p", (1, SEQ // PAGE, PAGE, KVR)), ("mla_lat_s", (1, NB, NT, KVR)),
        ("mla_rope_p", (1, SEQ // PAGE, PAGE, ROPE)), ("mla_rope_s", (1, NB, NT, ROPE)),
        ("ml_C_p", (1, 1, LH, P, 256)), ("ml_C_s", (1, NB, LH, P, 256)),
        ("ml_n_p", (1, 1, LH, P)), ("ml_n_s", (1, NB, LH, P)), ("ml_m_p", (1, 1, LH)), ("ml_m_s", (1, NB, LH))]


def kernel(**inputs):
    import concourse.bacc as bacc
    from concourse.bass_utils import run_bass_kernel_spmd

    nc = bacc.Bacc("TRN2", target_bir_lowering=False, num_devices=1)
    arrays = {name: np.ascontiguousarray(inputs[name]) for name in INS}
    arrays.update({name: np.ascontiguousarray(t[0]) for name, t in tables().items()})
    aps = {name: nc.dram_tensor(name, v.shape, mybir.dt.from_np(v.dtype), kind="ExternalInput").ap()
           for name, v in arrays.items()}
    for name, shape in OUTS:
        aps[name] = nc.dram_tensor(name, shape, F32, kind="ExternalOutput").ap()
    trunk(nc, aps, sublayers())
    r = run_bass_kernel_spmd(nc, [arrays], core_ids=[0])
    return tuple(r.results[0][name] for name, _ in OUTS)
```
